# Optimizing a Trainium2 kernel written in Bass

```python
import math
import jax, jax.numpy as jnp
from jax import lax
import numpy as np

D_MODEL = 1024
BATCH = 1
SEQ = 1024
DEPTH = 1
DEC_BATCH = 1
DEC_SEQ = 32
PAST_LEN = 512

CHUNK = 64
EPS = 1e-6
GLA_HEADS = 4
GLA_DK = D_MODEL // 8
GLA_DV = D_MODEL // 4
GLA_LOWRANK = 16
GLA_TAU = 16.0
GLA_BLOCK = 16
DIFF_HEADS = 8
DIFF_HD = D_MODEL // (2 * DIFF_HEADS)
DIFF_VD = 2 * DIFF_HD
ROPE_THETA = 10000.0
Q_BLOCK = 128
PEER_HEADS = 8
PEER_NKEYS = 128
PEER_NEXPERTS = PEER_NKEYS * PEER_NKEYS
PEER_DKEY = 256
PEER_TOPK = 16
PEER_BLOCK = 256
GLA_QK_W = GLA_HEADS * GLA_DK
GLA_V_W = GLA_HEADS * GLA_DV
DIFF_QK_W = DIFF_HEADS * 2 * DIFF_HD
DIFF_V_W = DIFF_HEADS * DIFF_VD
IN_SIZES = (GLA_QK_W, GLA_QK_W, GLA_V_W, GLA_V_W, GLA_LOWRANK, DIFF_QK_W, DIFF_QK_W, DIFF_V_W, 2 * D_MODEL)
IN_WIDTH = 2 * GLA_QK_W + 2 * GLA_V_W + GLA_LOWRANK + 2 * DIFF_QK_W + DIFF_V_W + 2 * D_MODEL

kernel_name = 'hybrid_gla_diffattn_peer_stream_step'

F32 = jnp.float32

def rmsnorm(x, gain):
    xf = x.astype(F32)
    y = xf * lax.rsqrt(jnp.mean(xf * xf, axis=-1, keepdims=True) + EPS)
    return (y * gain.astype(F32)).astype(x.dtype)

def modulate(x, gain, shift, scale):
    return rmsnorm(x, gain) * (1 + scale[:, None, :]) + shift[:, None, :]

def rope(x, pos):
    d = x.shape[-1]
    half = d // 2
    inv = ROPE_THETA ** (-jnp.arange(half, dtype=F32) / half)
    ang = pos.astype(F32)[:, None] * inv[None, :]
    ang = ang.reshape((1, ang.shape[0]) + (1,) * (x.ndim - 3) + (half,))
    cos, sin = jnp.cos(ang), jnp.sin(ang)
    xf = x.astype(F32)
    x1, x2 = xf[..., :half], xf[..., half:]
    return jnp.concatenate([x1 * cos - x2 * sin, x2 * cos + x1 * sin], axis=-1).astype(x.dtype)

def gla_recurrence(q, k, v, log_a, h0):
    B, L, H, _ = q.shape
    dv = v.shape[-1]
    n = L // GLA_BLOCK

    def blocks(t):
        return jnp.moveaxis(t.reshape(B, n, GLA_BLOCK, H, t.shape[-1]), 1, 0)

    causal = jnp.tril(jnp.ones((GLA_BLOCK, GLA_BLOCK), dtype=bool))

    def step(h, xs):
        qb, kb, vb, gb = xs
        b = jnp.cumsum(gb, axis=1)
        qe = qb * jnp.exp(b)
        ke = kb * jnp.exp(-b)
        a = jnp.where(causal, jnp.einsum('bthk,bshk->bhts', qe, ke), 0.0)
        o = jnp.einsum('bthk,bhkv->bthv', qe, h) + jnp.einsum('bhts,bshv->bthv', a, vb)
        b_last = b[:, -1]
        h = jnp.exp(b_last)[..., None] * h + jnp.einsum('bshk,bshv->bhkv', kb * jnp.exp(b_last[:, None] - b), vb)
        return h, o

    h, o = lax.scan(step, h0, (blocks(q), blocks(k), blocks(v), blocks(log_a)))
    o = jnp.moveaxis(o, 0, 1).reshape(B, L, H, dv)
    return o, h

def diff_attend(q1, q2, k1, k2, v, mask, lam):
    scale = DIFF_HD ** -0.5
    s1 = jnp.einsum('bqhd,bkhd->bhqk', q1, k1).astype(F32) * scale
    s2 = jnp.einsum('bqhd,bkhd->bhqk', q2, k2).astype(F32) * scale
    if mask is not None:
        s1 = jnp.where(mask, s1, -jnp.inf)
        s2 = jnp.where(mask, s2, -jnp.inf)
    p = jax.nn.softmax(s1, axis=-1) - lam * jax.nn.softmax(s2, axis=-1)
    return jnp.einsum('bhqk,bkhv->bqhv', p.astype(v.dtype), v)

def peer_ffn(x, w_pq, sub_keys1, sub_keys2, peer_u, peer_v):
    n = x.shape[0]
    pad = (-n) % PEER_BLOCK
    xb = jnp.pad(x, ((0, pad), (0, 0))).reshape(-1, PEER_BLOCK, D_MODEL)
    half = PEER_DKEY // 2

    def block(xt):
        q = (xt @ w_pq).reshape(PEER_BLOCK, PEER_HEADS, 2, half)
        s1 = jnp.einsum('thc,nc->thn', q[:, :, 0], sub_keys1)
        s2 = jnp.einsum('thc,nc->thn', q[:, :, 1], sub_keys2)
        v1, i1 = lax.top_k(s1, PEER_TOPK)
        v2, i2 = lax.top_k(s2, PEER_TOPK)
        cand = (v1[..., :, None] + v2[..., None, :]).reshape(PEER_BLOCK, PEER_HEADS, PEER_TOPK * PEER_TOPK)
        sc, ci = lax.top_k(cand, PEER_TOPK)
        e1 = jnp.take_along_axis(i1, ci // PEER_TOPK, axis=-1)
        e2 = jnp.take_along_axis(i2, ci % PEER_TOPK, axis=-1)
        idx = e1 * PEER_NKEYS + e2
        g = jax.nn.softmax(sc.astype(F32), axis=-1).astype(xt.dtype)
        act = jax.nn.gelu(jnp.einsum('td,thkd->thk', xt, peer_u[idx]), approximate=False)
        return jnp.einsum('thk,thkd->td', g * act, peer_v[idx])

    y = lax.map(block, xb)
    return y.reshape(-1, D_MODEL)[:n]

def trunk_layer(x, pos, c, past_k, past_v, gla_h0, lambda_init,
                norm1_gain, norm2_gain, w_mod, b_mod, w_in, w_alpha, b_alpha, gla_gain, w_gla_out,
                q_gain, k_gain, lam_q1, lam_k1, lam_q2, lam_k2, diff_gain, w_diff_out, w_out,
                w_pq, sub_keys1, sub_keys2, peer_u, peer_v):
    B, L, _ = x.shape
    mod = jax.nn.silu(c) @ w_mod + b_mod
    sh1, sc1, gt1, sh2, sc2, gt2 = jnp.split(mod, 6, axis=-1)

    h = modulate(x, norm1_gain, sh1, sc1)
    z = h @ w_in
    gq, gk, gv, gr, glr, dq, dk, dv, gates = jnp.split(z, np.cumsum(IN_SIZES)[:-1].tolist(), axis=-1)

    q = gq.reshape(B, L, GLA_HEADS, GLA_DK) * (GLA_DK ** -0.5)
    k = gk.reshape(B, L, GLA_HEADS, GLA_DK)
    v = gv.reshape(B, L, GLA_HEADS, GLA_DV)
    log_a = (jax.nn.log_sigmoid((glr @ w_alpha + b_alpha).astype(F32)) / GLA_TAU).reshape(B, L, GLA_HEADS, GLA_DK)
    pad = (-L) % GLA_BLOCK

    def prep(t):
        return jnp.pad(t.astype(F32), ((0, 0), (0, pad), (0, 0), (0, 0)))

    o_a, gla_state = gla_recurrence(prep(q), prep(k), prep(v), prep(log_a), gla_h0.astype(F32))
    o_a = o_a[:, :L].astype(x.dtype)
    o_a = rmsnorm(o_a, gla_gain) * jax.nn.silu(gr.reshape(B, L, GLA_HEADS, GLA_DV))
    y_a = o_a.reshape(B, L, GLA_V_W) @ w_gla_out

    qd = rope(rmsnorm(dq.reshape(B, L, DIFF_HEADS, 2, DIFF_HD), q_gain), pos)
    kd = rope(rmsnorm(dk.reshape(B, L, DIFF_HEADS, 2, DIFF_HD), k_gain), pos)
    k_rows = kd.reshape(B, L, DIFF_HEADS, 2 * DIFF_HD)
    v_rows = dv.reshape(B, L, DIFF_HEADS, DIFF_VD)
    lam = (jnp.exp(jnp.sum(lam_q1.astype(F32) * lam_k1.astype(F32)))
           - jnp.exp(jnp.sum(lam_q2.astype(F32) * lam_k2.astype(F32))) + lambda_init)
    q1, q2 = qd[..., 0, :], qd[..., 1, :]
    if past_k is None:
        k1, k2 = kd[..., 0, :], kd[..., 1, :]
        nq = L // Q_BLOCK

        def qblocks(t):
            return jnp.moveaxis(t.reshape((B, nq, Q_BLOCK) + t.shape[2:]), 1, 0)

        key_chunk = jnp.arange(L) // CHUNK

        def attend_block(args):
            q1b, q2b, qpos = args
            mask = (qpos[:, None] // CHUNK) >= key_chunk[None, :]
            return diff_attend(q1b, q2b, k1, k2, v_rows, mask, lam)

        o_b = lax.map(attend_block, (qblocks(q1), qblocks(q2), jnp.arange(L).reshape(nq, Q_BLOCK)))
        o_b = jnp.moveaxis(o_b, 0, 1).reshape(B, L, DIFF_HEADS, DIFF_VD)
    else:
        keys = jnp.concatenate([past_k.astype(k_rows.dtype), k_rows], axis=1)
        vals = jnp.concatenate([past_v.astype(v_rows.dtype), v_rows], axis=1)
        o_b = diff_attend(q1, q2, keys[..., :DIFF_HD], keys[..., DIFF_HD:], vals, None, lam)
    o_b = rmsnorm(o_b, diff_gain) * (1.0 - lambda_init)
    y_b = o_b.reshape(B, L, DIFF_V_W) @ w_diff_out

    g_a, g_b = jnp.split(gates, 2, axis=-1)
    mix = (jax.nn.sigmoid(g_a) * y_a + jax.nn.sigmoid(g_b) * y_b) @ w_out
    x = x + gt1[:, None, :] * mix

    h2 = modulate(x, norm2_gain, sh2, sc2)
    ff = peer_ffn(h2.reshape(B * L, D_MODEL), w_pq, sub_keys1, sub_keys2, peer_u, peer_v)
    x = x + gt2[:, None, :] * ff.reshape(B, L, D_MODEL)
    return x, k_rows, v_rows, gla_state.astype(x.dtype)

def setup_inputs(seed: int = 0) -> dict:
    key = jax.random.key(seed)
    ks = jax.random.split(key, 40)

    def nrm(k, shape, scale):
        return jax.random.normal(k, shape, F32) * scale

    def gain(k, shape):
        return 1.0 + 0.02 * jax.random.normal(k, shape, F32)

    D = D_MODEL
    return {
        'x_prompt': nrm(ks[0], (BATCH, SEQ, D), 1.0),
        'x_sample': nrm(ks[1], (DEC_BATCH, DEC_SEQ, D), 1.0),
        'c_prompt': nrm(ks[2], (BATCH, D), 1.0),
        'c_sample': nrm(ks[3], (DEC_BATCH, D), 1.0),
        'cache_k': nrm(ks[4], (DEPTH, DEC_BATCH, PAST_LEN, DIFF_HEADS, 2 * DIFF_HD), 1.0),
        'cache_v': nrm(ks[5], (DEPTH, DEC_BATCH, PAST_LEN, DIFF_HEADS, DIFF_VD), 1.0),
        'state_gla': nrm(ks[6], (DEPTH, DEC_BATCH, GLA_HEADS, GLA_DK, GLA_DV), GLA_DK ** -0.5),
        'norm1_gain': gain(ks[7], (DEPTH, D)),
        'norm2_gain': gain(ks[8], (DEPTH, D)),
        'w_mod': nrm(ks[9], (DEPTH, D, 6 * D), 0.5 * D ** -0.5),
        'b_mod': nrm(ks[10], (DEPTH, 6 * D), 0.01),
        'w_in': nrm(ks[11], (DEPTH, D, IN_WIDTH), D ** -0.5),
        'w_alpha': nrm(ks[12], (DEPTH, GLA_LOWRANK, GLA_QK_W), GLA_LOWRANK ** -0.5),
        'b_alpha': nrm(ks[13], (DEPTH, GLA_QK_W), 0.01),
        'gla_gain': gain(ks[14], (DEPTH, GLA_DV)),
        'w_gla_out': nrm(ks[15], (DEPTH, GLA_V_W, D), GLA_V_W ** -0.5),
        'q_gain': gain(ks[16], (DEPTH, 2, DIFF_HD)),
        'k_gain': gain(ks[17], (DEPTH, 2, DIFF_HD)),
        'lam_q1': nrm(ks[18], (DEPTH, DIFF_HD), 0.1),
        'lam_k1': nrm(ks[19], (DEPTH, DIFF_HD), 0.1),
        'lam_q2': nrm(ks[20], (DEPTH, DIFF_HD), 0.1),
        'lam_k2': nrm(ks[21], (DEPTH, DIFF_HD), 0.1),
        'diff_gain': gain(ks[22], (DEPTH, DIFF_VD)),
        'w_diff_out': nrm(ks[23], (DEPTH, DIFF_V_W, D), DIFF_V_W ** -0.5),
        'w_out': nrm(ks[24], (DEPTH, D, D), D ** -0.5),
        'w_pq': nrm(ks[25], (DEPTH, D, PEER_HEADS * PEER_DKEY), D ** -0.5),
        'sub_keys1': nrm(ks[26], (DEPTH, PEER_NKEYS, PEER_DKEY // 2), (PEER_DKEY // 2) ** -0.5),
        'sub_keys2': nrm(ks[27], (DEPTH, PEER_NKEYS, PEER_DKEY // 2), (PEER_DKEY // 2) ** -0.5),
        'peer_u': nrm(ks[28], (DEPTH, PEER_NEXPERTS, D), D ** -0.5),
        'peer_v': nrm(ks[29], (DEPTH, PEER_NEXPERTS, D), PEER_HEADS ** -0.5),
    }

def reference(x_prompt, x_sample, c_prompt, c_sample, cache_k, cache_v, state_gla,
              norm1_gain, norm2_gain, w_mod, b_mod, w_in, w_alpha, b_alpha, gla_gain, w_gla_out,
              q_gain, k_gain, lam_q1, lam_k1, lam_q2, lam_k2, diff_gain, w_diff_out, w_out,
              w_pq, sub_keys1, sub_keys2, peer_u, peer_v):
    pos_p = jnp.arange(x_prompt.shape[1])
    pos_s = cache_k.shape[2] + jnp.arange(x_sample.shape[1])
    h0_p = jnp.zeros((x_prompt.shape[0], GLA_HEADS, GLA_DK, GLA_DV), x_prompt.dtype)
    yp, ys = x_prompt, x_sample
    kp, vp, sp, ksm, vsm, ssm = [], [], [], [], [], []
    for l in range(DEPTH):
        lambda_init = 0.8 - 0.6 * math.exp(-0.3 * l)
        lw = (norm1_gain[l], norm2_gain[l], w_mod[l], b_mod[l], w_in[l], w_alpha[l], b_alpha[l],
              gla_gain[l], w_gla_out[l], q_gain[l], k_gain[l], lam_q1[l], lam_k1[l], lam_q2[l], lam_k2[l],
              diff_gain[l], w_diff_out[l], w_out[l], w_pq[l], sub_keys1[l], sub_keys2[l], peer_u[l], peer_v[l])
        yp, k_new, v_new, s_new = trunk_layer(yp, pos_p, c_prompt, None, None, h0_p, lambda_init, *lw)
        kp.append(k_new)
        vp.append(v_new)
        sp.append(s_new)
        ys, k_new, v_new, s_new = trunk_layer(ys, pos_s, c_sample, cache_k[l], cache_v[l], state_gla[l], lambda_init, *lw)
        ksm.append(k_new)
        vsm.append(v_new)
        ssm.append(s_new)
    return (yp, ys, jnp.stack(kp), jnp.stack(vp), jnp.stack(sp), jnp.stack(ksm), jnp.stack(vsm), jnp.stack(ssm))


_drawn_inputs = setup_inputs


def setup_inputs(seed=0):
    import zlib

    import numpy as np

    out = dict(_drawn_inputs(seed))
    spreads = {}
    factors = {'state_gla': 8.0,
     'norm2_gain': 6.621,
     'b_alpha': 8.0,
     'gla_gain': 8.0,
     'q_gain': 8.0,
     'k_gain': 2.888,
     'lam_q1': 3.174,
     'lam_q2': 8.0,
     'lam_k2': 6.517,
     'diff_gain': 8.0}
    for name, (base, spread) in spreads.items():
        noise = np.random.default_rng([zlib.crc32(name.encode()), seed]).standard_normal(out[name].shape)
        drawn = base * np.exp(spread * noise) if base else spread * noise
        out[name] = __import__('jax').numpy.asarray(drawn.astype(out[name].dtype))
    for name, factor in factors.items():
        out[name] = (out[name] * factor).astype(out[name].dtype)
    return out
```

```python
import concourse.bass as bass
from concourse import mybir
from contextlib import ExitStack

F32 = mybir.dt.float32
U32 = mybir.dt.uint32
ACT = mybir.ActivationFunctionType
ALU = mybir.AluOpType
AX = mybir.AxisListType

D = 1024
P = 128
KC = D // P
SEQ, DEC = 1024, 32
PAST = 512
NT = SEQ // P
TILES = NT + 1
TOK = TILES * P
EPS = 1e-6
GH, GDK, GDV, GLR, GBLK = 4, 128, 256, 16, 16
GTAU = 16.0
DH, HD, VD = 8, 64, 128
LAM_INIT = 0.2
PH, NKEY, TOPK = 8, 128, 16
BANK = 512
GROUPS, GCOL = 3, TOK // 3
W_QK, W_GVR, W_GLR = 0, 2 * GH * GDK, 2 * GH * GDK + 2 * GH * GDV
W_D = W_GLR + GLR
W_GATE = W_D + 3 * D
SH1, SC1, GT1, SH2, SC2, GT2 = range(6)
ZV, ZR, ZQ, ZK, ZDV = range(5)


def hold(eng, passed, sem, value):
    if isinstance(value, int) and value <= 0:
        return
    eng.wait_ge(sem, value)
    eng.sem_inc(passed, 1)



def modulation(nc, sem, d):
    CH, RING = 6 * D // BANK, 3
    with ExitStack() as ctx:
        def sb(name, shape, dt=F32):
            return ctx.enter_context(nc.sbuf_tensor(name, shape, dt))

        c_raw = sb("c_raw", [P, 2, KC])
        c_act = sb("c_act", [P, KC, 2])
        w = [sb(f"w_mod{i}", [P, KC, BANK]) for i in range(RING)]
        bias = sb("mod_bias", [2, 6 * D])
        gain = sb("mod_gain", [2, 2, D])
        rows = sb("mod_rows", [2, 6 * D])
        acc = ctx.enter_context(nc.psum_tensor("mod_acc", [2, 4, BANK], F32))
        c_in, small_in, c_ready = sem("mod_c_in"), sem("mod_small_in"), sem("mod_c_ready")
        w_in = [sem(f"mod_w_in{i}") for i in range(RING)]
        chunk_done, row_done, scaled, stored = (sem(n) for n in ("mod_chunk", "mod_row", "mod_scaled", "mod_stored"))
        block = ctx.enter_context(nc.Block())

        @block.sync
        def _(sp):
            for s, c in enumerate((d["c_prompt"], d["c_sample"])):
                sp.dma_start(c_raw[:, s, :], c[0, :].rearrange("(p k) -> p k", k=KC)).then_inc(c_in, 16)
            sp.dma_start(bias[:], d["b_mod"].to_broadcast([2, 6 * D])).then_inc(small_in, 16)
            for n, g in enumerate(("norm1_gain", "norm2_gain")):
                sp.dma_start(gain[:, n, :], d[g].to_broadcast([2, D])).then_inc(small_in, 16)
            for c in range(CH):
                if c >= RING:
                    sp.wait_ge(chunk_done, c - RING + 1)
                src = d["w_mod"][0, :, c * BANK:(c + 1) * BANK].rearrange("(p k) n -> p k n", k=KC)
                sp.dma_start(w[c % RING][:], src).then_inc(w_in[c % RING], 16)
            sp.wait_ge(scaled, 2)
            sp.dma_start(d["mod"], rows[:]).then_inc(stored, 16)
            sp.wait_ge(stored, 16)

        @block.scalar
        def _(act):
            act.wait_ge(c_in, 32)
            nc.scalar.activation(c_act[:].rearrange("p k s -> p s k"), c_raw[:], ACT.Silu).then_inc(c_ready, 1)

        @block.tensor
        def _(pe):
            pe.wait_ge(c_ready, 1)
            for c in range(CH):
                pe.wait_ge(w_in[c % RING], 16 * (c // RING + 1))
                if c >= 4:
                    pe.wait_ge(row_done, c - 3)
                for k in range(KC):
                    mm = nc.tensor.matmul(acc[:, c % 4, :], c_act[:, k, :], w[c % RING][:, k, :],
                                          start=(k == 0), stop=(k == KC - 1))
                mm.then_inc(chunk_done, 1)

        @block.vector
        def _(dve):
            dve.wait_ge(small_in, 48)
            for c in range(CH):
                dve.wait_ge(chunk_done, c + 1)
                cols = slice(c * BANK, (c + 1) * BANK)
                nc.vector.tensor_tensor(rows[:, cols], acc[:, c % 4, :], bias[:, cols], ALU.add).then_inc(row_done, 1)
            dve.wait_ge(row_done, CH)
            for n, part in enumerate((SC1, SC2)):
                row = rows[:, part * D:(part + 1) * D]
                nc.vector.scalar_tensor_tensor(row, row, 1.0, gain[:, n, :], ALU.add, ALU.mult).then_inc(scaled, 1)


def norm_in(nc, sem, d, hT):
    with ExitStack() as ctx:
        def sb(name, shape, dt=F32):
            return ctx.enter_context(nc.sbuf_tensor(name, shape, dt))

        ident = sb("n1_ident", [P, P])
        x = sb("n1_x", [P, TILES, D])
        modb = sb("n1_mod", [P, 2, 2, D])
        sq = sb("n1_sq", [P, 2, D])
        ms, mse, half, rstd = (sb(n, [P, TILES]) for n in ("n1_ms", "n1_mse", "n1_half", "n1_rstd"))
        xn, h = sb("n1_xn", [P, 3, D]), [sb(f"n1_h{i}", [P, D]) for i in range(3)]
        tp = [ctx.enter_context(nc.psum_tensor(f"n1_tp{i}", [P, KC, P], F32)) for i in range(3)]
        x_in, pad_done, small_in = sem("n1_x_in"), sem("n1_pad"), sem("n1_small_in")
        squared, mean_ready, rstd_ready, scaled, h_ready, turned, placed, consts, passed = (
            sem("n1_" + n) for n in ("squared", "mean", "rstd", "scaled", "h", "turned", "placed", "consts", "passed"))
        block = ctx.enter_context(nc.Block())

        @block.sync
        def _(sp):
            sp.dma_start(x[:, 0:NT, :], d["x_prompt"][0].rearrange("(t p) n -> p t n", p=P)).then_inc(x_in, 16)
            sp.wait_ge(pad_done, 1)
            sp.dma_start(x[0:DEC, NT, :], d["x_sample"][0]).then_inc(x_in, 16)
            sp.dma_start(ident[:], d["ident"]).then_inc(small_in, 16)
            for s in range(2):
                sp.dma_start(modb[:, s, :, :], d["mod"][s:s + 1, 0:2 * D].to_broadcast([P, 2 * D])
                             .rearrange("p (a n) -> p a n", a=2)).then_inc(small_in, 16)

        @block.gpsimd
        def _(pool):
            nc.gpsimd.memset(x[:, NT, :], 0.0).then_inc(pad_done, 1)
            nc.gpsimd.memset(half[:], -0.5).then_inc(consts, 1)
            pool.wait_ge(consts, 1)
            pool.wait_ge(mean_ready, 1)
            nc.gpsimd.tensor_tensor(rstd[:], mse[:], half[:], ALU.pow).then_inc(rstd_ready, 1)

        @block.scalar
        def _(act):
            act.wait_ge(x_in, 32)
            for t in range(TILES):
                if t >= 2:
                    act.wait_ge(squared, t - 1)
                nc.scalar.activation(sq[:, t % 2, :], x[:, t, :], ACT.Square, scale=D ** -0.5,
                                     accum_out=ms[:, t:t + 1]).then_inc(squared, 1)

            with act.Fori(0, TILES // 3) as r:
                for u in range(3):
                    hold(act, passed, turned, r * 3 + (u + 1))
                    nc.scalar.activation(hT[:, :, bass.ds(r * (3 * P) + u * P, P)], tp[u][:], ACT.Copy).then_inc(placed, 1)

        @block.vector
        def _(dve):
            dve.wait_ge(squared, TILES)
            nc.vector.tensor_scalar(mse[:], ms[:], EPS, None, ALU.add).then_inc(mean_ready, 1)
            dve.wait_ge(rstd_ready, 1)
            dve.wait_ge(small_in, 48)

            def tile(t, u, s):
                nc.vector.scalar_tensor_tensor(xn[:, u, :], x[:, t, :], rstd[:, t:t + 1], modb[:, s, 1, :],
                                               ALU.mult, ALU.mult).then_inc(scaled, 1)
                dve.wait_ge(scaled, t + 1)
                if t >= 3:
                    dve.wait_ge(turned, t - 2)
                nc.vector.tensor_tensor(h[u][:], xn[:, u, :], modb[:, s, 0, :], ALU.add).then_inc(h_ready, 1)

            for t in range(TILES):
                tile(t, t % 3, t // NT)

        @block.tensor
        def _(pe):
            pe.wait_ge(small_in, 48)
            for t in range(TILES):
                pe.wait_ge(h_ready, t + 1)
                if t >= 3:
                    pe.wait_ge(placed, t - 2)
                for k in range(KC):
                    tr = nc.tensor.transpose(tp[t % 3][:, k, :], h[t % 3][:, k * P:(k + 1) * P], ident[:])
                tr.then_inc(turned, 1)


def project(nc, sem, d, hT, qkT, laT):
    RING = 6
    U_T, U_L, U_A = 2 * GH * GROUPS, GROUPS, GH * GROUPS
    with ExitStack() as ctx:
        def sb(name, shape, dt=F32):
            return ctx.enter_context(nc.sbuf_tensor(name, shape, dt))

        wt = [sb(f"pj_wt{i}", [P, KC, P]) for i in range(2)]
        wl = sb("pj_wl", [P, KC, GLR])
        wa = sb("pj_wa", [GLR, GH * GDK])
        ba = sb("pj_ba", [P, GH])
        wn = [sb(f"pj_wn{i}", [P, KC, BANK]) for i in range(2)]
        stage = [sb(f"pj_stage{i}", [P, BANK]) for i in range(RING)]
        lowT = sb("pj_lowT", [GLR, TOK])
        ax, ex, lx, mn = (sb("pj_" + n, [P, 2, GCOL]) for n in ("abs", "exp", "ln", "min"))
        acc = [ctx.enter_context(nc.psum_tensor(f"pj_acc{i}", [P, BANK], F32)) for i in range(RING)]
        wt_in = [sem(f"pj_wt_in{i}") for i in range(2)]
        wn_in = [sem(f"pj_wn_in{i}", True) for i in range(2)]
        out_done = [sem(f"pj_out{i}") for i in range(RING)]
        small_in = sem("pj_small_in", True)
        made, freed, staged, passed = (sem("pj_" + n) for n in ("made", "freed", "staged", "passed"))
        abs_done, exp_done, ln_done, min_done, sub_done, freed_la = (
            sem("pj_" + n) for n in ("abs", "exp", "ln", "min", "sub", "freed_la"))
        U0 = U_T + U_L
        UN = U0 + U_A
        PAIR = 2 * TILES
        w_in = d["w_in"][0]
        block = ctx.enter_context(nc.Block())

        def w_cols(start, n):
            return w_in[:, bass.ds(start, n)].rearrange("(k p) n -> p k n", p=P)

        @block.gpsimd
        def _(pool):
            nc.gpsimd.dma_start(wl[:], w_cols(W_GLR, GLR)).then_inc(small_in, 16)
            nc.gpsimd.dma_start(wa[:], d["w_alpha"][0]).then_inc(small_in, 16)
            nc.gpsimd.dma_start(ba[:], d["b_alpha"][0].rearrange("(h p) -> p h", p=P), allow_slow_non_contiguous=True).then_inc(small_in, 16)
            for i in range(4):
                if i >= 2:
                    pool.wait_ge(made, UN + (i - 1) * TILES)
                nc.gpsimd.dma_start(wn[i % 2][:], w_cols(W_GVR + i * BANK, BANK)).then_inc(wn_in[i % 2], 16)
            with pool.Fori(0, 3) as r:
                for i in range(2):
                    hold(pool, passed, made, r * PAIR + (UN + (3 + i) * TILES))
                    nc.gpsimd.dma_start(wn[i][:], w_cols(r * (2 * BANK) + (W_D + i * BANK), BANK)).then_inc(wn_in[i], 16)

        @block.sync
        def _(sp):
            for i in range(2):
                sp.dma_start(wt[i][:], w_cols(i * P, P)).then_inc(wt_in[i], 16)
            with sp.Fori(0, GH - 1) as r:
                for i in range(2):
                    hold(sp, passed, made, r * RING + (i + 1) * GROUPS)
                    sp.dma_start(wt[i][:], w_cols(r * (2 * P) + (2 + i) * P, P)).then_inc(wt_in[i], 16)
            with sp.Fori(0, 5) as r:
                for u in range(PAIR):
                    c, t = u // TILES, u % TILES
                    hold(sp, passed, staged, r * PAIR + (RING + u + 1))
                    dst = d["z"][t * P:(t + 1) * P, bass.ds(r * (2 * BANK) + c * BANK, BANK)]
                    sp.dma_start(dst, stage[u % RING][:]).then_inc(out_done[u % RING], 16)
            for i in range(RING):
                sp.wait_ge(out_done[i], 16 * 5 * PAIR // RING)

        @block.tensor
        def _(pe):
            with pe.Fori(0, GH) as r:
                for i in range(2):
                    hold(pe, passed, wt_in[i], r * 16 + 16)
                    for g in range(GROUPS):
                        u = i * GROUPS + g
                        hold(pe, passed, freed, r * RING + (u + 1))
                        for k in range(KC):
                            mm = nc.tensor.matmul(acc[u][:, 0:GCOL], wt[i][:, k, :], hT[:, k, g * GCOL:(g + 1) * GCOL],
                                                  start=(k == 0), stop=(k == KC - 1))
                        mm.then_inc(made, 1)
            pe.wait_ge(small_in, 48)
            for g in range(GROUPS):
                u = U_T + g
                pe.wait_ge(freed, u + 1)
                for k in range(KC):
                    mm = nc.tensor.matmul(acc[u % RING][0:GLR, 0:GCOL], wl[:, k, :], hT[:, k, g * GCOL:(g + 1) * GCOL],
                                          start=(k == 0), stop=(k == KC - 1))
                mm.then_inc(made, 1)
            pe.wait_ge(freed, RING + U0)
            for u in range(U_A):
                h, g = u // GROUPS, u % GROUPS
                if u >= RING:
                    pe.wait_ge(freed_la, u - RING + 1)
                nc.tensor.matmul(acc[(U0 + u) % RING][:, 0:GCOL], wa[:, h * GDK:(h + 1) * GDK],
                                 lowT[:, g * GCOL:(g + 1) * GCOL], start=True, stop=True).then_inc(made, 1)
            pe.wait_ge(freed_la, U_A)
            with pe.Fori(0, 5) as r:
                for u in range(PAIR):
                    c, t = u // TILES, u % TILES
                    if t == 0:
                        hold(pe, passed, wn_in[c], r * 16 + 16)
                    hold(pe, passed, staged, r * PAIR + (u + 1))
                    for k in range(KC):
                        mm = nc.tensor.matmul(acc[(UN + u) % RING][:], hT[:, k, t * P:(t + 1) * P], wn[c][:, k, :],
                                              start=(k == 0), stop=(k == KC - 1))
                    mm.then_inc(made, 1)

        @block.scalar
        def _(act):
            act.sem_inc(freed, RING)
            act.sem_inc(staged, RING)

            def place(r, first, scale):
                for u in range(RING):
                    i, g = u // GROUPS, u % GROUPS
                    hold(act, passed, made, r * RING + (first * RING + u + 1))
                    dst = qkT[:, bass.ds(r * (2 * TOK) + (first * 2 + i) * TOK + g * GCOL, GCOL)]
                    nc.scalar.activation(dst, acc[u][:, 0:GCOL], ACT.Copy, scale=scale).then_inc(freed, 1)

            with act.Fori(0, GH // 2) as r:
                place(r, 0, GDK ** -0.5)
            with act.Fori(0, GH // 2) as r:
                place(r, GH // 2, 1.0)
            for g in range(GROUPS):
                act.wait_ge(made, U_T + g + 1)
                nc.scalar.activation(lowT[:, g * GCOL:(g + 1) * GCOL], acc[(U_T + g) % RING][0:GLR, 0:GCOL],
                                     ACT.Copy).then_inc(freed, 1)
            act.wait_ge(small_in, 48)
            for u in range(U_A):
                h, b = u // GROUPS, u % 2
                act.wait_ge(made, U0 + u + 1)
                if u >= 2:
                    act.wait_ge(sub_done, u - 1)
                nc.scalar.activation(ax[:, b, :], acc[(U0 + u) % RING][:, 0:GCOL], ACT.Abs,
                                     bias=ba[:, h:h + 1]).then_inc(abs_done, 1)
                act.wait_ge(abs_done, u + 1)
                nc.scalar.activation(ex[:, b, :], ax[:, b, :], ACT.Exp, scale=-1.0).then_inc(exp_done, 1)
                act.wait_ge(exp_done, u + 1)
                nc.scalar.activation(lx[:, b, :], ex[:, b, :], ACT.Ln, bias=1.0).then_inc(ln_done, 1)

            def store(r, first, func):
                for u in range(PAIR):
                    hold(act, passed, made, r * PAIR + (UN + first * PAIR + u + 1))
                    if first or u >= RING:
                        n = first * (PAIR // RING) + u // RING
                        hold(act, passed, out_done[u % RING], r * (16 * (PAIR // RING)) + 16 * n)
                    nc.scalar.activation(stage[u % RING][:], acc[(UN + u) % RING][:], func).then_inc(staged, 1)

            store(0, 0, ACT.Copy)
            store(0, 1, ACT.Silu)
            with act.Fori(0, 3) as r:
                store(r, 2, ACT.Copy)

        @block.vector
        def _(dve):
            dve.wait_ge(small_in, 48)
            for u in range(U_A):
                h, g, b = u // GROUPS, u % GROUPS, u % 2
                dve.wait_ge(ln_done, u + 1)
                nc.vector.tensor_scalar(mn[:, b, :], acc[(U0 + u) % RING][:, 0:GCOL], ba[:, h:h + 1], 0.0,
                                        ALU.add, ALU.min).then_inc(min_done, 1)
                dve.wait_ge(min_done, u + 1)
                nc.vector.tensor_tensor(mn[:, b, :], mn[:, b, :], lx[:, b, :], ALU.subtract).then_inc(sub_done, 1)
                dve.wait_ge(sub_done, u + 1)
                nc.vector.tensor_scalar(laT[:, h, g * GCOL:(g + 1) * GCOL], mn[:, b, :], 1.0 / GTAU, None,
                                        ALU.mult).then_inc(freed_la, 1)


def gla(nc, sem, d, qkT, laT, oaT):
    NB = P // GBLK
    OFF = [GBLK * i * (i + 1) // 2 for i in range(NB + 1)]
    with ExitStack() as ctx:
        def sb(name, shape, dt=F32):
            return ctx.enter_context(nc.sbuf_tensor(name, shape, dt))

        def ps(name, shape):
            return ctx.enter_context(nc.psum_tensor(name, shape, F32))

        ident, causal, ones = sb("gl_ident", [P, P]), sb("gl_causal", [P, P]), sb("gl_ones", [P, P])
        gain = sb("gl_gain", [P, GDV])
        v = [sb(f"gl_v{i}", [P, GH * GDV]) for i in range(2)]
        gate = [sb(f"gl_gate{i}", [P, GH * GDV]) for i in range(2)]
        state = [sb("gl_state_p", [P, GH, GDV]), sb("gl_state_s", [P, GH, GDV])]
        cum = sb("gl_cum", [P, GH, P + 1])
        blk = sb("gl_blk", [P, GH, P])
        e_blk, e_cum, e_end = (sb("gl_e_" + n, [P, GH, P]) for n in ("blk", "cum", "end"))
        e_key = sb("gl_e_key", [P, GH, OFF[NB]])
        q_blk, q_cum, k_end = (sb("gl_" + n, [P, GH, P]) for n in ("q_blk", "q_cum", "k_end"))
        k_blk = sb("gl_k_blk", [P, GH, NB, P])
        attn = sb("gl_attn", [P, GH, P])
        k_tok = sb("gl_k_tok", [P, GH, GDK])
        sq = sb("gl_sq", [P, GH, GDV])
        ms, mse, rstd, half = (sb("gl_" + n, [P, GH]) for n in ("ms", "mse", "rstd", "half"))
        on = sb("gl_on", [P, GH * GDV])
        p_attn, p_k = ps("gl_p_attn", [P, GH, P]), ps("gl_p_k", [P, GH, P])
        p_o, p_kv, p_t = ps("gl_p_o", [P, GH, GDV]), ps("gl_p_kv", [P, GH, GDV]), ps("gl_p_t", [P, KC, P])
        names = ("small_in consts scanned blocked decays keyed scored masked turned_k placed_k out_made kv_made "
                 "state_ready squared mean rstd normed gated turned placed stored passed")
        (small_in, consts, scanned, blocked, decays, keyed, scored, masked, turned_k, placed_k, out_made, kv_made,
         state_ready, squared, mean_ready, rstd_ready, normed, gated, turned, placed, stored, passed) = (
            sem("gl_" + n) for n in names.split())
        v_in = [sem(f"gl_v_in{i}") for i in range(2)]
        block = ctx.enter_context(nc.Block())

        def at(r, u, each, c):
            return r * (2 * each) + (u * each + c)

        def over_tiles(eng, tile):
            with eng.Fori(0, NT // 2) as r:
                for u in range(2):
                    tile(r, u, P)
            tile(NT // 2, 0, DEC)

        @block.sync
        def _(sp):
            sp.dma_start(ident[:], d["ident"]).then_inc(small_in, 16)
            sp.dma_start(causal[:], d["causal"]).then_inc(small_in, 16)
            sp.dma_start(gain[:], d["gla_gain"].to_broadcast([P, GDV])).then_inc(small_in, 16)
            sp.dma_start(state[1][:], d["state_gla"][0, 0].rearrange("h k v -> k h v")).then_inc(small_in, 16)

            def load(r, u, n):
                hold(sp, passed, gated, at(r, u, 1, 1))
                for dst, part in ((v[u], ZV), (gate[u], ZR)):
                    sp.dma_start(dst[0:n, :], d["z"][bass.ds(r * (2 * P) + u * P, n), part * D:(part + 1) * D]).then_inc(v_in[u], 16)

            over_tiles(sp, load)
            sp.wait_ge(state_ready, GH * NT)
            sp.dma_start(d["gla_prompt"][0, 0].rearrange("h k v -> k h v"), state[0][:]).then_inc(stored, 16)
            sp.wait_ge(state_ready, GH * TILES)
            sp.dma_start(d["gla_sample"][0, 0].rearrange("h k v -> k h v"), state[1][:]).then_inc(stored, 16)
            sp.wait_ge(stored, 32)

        @block.gpsimd
        def _(pool):
            for t in (cum, k_blk, state[0]):
                nc.gpsimd.memset(t[:], 0.0).then_inc(consts, 1)
            nc.gpsimd.memset(ones[:], 1.0).then_inc(consts, 1)
            nc.gpsimd.memset(half[:], -0.5).then_inc(consts, 1)
            nc.gpsimd.memset(oaT[:, :, NT * P:TOK], 0.0).then_inc(consts, 1)
            pool.wait_ge(consts, 6)

            def tile(r, u, n):
                hold(pool, passed, mean_ready, at(r, u, 1, 1))
                nc.gpsimd.tensor_tensor(rstd[0:n, :], mse[0:n, :], half[0:n, :], ALU.pow).then_inc(rstd_ready, 1)

            over_tiles(pool, tile)

        @block.scalar
        def _(act):
            act.wait_ge(consts, 6)

            def tile(r, u, n):
                nb = n // GBLK
                for h in range(GH):
                    hold(act, passed, blocked, at(r, u, GH, h + 1))
                    nc.scalar.activation(e_blk[:, h, 0:n], blk[:, h, 0:n], ACT.Exp)
                    nc.scalar.activation(e_cum[:, h, 0:n], cum[:, h, 1:n + 1], ACT.Exp)
                    nc.scalar.activation(e_end[:, h, 0:n], cum[:, h, 1:n + 1], ACT.Exp, scale=-1.0, bias=cum[:, h, n:n + 1])
                    for i in range(nb):
                        e = nc.scalar.activation(e_key[:, h, OFF[i]:OFF[i + 1]], cum[:, h, 1:GBLK * (i + 1) + 1], ACT.Exp,
                                                 scale=-1.0, bias=cum[:, h, GBLK * i:GBLK * i + 1])
                    e.then_inc(decays, 1)
                hold(act, passed, turned_k, at(r, u, GH, GH))
                for h in range(GH):
                    nc.scalar.activation(k_tok[0:n, h, :], p_k[0:n, h, :], ACT.Copy).then_inc(placed_k, 1)
                hold(act, passed, out_made, at(r, u, GH, GH))
                for h in range(GH):
                    nc.scalar.activation(sq[0:n, h, :], p_o[0:n, h, :], ACT.Square, scale=GDV ** -0.5,
                                         accum_out=ms[0:n, h:h + 1]).then_inc(squared, 1)
                hold(act, passed, turned, at(r, u, 1, 1))
                nc.scalar.activation(oaT[:, :, bass.ds(r * (2 * P) + u * P, n)], p_t[:, :, 0:n], ACT.Copy).then_inc(placed, 1)

            over_tiles(act, tile)

        @block.vector
        def _(dve):
            dve.wait_ge(consts, 6)
            dve.wait_ge(small_in, 64)
            dve.sem_inc(gated, 2)

            def tile(r, u, n):
                nb = n // GBLK
                s = state[0 if n == P else 1]
                for h in range(GH):
                    nc.vector.tensor_tensor_scan(cum[:, h, 1:n + 1], ones[:, 0:n], laT[:, h, bass.ds(r * (2 * P) + u * P, n)],
                                                 0.0, ALU.mult, ALU.add).then_inc(scanned, 1)
                hold(dve, passed, scanned, at(r, u, GH, GH))
                for h in range(GH):
                    start = cum[:, h, 0:n].rearrange("p (b c) -> p b c", c=GBLK)[:, :, 0:1].to_broadcast([P, nb, GBLK])
                    nc.vector.tensor_tensor(blk[:, h, 0:n].rearrange("p (b c) -> p b c", c=GBLK),
                                            cum[:, h, 1:n + 1].rearrange("p (b c) -> p b c", c=GBLK), start,
                                            ALU.subtract).then_inc(blocked, 1)
                for h in range(GH):
                    hold(dve, passed, decays, at(r, u, GH, h + 1))
                    q = qkT[:, bass.ds(r * (2 * P) + (u * P + h * TOK), n)]
                    nc.vector.tensor_tensor(q_blk[:, h, 0:n], q, e_blk[:, h, 0:n], ALU.mult)
                    nc.vector.tensor_tensor(q_cum[:, h, 0:n], q, e_cum[:, h, 0:n], ALU.mult)
                    for i in range(nb):
                        w = GBLK * (i + 1)
                        k = qkT[:, bass.ds(r * (2 * P) + (u * P + (GH + h) * TOK), w)]
                        nc.vector.tensor_tensor(k_blk[:, h, i, 0:w], k, e_key[:, h, OFF[i]:OFF[i + 1]], ALU.mult)
                    k = qkT[:, bass.ds(r * (2 * P) + (u * P + (GH + h) * TOK), n)]
                    nc.vector.tensor_tensor(k_end[:, h, 0:n], k, e_end[:, h, 0:n], ALU.mult).then_inc(keyed, 1)
                hold(dve, passed, scored, at(r, u, GH, GH))
                for h in range(GH):
                    nc.vector.tensor_tensor(attn[0:n, h, 0:n], p_attn[0:n, h, 0:n], causal[0:n, 0:n], ALU.mult).then_inc(masked, 1)
                hold(dve, passed, kv_made, at(r, u, GH, GH))
                for h in range(GH):
                    nc.vector.scalar_tensor_tensor(s[:, h, :], s[:, h, :], e_cum[:, h, n - 1:n], p_kv[:, h, :],
                                                   ALU.mult, ALU.add).then_inc(state_ready, 1)
                hold(dve, passed, squared, at(r, u, GH, GH))
                nc.vector.tensor_scalar(mse[0:n, :], ms[0:n, :], EPS, None, ALU.add).then_inc(mean_ready, 1)
                hold(dve, passed, rstd_ready, at(r, u, 1, 1))
                for h in range(GH):
                    o = nc.vector.scalar_tensor_tensor(on[0:n, h * GDV:(h + 1) * GDV], p_o[0:n, h, :], rstd[0:n, h:h + 1],
                                                       gain[0:n, :], ALU.mult, ALU.mult)
                o.then_inc(normed, 1)
                hold(dve, passed, normed, at(r, u, 1, 1))
                nc.vector.tensor_tensor(on[0:n, :], on[0:n, :], gate[u][0:n, :], ALU.mult).then_inc(gated, 1)

            over_tiles(dve, tile)

        @block.tensor
        def _(pe):
            pe.wait_ge(small_in, 64)
            pe.wait_ge(consts, 6)

            def tile(r, u, n):
                s = state[0 if n == P else 1]
                for h in range(GH):
                    hold(pe, passed, keyed, at(r, u, GH, h + 1))
                    for i in range(n // GBLK):
                        mm = nc.tensor.matmul(p_attn[0:n, h, i * GBLK:(i + 1) * GBLK], k_blk[:, h, i, 0:n],
                                              q_blk[:, h, i * GBLK:(i + 1) * GBLK], start=True, stop=True)
                    mm.then_inc(scored, 1)
                    nc.tensor.transpose(p_k[0:n, h, :], k_end[:, h, 0:n], ident[:]).then_inc(turned_k, 1)
                hold(pe, passed, v_in[u], r * 32 + 32)
                for h in range(GH):
                    hold(pe, passed, masked, at(r, u, GH, h + 1))
                    nc.tensor.matmul(p_o[0:n, h, :], attn[0:n, h, 0:n], v[u][0:n, h * GDV:(h + 1) * GDV], start=True, stop=False)
                    nc.tensor.matmul(p_o[0:n, h, :], q_cum[:, h, 0:n], s[:, h, :], start=False, stop=True).then_inc(out_made, 1)
                for h in range(GH):
                    hold(pe, passed, placed_k, at(r, u, GH, h + 1))
                    nc.tensor.matmul(p_kv[:, h, :], k_tok[0:n, h, :], v[u][0:n, h * GDV:(h + 1) * GDV],
                                     start=True, stop=True).then_inc(kv_made, 1)
                hold(pe, passed, gated, at(r, u, 1, 3))
                for k in range(KC):
                    tr = nc.tensor.transpose(p_t[:, k, 0:n], on[0:n, k * P:(k + 1) * P], ident[0:n, 0:n])
                tr.then_inc(turned, 1)

            over_tiles(pe, tile)


def rope(nc, sem, d):
    N = 2 * DH
    H = HD // 2
    with ExitStack() as ctx:
        def sb(name, shape, dt=F32):
            return ctx.enter_context(nc.sbuf_tensor(name, shape, dt))

        ident = sb("rp_ident", [P, P])
        gains = sb("rp_gains", [P, 2, 2 * HD])
        cs, sn = sb("rp_cos", [P, TILES, H]), sb("rp_sin", [P, TILES, H])
        x = [sb(f"rp_x{i}", [P, 2, D]) for i in range(2)]
        cache = [sb(f"rp_cache{i}", [P, D]) for i in range(2)]
        sq = sb("rp_sq", [P, 2, D])
        ms, mse, rstd, half = (sb("rp_" + n, [P, 2 * N]) for n in ("ms", "mse", "rstd", "half"))
        own, other = sb("rp_own", [P, 2, 2 * HD]), sb("rp_other", [P, 2, 2 * HD])
        xn, xa, xb = (sb("rp_" + n, [P, 2, D]) for n in ("xn", "xa", "xb"))
        y = sb("rp_y", [P, 2, D])
        tT = [sb(f"rp_tT{i}", [P, DH, P]) for i in range(2)]
        p_t = [ctx.enter_context(nc.psum_tensor(f"rp_p_t{i}", [P, DH, P], F32)) for i in range(2)]
        names = "small_in consts squared summed mean rstd normed tabled own other rotated turned placed passed"
        (small_in, consts, squared, summed, mean_ready, rstd_ready, normed, tabled, own_done, other_done, rotated,
         turned, placed, passed) = (sem("rp_" + n) for n in names.split())
        krow_out = sem("rp_krow_out", True)
        x_in = [sem(f"rp_x_in{i}") for i in range(2)]
        c_in = [sem(f"rp_c_in{i}") for i in range(2)]
        t_out = [sem(f"rp_t_out{i}") for i in range(2)]
        v_out = sem("rp_v_out")
        block = ctx.enter_context(nc.Block())

        def at(r, u, each, c):
            return r * (2 * each) + (u * each + c)

        def over_tiles(eng, tile):
            for u in range(2):
                tile(0, u, P)
            with eng.Fori(1, NT // 2) as r:
                for u in range(2):
                    tile(r, u, P)
            tile(NT // 2, 0, DEC)

        @block.sync
        def _(sp):
            sp.dma_start(ident[:], d["ident"]).then_inc(small_in, 16)
            for a, g in enumerate(("q_gain", "k_gain")):
                sp.dma_start(gains[:, a, :], d[g].rearrange("o a c -> o (a c)").to_broadcast([P, 2 * HD])).then_inc(small_in, 16)
            sp.dma_start(cs[:], d["rope_cos"].rearrange("(t p) c -> p t c", p=P)).then_inc(small_in, 16)
            sp.dma_start(sn[:], d["rope_sin"].rearrange("(t p) c -> p t c", p=P)).then_inc(small_in, 16)

            def load(r, u, n):
                hold(sp, passed, normed, at(r, u, 1, 1))
                rows = d["z"][bass.ds(r * (2 * P) + u * P, P), ZQ * D:(ZK + 1) * D]
                sp.dma_start(x[u][:], rows.rearrange("p (a n) -> p a n", a=2)).then_inc(x_in[u], 16)

            over_tiles(sp, load)
            z_v = d["z"][:, ZDV * D:(ZDV + 1) * D]
            sp.dma_start(d["v_prompt"][0, 0].rearrange("t h v -> t (h v)"), z_v[0:SEQ, :]).then_inc(v_out, 16)
            sp.dma_start(d["v_sample"][0, 0].rearrange("t h v -> t (h v)"), z_v[SEQ:SEQ + DEC, :]).then_inc(v_out, 16)
            for c in range(PAST // P):
                if c >= 2:
                    sp.wait_ge(turned, 2 + 2 * TILES + c - 1)
                sp.dma_start(cache[c % 2][:], d["cache_k"][0, 0, c * P:(c + 1) * P].rearrange("t h v -> t (h v)")).then_inc(c_in[c % 2], 16)
            sp.wait_ge(v_out, 32)

        @block.gpsimd
        def _(pool):
            nc.gpsimd.memset(half[:], -0.5).then_inc(consts, 1)
            pool.wait_ge(consts, 1)

            def tile(r, u, n):
                hold(pool, passed, mean_ready, at(r, u, 1, 1))
                nc.gpsimd.tensor_tensor(rstd[:], mse[:], half[:], ALU.pow).then_inc(rstd_ready, 1)
                hold(pool, passed, rotated, at(r, u, 1, 1))
                dst = (d["k_prompt"][0, 0, bass.ds(r * (2 * P) + u * P, P)] if n == P else d["k_sample"][0, 0])
                nc.gpsimd.dma_start(dst.rearrange("t h c -> t (h c)"), y[0:n, 1, :]).then_inc(krow_out, 16)

            over_tiles(pool, tile)
            pool.wait_ge(krow_out, 16 * TILES)

        @block.scalar
        def _(act):
            def place(r, u, j, cols, name):
                hold(act, passed, turned, at(r, u, 2, j + 3))
                hold(act, passed, t_out[j], at(r, u, 16, 0))
                nc.scalar.activation(tT[j][:], p_t[j][:], ACT.Copy).then_inc(placed, 1)
                hold(act, passed, placed, at(r, u, 2, j + 3))
                act.dma_start(d[name][:, :, cols].rearrange("h p t -> p h t"), tT[j][:]).then_inc(t_out[j], 16)

            def tile(r, u, n):
                hold(act, passed, x_in[u], r * 16 + 16)
                hold(act, passed, summed, at(r, u, 1, 1))
                nc.scalar.activation(sq[:], x[u][:], ACT.Square, scale=HD ** -0.5).then_inc(squared, 1)
                cols = bass.ds(r * (2 * P) + u * P, P)
                for j, name in enumerate(("qT", "kT")):
                    place(r, u, j, cols, name)

            over_tiles(act, tile)
            for c in range(PAST // P):
                j = c % 2
                n = 2 + 2 * TILES + c
                act.wait_ge(turned, n + 1)
                act.wait_ge(t_out[j], 16 * (TILES + c // 2))
                nc.scalar.activation(tT[j][:], p_t[j][:], ACT.Copy).then_inc(placed, 1)
                act.wait_ge(placed, n + 1)
                act.dma_start(d["kT"][:, :, TOK + c * P:TOK + (c + 1) * P].rearrange("h p t -> p h t"), tT[j][:]).then_inc(t_out[j], 16)
            for j in range(2):
                act.wait_ge(t_out[j], 16 * (TILES + PAST // P // 2))

        @block.vector
        def _(dve):
            dve.wait_ge(small_in, 80)
            dve.sem_inc(normed, 2)
            dve.sem_inc(summed, 1)

            def halves(ap):
                return ap.rearrange("p (m e c) -> p m e c", m=2, e=2)

            def tile(r, u, n):
                t = r * 2 + u
                c, s = cs[:, bass.ds(t, 1), :], sn[:, bass.ds(t, 1), :]
                c = cs[:].rearrange("p t c -> p (t c)")[:, bass.ds(r * (2 * H) + u * H, H)]
                s = sn[:].rearrange("p t c -> p (t c)")[:, bass.ds(r * (2 * H) + u * H, H)]
                c4 = c.unsqueeze(1).to_broadcast([P, 4, H])
                s2 = s.unsqueeze(1).to_broadcast([P, 2, H])
                hold(dve, passed, other_done, at(r, u, 1, 1))
                for a in range(2):
                    scale = (HD ** -0.5, 1.0)[a]
                    g = gains[:, a, :]
                    nc.vector.scalar_tensor_tensor(own[:, a, :].rearrange("p (m c) -> p m c", m=4),
                                                   g.rearrange("p (m c) -> p m c", m=4), scale, c4, ALU.mult, ALU.mult)
                    gh, oh = halves(g), halves(other[:, a, :])
                    nc.vector.scalar_tensor_tensor(oh[:, :, 0, :], gh[:, :, 1, :], -scale, s2, ALU.mult, ALU.mult)
                    w = nc.vector.scalar_tensor_tensor(oh[:, :, 1, :], gh[:, :, 0, :], scale, s2, ALU.mult, ALU.mult)
                w.then_inc(tabled, 1)
                hold(dve, passed, squared, at(r, u, 1, 1))
                nc.vector.tensor_reduce(ms[:], sq[:].rearrange("p a (g c) -> p (a g) c", c=HD), AX.X, ALU.add).then_inc(summed, 1)
                hold(dve, passed, summed, at(r, u, 1, 2))
                nc.vector.tensor_scalar(mse[:], ms[:], EPS, None, ALU.add).then_inc(mean_ready, 1)
                hold(dve, passed, rstd_ready, at(r, u, 1, 1))
                nc.vector.tensor_tensor(xn[:].rearrange("p a (g c) -> p (a g) c", c=HD), x[u][:].rearrange("p a (g c) -> p (a g) c", c=HD),
                                        rstd[:].unsqueeze(2).to_broadcast([P, 2 * N, HD]), ALU.mult).then_inc(normed, 1)
                hold(dve, passed, normed, at(r, u, 1, 3))
                for a in range(2):
                    o = own[:, a, :].unsqueeze(1).to_broadcast([P, DH, 2 * HD])
                    nc.vector.tensor_tensor(xa[:, a, :].rearrange("p (h c) -> p h c", h=DH), xn[:, a, :].rearrange("p (h c) -> p h c", h=DH), o, ALU.mult)
                    for e in range(2):
                        for m in range(2):
                            def part(ap, e):
                                return ap.rearrange("p (h m e c) -> p h m e c", h=DH, m=2, e=2)[:, :, m, e, :]
                            f = other[:, a, :].rearrange("p (m e c) -> p m e c", m=2, e=2)[:, m, e, :].unsqueeze(1).to_broadcast([P, DH, H])
                            b = nc.vector.tensor_tensor(part(xb[:, a, :], e), part(xn[:, a, :], 1 - e), f, ALU.mult)
                b.then_inc(other_done, 1)
                hold(dve, passed, other_done, at(r, u, 1, 2))
                hold(dve, passed, turned, at(r, u, 2, 2))
                hold(dve, passed, krow_out, at(r, u, 16, 0))
                nc.vector.tensor_tensor(y[:], xa[:], xb[:], ALU.add).then_inc(rotated, 1)

            dve.sem_inc(other_done, 1)
            dve.sem_inc(turned, 2)
            dve.sem_inc(placed, 2)
            over_tiles(dve, tile)

        @block.tensor
        def _(pe):
            pe.wait_ge(small_in, 80)

            def tile(r, u, n):
                hold(pe, passed, rotated, at(r, u, 1, 1))
                for j in range(2):
                    hold(pe, passed, placed, at(r, u, 2, j + 1))
                    for h in range(DH):
                        tr = nc.tensor.transpose(p_t[j][:, h, :], y[:, j, h * P:(h + 1) * P], ident[:])
                    tr.then_inc(turned, 1)

            over_tiles(pe, tile)
            for c in range(PAST // P):
                j = c % 2
                pe.wait_ge(c_in[j], 16 * (c // 2 + 1))
                pe.wait_ge(placed, 2 * TILES + c + 1)
                for h in range(DH):
                    tr = nc.tensor.transpose(p_t[j][:, h, :], cache[j][:, h * P:(h + 1) * P], ident[:])
                tr.then_inc(turned, 1)


def attend(nc, sem, d, obT):
    KEYS = TOK + PAST
    HALF = P // 2
    UNITS = []
    for i in range(NT):
        tiles = [(j * P, j, P) for j in range(i + 1)]
        n = (i + 1) * P
        UNITS.append((i * P, P, tiles, [(c, c, min(BANK, n - c)) for c in range(0, n, BANK)]))
    UNITS.append((SEQ, DEC, [(TOK + j * P, TILES + j, P) for j in range(PAST // P)] + [(SEQ, NT, DEC)],
                  [(TOK, 0, PAST), (SEQ, PAST, DEC)]))
    NU = len(UNITS)
    GRP = [(i, g) for i, (_, _, tiles, _) in enumerate(UNITS) for g in range(0, len(tiles), 4)]
    NG = len(GRP)
    assert NG % 2 == 0
    with ExitStack() as ctx:
        def sb(name, shape, dt=F32):
            return ctx.enter_context(nc.sbuf_tensor(name, shape, dt))

        def ps(name, shape):
            return ctx.enter_context(nc.psum_tensor(name, shape, F32))

        ident = sb("at_ident", [P, P])
        lamv, lamp = sb("at_lamv", [P, 4, HD]), sb("at_lamp", [P, 2, HD])
        lams, lame, nlam = sb("at_lams", [P, 2]), sb("at_lame", [P, 2]), sb("at_nlam", [P, 1])
        gain = sb("at_gain", [P, VD])
        q = [sb(f"at_q{u}", [P, TOK]) for u in range(2)]
        k = [sb(f"at_k{u}", [P, KEYS]) for u in range(2)]
        v = [sb(f"at_v{u}", [P, TILES + PAST // P, VD]) for u in range(2)]
        prob = [sb(f"at_prob{m}", [P, SEQ]) for m in range(2)]
        mix = sb("at_mix", [P, SEQ])
        mixT = [sb(f"at_mixT{b}", [P, 4, P]) for b in range(2)]
        negmax, total, recip = (sb("at_" + n, [P, 2, 2]) for n in ("negmax", "total", "recip"))
        ratio = sb("at_ratio", [P, 2])
        out = [sb(f"at_out{u}", [P, TILES, VD]) for u in range(2)]
        sq = sb("at_sq", [P, TILES, VD])
        ms, mse, rstd, half = (sb("at_" + n, [P, TILES]) for n in ("ms", "mse", "rstd", "half"))
        p_s = [ps(f"at_p_s{m}", [P, SEQ]) for m in range(2)]
        p_t = [ps(f"at_p_t{b}", [P, 4, P]) for b in range(2)]
        p_o = [ps(f"at_p_o{b}", [P, BANK]) for b in range(2)]
        names = ("small_in consts lam_a lam_b lam_c masked recips ratios mixed turned copied applied "
                 "out_made out_read squared summed mean rstd normed gained head_turned head_placed passed")
        (small_in, consts, lam_a, lam_b, lam_c, masked, recips, ratios, mixed, turned, copied, applied, out_made, out_read,
         squared, summed, mean_ready, rstd_ready, normed, gained, head_turned, head_placed, passed) = (
            sem("at_" + n) for n in names.split())
        scored, maxed, exped = ([sem(f"at_{n}{m}") for m in range(2)] for n in ("scored", "maxed", "exped"))
        h_in = [sem(f"at_h_in{u}") for u in range(2)]
        block = ctx.enter_context(nc.Block())

        def at(r, u, each, c):
            return r * (2 * each) + (u * each + c)

        @block.sync
        def _(sp):
            sp.dma_start(ident[:], d["ident"]).then_inc(small_in, 16)
            for n, name in enumerate(("lam_q1", "lam_k1", "lam_q2", "lam_k2")):
                sp.dma_start(lamv[:, n, :], d[name].to_broadcast([P, HD])).then_inc(small_in, 16)
            sp.dma_start(gain[:], d["diff_gain"].to_broadcast([P, VD])).then_inc(small_in, 16)
            with sp.Fori(0, DH // 2) as r:
                for u in range(2):
                    hold(sp, passed, head_placed, at(r, u, 1, 1))
                    sp.dma_start(q[u][:], d["qT"][bass.ds(r * 2 + u, 1)].rearrange("o p t -> (o p) t")).then_inc(h_in[u], 16)
                    sp.dma_start(k[u][:], d["kT"][bass.ds(r * 2 + u, 1)].rearrange("o p t -> (o p) t")).then_inc(h_in[u], 16)
                    zv = d["z"][:, bass.ds(r * (2 * VD) + (ZDV * D + u * VD), VD)].rearrange("(t p) c -> p t c", p=P)
                    sp.dma_start(v[u][:, 0:TILES, :], zv).then_inc(h_in[u], 16)
                    cv = d["cache_v"][0, 0].rearrange("t h c -> t (h c)")[:, bass.ds(r * (2 * VD) + u * VD, VD)]
                    sp.dma_start(v[u][:, TILES:, :], cv.rearrange("(t p) c -> p t c", p=P)).then_inc(h_in[u], 16)

        @block.gpsimd
        def _(pool):
            nc.gpsimd.memset(half[:], -0.5).then_inc(consts, 1)
            for u in range(2):
                nc.gpsimd.memset(out[u][:, NT, :], 0.0).then_inc(consts, 1)
            pool.wait_ge(consts, 3)
            with pool.Fori(0, DH // 2) as r:
                for u in range(2):
                    hold(pool, passed, mean_ready, at(r, u, 1, 1))
                    nc.gpsimd.tensor_tensor(rstd[:], mse[:], half[:], ALU.pow).then_inc(rstd_ready, 1)

        @block.tensor
        def _(pe):
            pe.wait_ge(small_in, 96)

            def scores(r, u, i):
                qc, n, _, chunks = UNITS[i]
                for m in range(2):
                    hold(pe, passed, exped[m], at(r, u, NU, i + 1))
                    rows = slice(m * HD, (m + 1) * HD)
                    for kc, c, w in chunks:
                        mm = nc.tensor.matmul(p_s[m][0:n, c:c + w], q[u][rows, qc:qc + n], k[u][rows, kc:kc + w],
                                              start=True, stop=True)
                    mm.then_inc(scored[m], 1)

            def apply(r, u, i):
                _, n, tiles, _ = UNITS[i]
                hold(pe, passed, mixed, at(r, u, NU, i + 1))
                groups = [G for G, (a, _) in enumerate(GRP) if a == i]
                for G in groups:
                    b, first = G % 2, GRP[G][1]
                    hold(pe, passed, copied, at(r, u, NG, G + 1))
                    for j, (_, _, w) in enumerate(tiles[first:first + 4]):
                        tr = nc.tensor.transpose(p_t[b][0:w, j, 0:n], mix[0:n, (first + j) * P:(first + j) * P + w], ident[0:n, 0:n])
                    tr.then_inc(turned, 1)
                hold(pe, passed, out_read, at(r, u, NU, i + 1))
                for G in groups:
                    b, first = G % 2, GRP[G][1]
                    hold(pe, passed, copied, at(r, u, NG, 2 + G + 1))
                    for j, (_, vt, w) in enumerate(tiles[first:first + 4]):
                        mm = nc.tensor.matmul(p_o[(u * NU + i) % 2][0:n, 0:VD], mixT[b][0:w, j, 0:n], v[u][0:w, vt, :],
                                              start=(first + j == 0), stop=(first + j == len(tiles) - 1))
                    mm.then_inc(applied, 1)

            with pe.Fori(0, DH // 2) as r:
                for u in range(2):
                    hold(pe, passed, h_in[u], r * 64 + 64)
                    hold(pe, passed, head_placed, at(r, u, 1, 2))
                    scores(r, u, 0)
                    for i in range(NU):
                        if i + 1 < NU:
                            scores(r, u, i + 1)
                        apply(r, u, i)
                    hold(pe, passed, gained, at(r, u, 1, 1))
                    hold(pe, passed, exped[1], at(r, u, NU, 1 + NU))
                    for t in range(TILES):
                        dst = p_s[0][:, t * P:(t + 1) * P] if t < NT else p_s[1][:, 0:P]
                        tr = nc.tensor.transpose(dst, sq[:, t, :], ident[:])
                    tr.then_inc(head_turned, 1)

        @block.scalar
        def _(act):
            act.wait_ge(lam_a, 3)
            nc.scalar.activation(lame[:], lams[:], ACT.Exp).then_inc(lam_b, 1)
            for m in range(2):
                act.sem_inc(exped[m], 1)
            act.sem_inc(copied, 2)
            act.sem_inc(head_placed, 2)

            def exps(r, u, i):
                n, nk = UNITS[i][1], sum(w for _, _, w in UNITS[i][2])
                b = (u * NU + i) % 2
                for m in range(2):
                    hold(act, passed, maxed[m], at(r, u, NU, i + 1))
                    nc.scalar.activation(prob[m][0:n, 0:nk], p_s[m][0:n, 0:nk], ACT.Exp, bias=negmax[0:n, b, m:m + 1],
                                         accum_out=total[0:n, b, m:m + 1]).then_inc(exped[m], 1)

            def copies(r, u, i):
                n = UNITS[i][1]
                for G, (a, first) in enumerate(GRP):
                    if a == i:
                        part = UNITS[i][2][first:first + 4]
                        hold(act, passed, turned, at(r, u, NG, G + 1))
                        hold(act, passed, applied, at(r, u, NG, G + 1))
                        w = part[-1][2] if len(part) == 1 else P
                        nc.scalar.activation(mixT[G % 2][0:w, 0:len(part), 0:n], p_t[G % 2][0:w, 0:len(part), 0:n],
                                             ACT.Copy).then_inc(copied, 1)

            with act.Fori(0, DH // 2) as r:
                for u in range(2):
                    exps(r, u, 0)
                    for i in range(NU):
                        if i + 1 < NU:
                            exps(r, u, i + 1)
                        copies(r, u, i)
                    hold(act, passed, out_read, at(r, u, NU, 2 + NU))
                    nc.scalar.activation(sq[:], out[u][:], ACT.Square, scale=VD ** -0.5).then_inc(squared, 1)
                    hold(act, passed, head_turned, at(r, u, 1, 1))
                    nc.scalar.activation(obT[:, bass.ds(r * (2 * TOK) + u * TOK, SEQ)], p_s[0][:], ACT.Copy)
                    nc.scalar.activation(obT[:, bass.ds(r * (2 * TOK) + (u * TOK + SEQ), P)], p_s[1][:, 0:P],
                                         ACT.Copy).then_inc(head_placed, 1)

        @block.vector
        def _(dve):
            dve.wait_ge(small_in, 96)
            dve.sem_inc(applied, 2)
            dve.sem_inc(out_read, 2)
            lv = lamv[:].rearrange("p (a b) c -> p a b c", b=2)
            nc.vector.tensor_tensor(lamp[:], lv[:, :, 0, :], lv[:, :, 1, :], ALU.mult).then_inc(lam_a, 1)
            dve.wait_ge(lam_a, 1)
            nc.vector.tensor_reduce(lams[:], lamp[:], AX.X, ALU.add).then_inc(lam_a, 1)
            nc.vector.tensor_scalar(gain[:], gain[:], 1.0 - LAM_INIT, None, ALU.mult).then_inc(lam_a, 1)
            dve.wait_ge(lam_b, 1)
            nc.vector.tensor_tensor(nlam[:], lame[:, 1:2], lame[:, 0:1], ALU.subtract).then_inc(lam_c, 1)
            dve.wait_ge(lam_c, 1)
            nc.vector.tensor_scalar(nlam[:], nlam[:], -LAM_INIT, None, ALU.add).then_inc(lam_c, 1)
            dve.wait_ge(lam_c, 2)
            dve.wait_ge(consts, 3)

            def maxima(r, u, i):
                n, nk = UNITS[i][1], sum(w for _, _, w in UNITS[i][2])
                b = (u * NU + i) % 2
                for m in range(2):
                    hold(dve, passed, scored[m], at(r, u, NU, i + 1))
                    if i < NT:
                        nc.vector.memset(p_s[m][0:HALF, i * P + HALF:(i + 1) * P], -1e30).then_inc(masked, 1)
                for m in range(2):
                    if i < NT:
                        hold(dve, passed, masked, at(r, u, 2 * NT, 2 * i + m + 1))
                    nc.vector.tensor_reduce(negmax[0:n, b, m:m + 1], p_s[m][0:n, 0:nk], AX.X, ALU.max,
                                            negate=True).then_inc(maxed[m], 1)

            def combine(r, u, i):
                n, nk = UNITS[i][1], sum(w for _, _, w in UNITS[i][2])
                b = (u * NU + i) % 2
                hold(dve, passed, exped[1], at(r, u, NU, i + 2))
                nc.vector.reciprocal(recip[0:n, b, :], total[0:n, b, :]).then_inc(recips, 1)
                hold(dve, passed, recips, at(r, u, NU, i + 1))
                nc.vector.scalar_tensor_tensor(ratio[0:n, b:b + 1], recip[0:n, b, 1:2], nlam[0:n, :], total[0:n, b, 0:1],
                                               ALU.mult, ALU.mult).then_inc(ratios, 1)
                hold(dve, passed, ratios, at(r, u, NU, i + 1))
                nc.vector.scalar_tensor_tensor(mix[0:n, 0:nk], prob[1][0:n, 0:nk], ratio[0:n, b:b + 1], prob[0][0:n, 0:nk],
                                               ALU.mult, ALU.add).then_inc(mixed, 1)

            def read_out(r, u, i):
                n, b = UNITS[i][1], (u * NU + i) % 2
                G = max(G for G, (a, _) in enumerate(GRP) if a == i)
                hold(dve, passed, applied, at(r, u, NG, 2 + G + 1))
                nc.vector.tensor_scalar(out[u][0:n, i, :], p_o[b][0:n, 0:VD], recip[0:n, b, 0:1], None,
                                        ALU.mult).then_inc(out_read, 1)

            with dve.Fori(0, DH // 2) as r:
                for u in range(2):
                    maxima(r, u, 0)
                    for i in range(NU):
                        combine(r, u, i)
                        if i + 1 < NU:
                            maxima(r, u, i + 1)
                        read_out(r, u, i)
                    hold(dve, passed, squared, at(r, u, 1, 1))
                    nc.vector.tensor_reduce(ms[:], sq[:], AX.X, ALU.add).then_inc(summed, 1)
                    hold(dve, passed, summed, at(r, u, 1, 1))
                    nc.vector.tensor_scalar(mse[:], ms[:], EPS, None, ALU.add).then_inc(mean_ready, 1)
                    hold(dve, passed, rstd_ready, at(r, u, 1, 1))
                    nc.vector.tensor_tensor(sq[:], out[u][:], rstd[:].unsqueeze(2).to_broadcast([P, TILES, VD]),
                                            ALU.mult).then_inc(normed, 1)
                    hold(dve, passed, normed, at(r, u, 1, 1))
                    nc.vector.tensor_tensor(sq[:], sq[:], gain[:].unsqueeze(1).to_broadcast([P, TILES, VD]),
                                            ALU.mult).then_inc(gained, 1)


def merge(nc, sem, d, hT, oaT, obT):
    UNIT = 2 * GROUPS
    with ExitStack() as ctx:
        def sb(name, shape, dt=F32):
            return ctx.enter_context(nc.sbuf_tensor(name, shape, dt))

        w = [[sb(f"mg_w{i}_{n}", [P, KC, P]) for n in range(4)] for i in range(2)]
        sig = [sb(f"mg_sig{b}", [P, 2, GCOL]) for b in range(2)]
        prod = [sb(f"mg_prod{b}", [P, 2, GCOL]) for b in range(2)]
        m = [sb(f"mg_m{i}", [P, TOK]) for i in range(2)]
        p = [[ctx.enter_context(nc.psum_tensor(f"mg_p{b}_{n}", [P, BANK], F32)) for n in range(4)] for b in range(2)]
        made_g, made, gated, multiplied, summed, passed = (sem("mg_" + n) for n in ("made_g", "made", "gated", "multiplied", "summed", "passed"))
        w_in = [sem(f"mg_w_in{i}") for i in range(2)]
        m_out = [sem(f"mg_m_out{i}", True) for i in range(2)]
        obT3 = obT[:].rearrange("p (h t) -> p h t", h=DH)
        block = ctx.enter_context(nc.Block())

        @block.sync
        def _(sp):
            with sp.Fori(0, KC // 2) as r:
                for i in range(2):
                    hold(sp, passed, summed, r * UNIT + (i * GROUPS + 1))
                    for n, (src, col) in enumerate(((d["w_in"], W_GATE), (d["w_in"], W_GATE + D), (d["w_gla_out"], 0), (d["w_diff_out"], 0))):
                        cols = src[0, :, bass.ds(r * (2 * P) + (col + i * P), P)]
                        sp.dma_start(w[i][n][:], cols.rearrange("(k p) n -> p k n", p=P)).then_inc(w_in[i], 16)

        @block.tensor
        def _(pe):
            with pe.Fori(0, KC // 2) as r:
                for i in range(2):
                    hold(pe, passed, w_in[i], r * 64 + 64)
                    for g in range(GROUPS):
                        u = i * GROUPS + g
                        b, cols = u % 2, slice(g * GCOL, (g + 1) * GCOL)
                        hold(pe, passed, multiplied, r * UNIT + (u + 1))
                        for n, src in enumerate((hT, hT, oaT, obT3)):
                            for k in range(KC):
                                mm = nc.tensor.matmul(p[b][n][:, 0:GCOL], w[i][n][:, k, :], src[:, k, cols],
                                                      start=(k == 0), stop=(k == KC - 1))
                            if n == 1:
                                mm.then_inc(made_g, 1)
                        mm.then_inc(made, 1)

        @block.scalar
        def _(act):
            with act.Fori(0, KC // 2) as r:
                for u in range(UNIT):
                    b = u % 2
                    hold(act, passed, made_g, r * UNIT + (u + 1))
                    hold(act, passed, multiplied, r * UNIT + (u + 1))
                    for n in range(2):
                        s = nc.scalar.activation(sig[b][:, n, :], p[b][n][:, 0:GCOL], ACT.Sigmoid)
                    s.then_inc(gated, 1)

        @block.vector
        def _(dve):
            dve.sem_inc(multiplied, 2)
            dve.sem_inc(summed, UNIT + 1 - GROUPS)

            def unit(r, u):
                i, b, g = u // GROUPS, u % 2, u % GROUPS
                hold(dve, passed, gated, r * UNIT + (u + 1))
                hold(dve, passed, made, r * UNIT + (u + 1))
                for n in range(2):
                    x = nc.vector.tensor_tensor(prod[b][:, n, :], sig[b][:, n, :], p[b][2 + n][:, 0:GCOL], ALU.mult)
                x.then_inc(multiplied, 1)
                if g == 0:
                    hold(dve, passed, m_out[i], r * 16)
                hold(dve, passed, multiplied, r * UNIT + (2 + u + 1))
                nc.vector.tensor_tensor(m[i][:, g * GCOL:(g + 1) * GCOL], prod[b][:, 0, :], prod[b][:, 1, :],
                                        ALU.add).then_inc(summed, 1)

            for u in range(UNIT):
                unit(0, u)
            with dve.Fori(1, KC // 2) as r:
                for u in range(UNIT):
                    unit(r, u)

        @block.gpsimd
        def _(pool):
            with pool.Fori(0, KC // 2) as r:
                for i in range(2):
                    hold(pool, passed, summed, r * UNIT + (UNIT + 1 - GROUPS + (i + 1) * GROUPS))
                    nc.gpsimd.dma_start(d["mT"][bass.ds(r * 2 + i, 1)].rearrange("o p t -> (o p) t"), m[i][:]).then_inc(m_out[i], 16)
            for i in range(2):
                pool.wait_ge(m_out[i], 16 * KC // 2)


def mix_out(nc, sem, d, h2T):
    with ExitStack() as ctx:
        def sb(name, shape, dt=F32):
            return ctx.enter_context(nc.sbuf_tensor(name, shape, dt))

        ident, w = sb("mo_ident", [P, P]), sb("mo_w", [P, KC, D])
        rows = sb("mo_rows", [P, 2, 3, D])
        mt = [sb(f"mo_mt{u}", [P, KC, P]) for u in range(2)]
        x = [sb(f"mo_x{u}", [P, D]) for u in range(2)]
        xm, xs, sq = (sb("mo_" + n, [P, D]) for n in ("xm", "xs", "sq"))
        x1 = [sb(f"mo_x1{u}", [P, D]) for u in range(2)]
        h2 = [sb(f"mo_h2{u}", [P, D]) for u in range(2)]
        ms, mse, rstd, half = (sb("mo_" + n, [P, 1]) for n in ("ms", "mse", "rstd", "half"))
        p_m = [ctx.enter_context(nc.psum_tensor(f"mo_pm{b}", [P, D], F32)) for b in range(2)]
        p_t = ctx.enter_context(nc.psum_tensor("mo_pt", [P, KC, P], F32))
        names = "small_in consts made scaled added squared mean rstd normed shifted turned placed passed"
        (small_in, consts, made, scaled, added, squared, mean_ready, rstd_ready, normed, shifted, turned, placed,
         passed) = (sem("mo_" + n) for n in names.split())
        t_in = [sem(f"mo_t_in{u}") for u in range(2)]
        x1_out = [sem(f"mo_x1_out{u}", True) for u in range(2)]
        block = ctx.enter_context(nc.Block())

        def at(r, u, each, c):
            return r * (2 * each) + (u * each + c)

        def over_tiles(eng, tile):
            for u in range(2):
                tile(0, u, 0)
            with eng.Fori(1, NT // 2) as r:
                for u in range(2):
                    tile(r, u, 0)
            tile(NT // 2, 0, 1)

        def cols(r, u):
            return bass.ds(r * (2 * P) + u * P, P)

        @block.sync
        def _(sp):
            sp.dma_start(w[:], d["w_out"][0].rearrange("(k p) n -> p k n", p=P)).then_inc(small_in, 16)
            sp.dma_start(ident[:], d["ident"]).then_inc(small_in, 16)
            for s in range(2):
                sp.dma_start(rows[:, s, :, :], d["mod"][s:s + 1, GT1 * D:(SC2 + 1) * D].to_broadcast([P, 3 * D])
                             .rearrange("p (a n) -> p a n", a=3)).then_inc(small_in, 16)

            def tile(r, u, s):
                hold(sp, passed, added, at(r, u, 1, -1))
                sp.dma_start(mt[u][:], d["mT"][:, :, cols(r, u)].rearrange("k p t -> p k t")).then_inc(t_in[u], 16)
                if s:
                    sp.wait_ge(consts, 3)
                    sp.dma_start(x[u][0:DEC, :], d["x_sample"][0]).then_inc(t_in[u], 16)
                else:
                    sp.dma_start(x[u][:], d["x_prompt"][0, cols(r, u)]).then_inc(t_in[u], 16)

            over_tiles(sp, tile)

        @block.gpsimd
        def _(pool):
            nc.gpsimd.memset(half[:], -0.5).then_inc(consts, 1)
            pool.wait_ge(consts, 1)

            def tile(r, u, s):
                hold(pool, passed, mean_ready, at(r, u, 1, 1))
                nc.gpsimd.tensor_tensor(rstd[:], mse[:], half[:], ALU.pow).then_inc(rstd_ready, 1)
                hold(pool, passed, shifted, at(r, u, 1, 1))
                nc.gpsimd.dma_start(d["x1"][cols(r, u), :], x1[u][:]).then_inc(x1_out[u], 16)
                nc.gpsimd.dma_start(d["h2"][cols(r, u), :], h2[u][:]).then_inc(x1_out[u], 16)

            for u in range(2):
                tile(0, u, 0)
            with pool.Fori(1, NT // 2) as r:
                for u in range(2):
                    tile(r, u, 0)
            nc.gpsimd.memset(x[0][:], 0.0).then_inc(consts, 2)
            tile(NT // 2, 0, 1)
            pool.wait_ge(x1_out[0], 32 * (NT // 2 + 1))
            pool.wait_ge(x1_out[1], 32 * (NT // 2))

        @block.tensor
        def _(pe):
            pe.wait_ge(small_in, 64)

            def tile(r, u, s):
                hold(pe, passed, t_in[u], r * 32 + 32)
                hold(pe, passed, scaled, at(r, u, 1, -1))
                for c in range(2):
                    for k in range(KC):
                        mm = nc.tensor.matmul(p_m[u][:, c * BANK:(c + 1) * BANK], mt[u][:, k, :], w[:, k, c * BANK:(c + 1) * BANK],
                                              start=(k == 0), stop=(k == KC - 1))
                mm.then_inc(made, 1)

            def turn(r, u, s):
                hold(pe, passed, shifted, at(r, u, 1, 1))
                hold(pe, passed, placed, at(r, u, 1, 0))
                for k in range(KC):
                    tr = nc.tensor.transpose(p_t[:, k, :], h2[u][:, k * P:(k + 1) * P], ident[:])
                tr.then_inc(turned, 1)

            tile(0, 0, 0)
            tile(0, 1, 0)
            turn(0, 0, 0)
            with pe.Fori(1, NT // 2) as r:
                tile(r, 0, 0)
                turn(r - 1, 1, 0)
                tile(r, 1, 0)
                turn(r, 0, 0)
            tile(NT // 2, 0, 1)
            turn(NT // 2 - 1, 1, 0)
            turn(NT // 2, 0, 1)

        @block.scalar
        def _(act):
            def tile(r, u, s):
                hold(act, passed, added, at(r, u, 1, 1))
                nc.scalar.activation(sq[:], x1[u][:], ACT.Square, scale=D ** -0.5, accum_out=ms[:]).then_inc(squared, 1)
                hold(act, passed, turned, at(r, u, 1, 1))
                nc.scalar.activation(h2T[:, :, cols(r, u)], p_t[:], ACT.Copy).then_inc(placed, 1)

            over_tiles(act, tile)

        @block.vector
        def _(dve):
            dve.wait_ge(small_in, 64)

            def tile(r, u, s):
                hold(dve, passed, t_in[u], r * 32 + 32)
                hold(dve, passed, made, at(r, u, 1, 1))
                nc.vector.tensor_tensor(xm[:], p_m[u][:], rows[:, s, 0, :], ALU.mult).then_inc(scaled, 1)
                hold(dve, passed, scaled, at(r, u, 1, 1))
                hold(dve, passed, x1_out[u], r * 32)
                nc.vector.tensor_tensor(x1[u][:], xm[:], x[u][:], ALU.add).then_inc(added, 1)
                hold(dve, passed, squared, at(r, u, 1, 1))
                nc.vector.tensor_scalar(mse[:], ms[:], EPS, None, ALU.add).then_inc(mean_ready, 1)
                hold(dve, passed, rstd_ready, at(r, u, 1, 1))
                nc.vector.scalar_tensor_tensor(xs[:], x1[u][:], rstd[:], rows[:, s, 2, :], ALU.mult, ALU.mult).then_inc(normed, 1)
                hold(dve, passed, normed, at(r, u, 1, 1))
                hold(dve, passed, turned, at(r, u, 1, -1))
                nc.vector.tensor_tensor(h2[u][:], xs[:], rows[:, s, 1, :], ALU.add).then_inc(shifted, 1)

            over_tiles(dve, tile)


def keys(nc, sem, d, h2T):
    UNIT = 2 * GROUPS
    with ExitStack() as ctx:
        def sb(name, shape, dt=F32):
            return ctx.enter_context(nc.sbuf_tensor(name, shape, dt))

        ident = sb("ky_ident", [P, P])
        sub, subT = sb("ky_sub", [P, 2, P]), sb("ky_subT", [P, 2, P])
        w = [sb(f"ky_w{i}", [P, KC, P]) for i in range(2)]
        qc = [sb(f"ky_q{i}", [P, TOK]) for i in range(2)]
        sc = [sb(f"ky_s{i}", [P, TILES, NKEY]) for i in range(2)]
        p_q = [ctx.enter_context(nc.psum_tensor(f"ky_pq{g}", [P, BANK], F32)) for g in range(GROUPS)]
        p_s = [ctx.enter_context(nc.psum_tensor(f"ky_ps{g}", [P, GROUPS, NKEY], F32)) for g in range(TILES // 3)]
        small_in, turned, made, copied, scored, placed, passed = (
            sem("ky_" + n) for n in ("small_in", "turned", "made", "copied", "scored", "placed", "passed"))
        w_in = [sem(f"ky_w_in{i}") for i in range(2)]
        s_out = [sem(f"ky_s_out{i}", True) for i in range(2)]
        block = ctx.enter_context(nc.Block())

        @block.sync
        def _(sp):
            sp.dma_start(ident[:], d["ident"]).then_inc(small_in, 16)
            for n, s in enumerate(("sub_keys1", "sub_keys2")):
                sp.dma_start(sub[:, n, :], d[s][0]).then_inc(small_in, 16)
            with sp.Fori(0, PH) as r:
                for i in range(2):
                    hold(sp, passed, copied, r * UNIT + (i + 1) * GROUPS)
                    sp.dma_start(w[i][:], d["w_pq"][0, :, bass.ds(r * (2 * P) + i * P, P)].rearrange("(k p) n -> p k n", p=P)).then_inc(w_in[i], 16)

        @block.tensor
        def _(pe):
            pe.wait_ge(small_in, 48)
            for n in range(2):
                tr = nc.tensor.transpose(p_s[0][:, n, :], sub[:, n, :], ident[:])
            tr.then_inc(turned, 1)
            pe.wait_ge(turned, 2)
            with pe.Fori(0, PH) as r:
                for i in range(2):
                    hold(pe, passed, w_in[i], r * 16 + 16)
                    for g in range(GROUPS):
                        hold(pe, passed, copied, r * UNIT + (UNIT - GROUPS + i * GROUPS + g + 1))
                        for k in range(KC):
                            mm = nc.tensor.matmul(p_q[g][:, 0:GCOL], w[i][:, k, :], h2T[:, k, g * GCOL:(g + 1) * GCOL],
                                                  start=(k == 0), stop=(k == KC - 1))
                        mm.then_inc(made, 1)
                for i in range(2):
                    hold(pe, passed, copied, r * UNIT + (UNIT + (i + 1) * GROUPS))
                    for g in range(GROUPS):
                        hold(pe, passed, placed, r * UNIT + (i * GROUPS + g + 1))
                        for t in range(GROUPS):
                            c = (g * GROUPS + t) * P
                            mm = nc.tensor.matmul(p_s[g][:, t, :], qc[i][:, c:c + P], subT[:, i, :], start=True, stop=True)
                        mm.then_inc(scored, 1)

        @block.scalar
        def _(act):
            act.sem_inc(copied, UNIT)
            with act.Fori(0, PH) as r:
                for i in range(2):
                    hold(act, passed, scored, r * UNIT + (i + 1) * GROUPS)
                    for g in range(GROUPS):
                        hold(act, passed, made, r * UNIT + (i * GROUPS + g + 1))
                        nc.scalar.activation(qc[i][:, g * GCOL:(g + 1) * GCOL], p_q[g][:, 0:GCOL], ACT.Copy).then_inc(copied, 1)

        @block.vector
        def _(dve):
            dve.sem_inc(placed, GROUPS)
            dve.sem_inc(scored, UNIT)
            dve.wait_ge(turned, 1)
            nc.vector.tensor_copy(subT[:], p_s[0][:, 0:2, :]).then_inc(turned, 1)

            def round_(r):
                for i in range(2):
                    hold(dve, passed, s_out[i], r * 16)
                    for g in range(GROUPS):
                        hold(dve, passed, scored, r * UNIT + (UNIT + i * GROUPS + g + 1))
                        nc.vector.tensor_copy(sc[i][:, g * GROUPS:(g + 1) * GROUPS, :], p_s[g][:]).then_inc(placed, 1)

            round_(0)
            with dve.Fori(1, PH) as r:
                round_(r)

        @block.gpsimd
        def _(pool):
            with pool.Fori(0, PH) as r:
                for i in range(2):
                    hold(pool, passed, placed, r * UNIT + (GROUPS + (i + 1) * GROUPS))
                    dst = d["scores"].rearrange("t j n -> t (j n)")[:, bass.ds(r * (2 * NKEY) + i * NKEY, NKEY)]
                    nc.gpsimd.dma_start(dst.rearrange("(t p) n -> p t n", p=P), sc[i][:]).then_inc(s_out[i], 16)
            for i in range(2):
                pool.wait_ge(s_out[i], 16 * PH)


def retrieve(nc, sem, d):
    SLOTS = PH * TOPK
    W, RING = 8, 16
    ROUNDS = SLOTS // RING
    FAR = -3.0e38
    with ExitStack() as ctx:
        def sb(name, shape, dt=F32):
            return ctx.enter_context(nc.sbuf_tensor(name, shape, dt))

        ident = sb("rt_ident", [P, P])
        zero = sb("rt_zero", [P, BANK])
        iota = sb("rt_iota", [P, TOPK])
        gate2 = sb("rt_gate2", [P, 2, D])
        sc, sc2 = sb("rt_sc", [P, 2 * PH, NKEY]), sb("rt_sc2", [P, 2 * PH, NKEY])
        val, ind, indf = sb("rt_val", [P, 2 * PH, TOPK]), sb("rt_ind", [P, 2 * PH, TOPK], U32), sb("rt_indf", [P, 2 * PH, TOPK])
        cand, cand2 = sb("rt_cand", [P, PH, TOPK * TOPK]), sb("rt_cand2", [P, PH, TOPK * TOPK])
        best, pos = sb("rt_best", [P, PH, TOPK]), sb("rt_pos", [P, PH, TOPK], U32)
        part, partf = sb("rt_part", [P, 2, SLOTS], U32), sb("rt_partf", [P, 2, SLOTS])
        pick = [sb(f"rt_pick{i}", [P, SLOTS, TOPK]) for i in range(2)]
        chosen = sb("rt_chosen", [P, 2, SLOTS])
        idxf = sb("rt_idxf", [P, SLOTS])
        idx = [sb(f"rt_idx{u}", [P, SLOTS], U32) for u in range(2)]
        win = [sb(f"rt_win{w}", [P, W], U32) for w in range(2)]
        below, e, esum, erec = sb("rt_below", [P, PH, TOPK]), sb("rt_e", [P, PH, TOPK]), sb("rt_esum", [P, PH]), sb("rt_erec", [P, PH])
        prob = [sb(f"rt_prob{u}", [P, SLOTS]) for u in range(2)]
        dot, act_dot = sb("rt_dot", [P, SLOTS]), sb("rt_act_dot", [P, SLOTS])
        weight = sb("rt_weight", [P, SLOTS])
        h2 = [sb(f"rt_h2{u}", [P, D]) for u in range(2)]
        x1 = [sb(f"rt_x1{u}", [P, D]) for u in range(2)]
        y = [sb(f"rt_y{u}", [P, D]) for u in range(2)]
        ring = [sb(f"rt_ring{b}", [P, D]) for b in range(RING)]
        diag = [sb(f"rt_diag{b}", [P, P]) for b in range(W)]
        ffn = ctx.enter_context(nc.psum_tensor("rt_ffn", [P, D], F32))
        names = ("small_in consts sc_in sc_used step idx_ready shifted exped dotted gelued weighted diag_ready added "
                 "summed_v ffn_read y_ready windowed passed")
        (small_in, consts, sc_in, sc_used, step, idx_ready, shifted, exped, dotted, gelued, weighted, diag_ready, added,
         ffn_done, ffn_read, y_ready, windowed, passed) = (sem("rt_" + n) for n in names.split())
        rows_in = [sem(f"rt_rows_in{u}") for u in range(2)]
        slot_in = [sem(f"rt_slot_in{b}", True) for b in range(RING)]
        y_out = [sem(f"rt_y_out{u}") for u in range(2)]
        block = ctx.enter_context(nc.Block())

        def at(r, u, each, c):
            return r * (2 * each) + (u * each + c)

        def over_tiles(eng, tile):
            with eng.Fori(0, NT // 2) as r:
                for u in range(2):
                    tile(r, u, P)
            tile(NT // 2, 0, DEC)

        @block.sync
        def _(sp):
            sp.dma_start(ident[:], d["ident"]).then_inc(small_in, 16)
            sp.dma_start(iota[:], d["iota"].to_broadcast([P, TOPK])).then_inc(small_in, 16)
            for s in range(2):
                sp.dma_start(gate2[:, s, :], d["mod"][s:s + 1, GT2 * D:].to_broadcast([P, D])).then_inc(small_in, 16)

            def load(r, u, n):
                rows = bass.ds(r * (2 * P) + u * P, P)
                hold(sp, passed, sc_used, at(r, u, 1, 1))
                sp.dma_start(sc[:], d["scores"][rows]).then_inc(sc_in, 16)
                hold(sp, passed, y_ready, at(r, u, 1, 1))
                sp.dma_start(h2[u % 2][:], d["h2"][rows]).then_inc(rows_in[u % 2], 16)
                sp.dma_start(x1[u % 2][:], d["x1"][rows]).then_inc(rows_in[u % 2], 16)

            def store(r, u, n):
                hold(sp, passed, y_ready, at(r, u, 1, 3))
                dst = d["y_prompt"][0, bass.ds(r * (2 * P) + u * P, P)] if n == P else d["y_sample"][0]
                sp.dma_start(dst, y[u % 2][0:n, :]).then_inc(y_out[u % 2], 16)

            load(0, 0, P)
            load(0, 1, P)
            with sp.Fori(0, NT // 2 - 1) as r:
                for u in range(2):
                    store(r, u, P)
                    load(r, u + 2, P)
            store(NT // 2 - 1, 0, P)
            load(NT // 2, 0, DEC)
            store(NT // 2 - 1, 1, P)
            store(NT // 2, 0, DEC)
            sp.wait_ge(y_out[0], 16 * (NT // 2 + 1))
            sp.wait_ge(y_out[1], 16 * (NT // 2))

        @block.gpsimd
        def _(pool):
            nc.gpsimd.memset(zero[:], 0.0).then_inc(consts, 1)

            def fetch(r, u, n, table, first_dot, first_add, phase):
                with pool.Fori(0, ROUNDS) as q:
                    for w in range(2):
                        hold(pool, passed, dotted, first_dot(q, w))
                        hold(pool, passed, added, first_add(q, w))
                        nc.gpsimd.tensor_copy(win[w][0:n, :], idx[u][0:n, bass.ds(q * RING + w * W, W)]).then_inc(windowed, 1)
                        hold(pool, passed, windowed, at(r, u, 4 * ROUNDS, phase * 2 * ROUNDS + w + 1) + q * 2)
                        for b in range(W):
                            s = w * W + b
                            nc.gpsimd.indirect_dma_start(ring[s][0:n, :], None, table,
                                                         bass.IndirectOffsetOnAxis(ap=win[w][0:n, b:b + 1], axis=0)).then_inc(slot_in[s], 16)

            def tile(r, u, n):
                hold(pool, passed, idx_ready, at(r, u, 1, 1))
                fetch(r, u, n, d["peer_u"][0],
                      lambda q, w: at(r, u, SLOTS, W * (w + 1)) + q * RING,
                      lambda q, w: at(r, u, SLOTS, W * (w + 1)), 0)
                fetch(r, u, n, d["peer_v"][0],
                      lambda q, w: at(r, u, SLOTS, SLOTS + W * (w + 1)),
                      lambda q, w: at(r, u, SLOTS, W * (w + 1)) + q * RING, 1)

            over_tiles(pool, tile)

        @block.scalar
        def _(act):
            def softmax_exp(r, u):
                hold(act, passed, shifted, at(r, u, 1, 1))
                nc.scalar.activation(e[:], below[:], ACT.Exp).then_inc(exped, 1)

            def tile(r, u, n):
                hold(act, passed, dotted, at(r, u, SLOTS, RING + SLOTS))
                nc.scalar.activation(act_dot[0:n, :], dot[0:n, :], ACT.Gelu).then_inc(gelued, 1)
                hold(act, passed, weighted, at(r, u, 1, 1))
                with act.Fori(0, ROUNDS) as q:
                    for s in range(RING):
                        hold(act, passed, added, at(r, u, SLOTS, RING + s + 1 - W) + q * RING)
                        nc.scalar.activation(diag[s % W][0:n, 0:n], ident[0:n, 0:n], ACT.Copy,
                                             scale=weight[0:n, bass.ds(q * RING + s, 1)]).then_inc(diag_ready, 1)
                if n == P:
                    softmax_exp(r, u + 1)

            act.wait_ge(small_in, 64)
            softmax_exp(0, 0)
            over_tiles(act, tile)

        @block.tensor
        def _(pe):
            pe.wait_ge(consts, 1)
            pe.wait_ge(small_in, 64)

            def edge(n, first):
                for c in range(D // BANK):
                    mm = nc.tensor.matmul(ffn[0:n, c * BANK:(c + 1) * BANK], zero[0:n, 0:n], zero[0:n, :],
                                          start=first, stop=not first)
                return mm

            def tile(r, u, n):
                hold(pe, passed, ffn_read, at(r, u, 1, 1))
                edge(n, True)
                with pe.Fori(0, ROUNDS) as q:
                    for s in range(RING):
                        hold(pe, passed, diag_ready, at(r, u, SLOTS, s + 1) + q * RING)
                        hold(pe, passed, slot_in[s], at(r, u, 32 * ROUNDS, 16 * ROUNDS + 16) + q * 16)
                        for c in range(D // BANK):
                            mm = nc.tensor.matmul(ffn[0:n, c * BANK:(c + 1) * BANK], diag[s % W][0:n, 0:n],
                                                  ring[s][0:n, c * BANK:(c + 1) * BANK], start=False, stop=False)
                        mm.then_inc(added, 1)
                edge(n, False).then_inc(ffn_done, 1)

            over_tiles(pe, tile)

        @block.vector
        def _(dve):
            dve.wait_ge(small_in, 64)
            dve.sem_inc(sc_used, 1)
            dve.sem_inc(y_ready, 2)
            dve.sem_inc(dotted, RING)
            dve.sem_inc(added, RING)
            dve.sem_inc(ffn_read, 1)
            STEPS = 18

            def select(r, u):
                done = [0]

                def settle(ins):
                    done[0] += 1
                    ins.then_inc(step, 1)
                    hold(dve, passed, step, at(r, u, STEPS, done[0]))

                hold(dve, passed, sc_in, at(r, u, 16, 16))
                maps, heads = range(2 * PH), range(PH)

                def top16(rows, values, spare, top, where):
                    for j in rows:
                        m = nc.vector.max(top[:, j, 0:8], values[:, j, :])
                    settle(m)
                    for j in rows:
                        nc.vector.max_index(where[:, j, 0:8], top[:, j, 0:8], values[:, j, :])
                        m = nc.vector.match_replace(spare[:, j, :], top[:, j, 0:8], values[:, j, :], FAR)
                    settle(m)
                    for j in rows:
                        m = nc.vector.max(top[:, j, 8:16], spare[:, j, :])
                    settle(m)
                    for j in rows:
                        m = nc.vector.max_index(where[:, j, 8:16], top[:, j, 8:16], spare[:, j, :])
                    settle(m)

                top16(maps, sc, sc2, val, ind)
                dve.sem_inc(sc_used, 1)
                pair = val[:].rearrange("p (h e) k -> p h e k", e=2)
                nc.vector.tensor_copy(indf[:], ind[:])
                settle(nc.vector.tensor_tensor(cand[:].rearrange("p h (i j) -> p h i j", j=TOPK),
                                               pair[:, :, 0, :].unsqueeze(3).to_broadcast([P, PH, TOPK, TOPK]),
                                               pair[:, :, 1, :].unsqueeze(2).to_broadcast([P, PH, TOPK, TOPK]), ALU.add))
                top16(heads, cand, cand2, best, pos)
                nc.vector.tensor_tensor(below[:], best[:], best[:, :, 0:1].to_broadcast([P, PH, TOPK]), ALU.subtract).then_inc(shifted, 1)
                flat = pos[:].rearrange("p h k -> p (h k)")
                nc.vector.tensor_scalar(part[:, 0, :], flat, 4, None, ALU.logical_shift_right)
                settle(nc.vector.tensor_scalar(part[:, 1, :], flat, TOPK - 1, None, ALU.bitwise_and))
                settle(nc.vector.tensor_copy(partf[:], part[:]))
                for i in range(2):
                    eq = nc.vector.tensor_tensor(pick[i][:], partf[:, i, :].unsqueeze(2).to_broadcast([P, SLOTS, TOPK]),
                                                 iota[:].unsqueeze(1).to_broadcast([P, SLOTS, TOPK]), ALU.is_equal)
                settle(eq)
                lists = indf[:].rearrange("p (h e) k -> p h e k", e=2)
                for i in range(2):
                    grid = pick[i][:].rearrange("p (h k) i -> p h k i", h=PH)
                    mu = nc.vector.tensor_tensor(grid, grid, lists[:, :, i, :].unsqueeze(2).to_broadcast([P, PH, TOPK, TOPK]), ALU.mult)
                settle(mu)
                for i in range(2):
                    re = nc.vector.tensor_reduce(chosen[:, i, :], pick[i][:], AX.X, ALU.add)
                settle(re)
                settle(nc.vector.scalar_tensor_tensor(idxf[:], chosen[:, 0, :], float(NKEY), chosen[:, 1, :], ALU.mult, ALU.add))
                nc.vector.tensor_copy(idx[u % 2][:], idxf[:]).then_inc(idx_ready, 1)
                hold(dve, passed, exped, at(r, u, 1, 1))
                settle(nc.vector.tensor_reduce(esum[:], e[:], AX.X, ALU.add))
                settle(nc.vector.reciprocal(erec[:], esum[:]))
                nc.vector.tensor_tensor(prob[u % 2][:].rearrange("p (h k) -> p h k", h=PH), e[:],
                                        erec[:].unsqueeze(2).to_broadcast([P, PH, TOPK]), ALU.mult).then_inc(step, 1)
                assert done[0] + 1 == STEPS, done

            def dots(r, u, n):
                hold(dve, passed, rows_in[u % 2], r * 32 + (32 + 32 * (u // 2)))
                with dve.Fori(0, ROUNDS) as q:
                    for s in range(RING):
                        hold(dve, passed, slot_in[s], at(r, u, 32 * ROUNDS, 16) + q * 16)
                        nc.vector.scalar_tensor_tensor(ring[s][0:n, :], ring[s][0:n, :], 1.0, h2[u % 2][0:n, :], ALU.mult, ALU.mult,
                                                       accum_out=dot[0:n, bass.ds(q * RING + s, 1)]).then_inc(dotted, 1)

            def weigh(r, u, n):
                hold(dve, passed, gelued, at(r, u, 1, 1))
                hold(dve, passed, step, at(r, u, STEPS, STEPS))
                nc.vector.tensor_tensor(weight[0:n, :], act_dot[0:n, :], prob[u % 2][0:n, :], ALU.mult).then_inc(weighted, 1)

            def finish(r, u, n):
                b = u % 2
                hold(dve, passed, ffn_done, at(r, u, 1, 1))
                hold(dve, passed, y_out[b], r * 16 + 16 * (u // 2))
                nc.vector.tensor_tensor(y[b][0:n, :], ffn[0:n, :], gate2[0:n, 0 if n == P else 1, :], ALU.mult).then_inc(ffn_read, 1)
                hold(dve, passed, ffn_read, at(r, u, 1, 2))
                nc.vector.tensor_tensor(y[b][0:n, :], y[b][0:n, :], x1[b][0:n, :], ALU.add).then_inc(y_ready, 1)

            def turn(r, u, n, after):
                weigh(r, u, n)
                select(r, u + 1)
                dots(r, u + 1, after)
                finish(r, u, n)

            select(0, 0)
            dots(0, 0, P)
            for u in range(2):
                turn(0, u, P, P)
            with dve.Fori(1, NT // 2 - 1) as r:
                for u in range(2):
                    turn(r, u, P, P)
            turn(NT // 2 - 1, 0, P, P)
            turn(NT // 2 - 1, 1, P, DEC)
            weigh(NT // 2, 0, DEC)
            finish(NT // 2, 0, DEC)


SCRATCH = {"mod": (2, 6 * D), "z": (TOK, 5 * D), "qT": (DH, P, TOK), "kT": (DH, P, TOK + PAST), "mT": (KC, P, TOK), "x1": (TOK, D), "h2": (TOK, D),
           "scores": (TOK, 2 * PH, NKEY)}


def trunk(nc, d):
    for name, shape in SCRATCH.items():
        if name not in d:
            d[name] = nc.dram_tensor(name, shape, F32, kind="Internal").ap()
    def stage(build, *args):
        with ExitStack() as ctx:
            used = []

            def sem(name, software_dma=False):
                if software_dma:
                    return nc.alloc_semaphore(name)
                used.append(ctx.enter_context(nc.semaphore(name)))
                return used[-1]

            build(nc, sem, d, *args)
            with nc.Block() as block:
                @block.sync
                def _(sp):
                    for s in used:
                        sp.sem_clear(s)

    stage(modulation)
    with ExitStack() as outer:
        hT = outer.enter_context(nc.sbuf_tensor("hT", [P, KC, TOK], F32))
        stage(norm_in, hT)
        oaT = outer.enter_context(nc.sbuf_tensor("oaT", [P, KC, TOK], F32))
        with ExitStack() as inner:
            qkT = inner.enter_context(nc.sbuf_tensor("qkT", [P, 2 * GH * TOK], F32))
            laT = inner.enter_context(nc.sbuf_tensor("laT", [P, GH, TOK], F32))
            stage(project, hT, qkT, laT)
            stage(gla, qkT, laT, oaT)
        stage(rope)
        obT = outer.enter_context(nc.sbuf_tensor("obT", [P, DH * TOK], F32))
        stage(attend, obT)
        stage(merge, hT, oaT, obT)
    with ExitStack() as outer:
        h2T = outer.enter_context(nc.sbuf_tensor("h2T", [P, KC, TOK], F32))
        stage(mix_out, h2T)
        stage(keys, h2T)
    stage(retrieve)


def _inputs(inputs):
    import numpy as np
    out = {k: np.ascontiguousarray(v) for k, v in inputs.items()}
    out["ident"] = np.eye(P, dtype=np.float32)
    out["iota"] = np.arange(TOPK, dtype=np.float32)[None, :]
    out["causal"] = np.triu(np.ones((P, P), np.float32))
    pos = np.concatenate([np.arange(SEQ), PAST + np.arange(P)]).astype(np.float64)
    inv = (np.float32(10000.0) ** (-np.arange(HD // 2, dtype=np.float32) / np.float32(HD // 2)))
    ang = pos.astype(np.float32)[:, None] * inv[None, :]
    out["rope_cos"] = np.cos(ang).astype(np.float32)
    out["rope_sin"] = np.sin(ang).astype(np.float32)
    return out


_OUTS = [("y_prompt", (1, SEQ, D)), ("y_sample", (1, DEC, D)),
         ("k_prompt", (1, 1, SEQ, DH, 2 * HD)), ("v_prompt", (1, 1, SEQ, DH, VD)), ("gla_prompt", (1, 1, GH, GDK, GDV)),
         ("k_sample", (1, 1, DEC, DH, 2 * HD)), ("v_sample", (1, 1, DEC, DH, VD)), ("gla_sample", (1, 1, GH, GDK, GDV))]


def kernel(**inputs):
    import concourse.bacc as bacc
    from concourse.bass_utils import run_bass_kernel_spmd

    nc = bacc.Bacc("TRN2", target_bir_lowering=False, num_devices=1)
    arrays, d = {}, {}
    for name, a in _inputs(inputs).items():
        arrays["in_" + name] = a
        d[name] = nc.dram_tensor("in_" + name, a.shape, mybir.dt.from_np(a.dtype), kind="ExternalInput").ap()
    for name, shape in _OUTS:
        d[name] = nc.dram_tensor("out_" + name, shape, F32, kind="ExternalOutput").ap()
    trunk(nc, d)
    r = run_bass_kernel_spmd(nc, [arrays], core_ids=[0])
    return tuple(r.results[0]["out_" + name] for name, _ in _OUTS)
```

```python
import concourse.bass as bass
from concourse import mybir
from contextlib import ExitStack

F32 = mybir.dt.float32
U32 = mybir.dt.uint32
ACT = mybir.ActivationFunctionType
ALU = mybir.AluOpType
AX = mybir.AxisListType

D = 1024
P = 128
KC = D // P
SEQ, DEC = 1024, 32
PAST = 512
NT = SEQ // P
TILES = NT + 1
TOK = TILES * P
EPS = 1e-6
GH, GDK, GDV, GLR, GBLK = 4, 128, 256, 16, 16
GTAU = 16.0
DH, HD, VD = 8, 64, 128
LAM_INIT = 0.2
PH, NKEY, TOPK = 8, 128, 16
BANK = 512
GROUPS, GCOL = 3, TOK // 3
W_QK, W_GVR, W_GLR = 0, 2 * GH * GDK, 2 * GH * GDK + 2 * GH * GDV
W_D = W_GLR + GLR
W_GATE = W_D + 3 * D
SH1, SC1, GT1, SH2, SC2, GT2 = range(6)
ZV, ZR, ZQ, ZK, ZDV = range(5)


def hold(eng, passed, sem, value):
    if isinstance(value, int) and value <= 0:
        return
    eng.wait_ge(sem, value)
    eng.sem_inc(passed, 1)



def modulation(nc, sem, d):
    CH, RING = 6 * D // BANK, 3
    with ExitStack() as ctx:
        def sb(name, shape, dt=F32):
            return ctx.enter_context(nc.sbuf_tensor(name, shape, dt))

        c_raw = sb("c_raw", [P, 2, KC])
        c_act = sb("c_act", [P, KC, 2])
        w = [sb(f"w_mod{i}", [P, KC, BANK]) for i in range(RING)]
        bias = sb("mod_bias", [2, 6 * D])
        gain = sb("mod_gain", [2, 2, D])
        rows = sb("mod_rows", [2, 6 * D])
        acc = ctx.enter_context(nc.psum_tensor("mod_acc", [2, 4, BANK], F32))
        c_in, small_in, c_ready = sem("mod_c_in"), sem("mod_small_in"), sem("mod_c_ready")
        w_in = [sem(f"mod_w_in{i}") for i in range(RING)]
        chunk_done, row_done, scaled, stored = (sem(n) for n in ("mod_chunk", "mod_row", "mod_scaled", "mod_stored"))
        block = ctx.enter_context(nc.Block())

        @block.sync
        def _(sp):
            for s, c in enumerate((d["c_prompt"], d["c_sample"])):
                sp.dma_start(c_raw[:, s, :], c[0, :].rearrange("(p k) -> p k", k=KC)).then_inc(c_in, 16)
            sp.dma_start(bias[:], d["b_mod"].to_broadcast([2, 6 * D])).then_inc(small_in, 16)
            for n, g in enumerate(("norm1_gain", "norm2_gain")):
                sp.dma_start(gain[:, n, :], d[g].to_broadcast([2, D])).then_inc(small_in, 16)
            for c in range(CH):
                if c >= RING:
                    sp.wait_ge(chunk_done, c - RING + 1)
                src = d["w_mod"][0, :, c * BANK:(c + 1) * BANK].rearrange("(p k) n -> p k n", k=KC)
                sp.dma_start(w[c % RING][:], src).then_inc(w_in[c % RING], 16)
            sp.wait_ge(scaled, 2)
            sp.dma_start(d["mod"], rows[:]).then_inc(stored, 16)
            sp.wait_ge(stored, 16)

        @block.scalar
        def _(act):
            act.wait_ge(c_in, 32)
            nc.scalar.activation(c_act[:].rearrange("p k s -> p s k"), c_raw[:], ACT.Silu).then_inc(c_ready, 1)

        @block.tensor
        def _(pe):
            pe.wait_ge(c_ready, 1)
            for c in range(CH):
                pe.wait_ge(w_in[c % RING], 16 * (c // RING + 1))
                if c >= 4:
                    pe.wait_ge(row_done, c - 3)
                for k in range(KC):
                    mm = nc.tensor.matmul(acc[:, c % 4, :], c_act[:, k, :], w[c % RING][:, k, :],
                                          start=(k == 0), stop=(k == KC - 1))
                mm.then_inc(chunk_done, 1)

        @block.vector
        def _(dve):
            dve.wait_ge(small_in, 48)
            for c in range(CH):
                dve.wait_ge(chunk_done, c + 1)
                cols = slice(c * BANK, (c + 1) * BANK)
                nc.vector.tensor_tensor(rows[:, cols], acc[:, c % 4, :], bias[:, cols], ALU.add).then_inc(row_done, 1)
            dve.wait_ge(row_done, CH)
            for n, part in enumerate((SC1, SC2)):
                row = rows[:, part * D:(part + 1) * D]
                nc.vector.scalar_tensor_tensor(row, row, 1.0, gain[:, n, :], ALU.add, ALU.mult).then_inc(scaled, 1)


def norm_in(nc, sem, d, hT):
    with ExitStack() as ctx:
        def sb(name, shape, dt=F32):
            return ctx.enter_context(nc.sbuf_tensor(name, shape, dt))

        ident = sb("n1_ident", [P, P])
        x = sb("n1_x", [P, TILES, D])
        modb = sb("n1_mod", [P, 2, 2, D])
        sq = sb("n1_sq", [P, 2, D])
        ms, mse, half, rstd = (sb(n, [P, TILES]) for n in ("n1_ms", "n1_mse", "n1_half", "n1_rstd"))
        xn, h = sb("n1_xn", [P, 3, D]), [sb(f"n1_h{i}", [P, D]) for i in range(3)]
        tp = [ctx.enter_context(nc.psum_tensor(f"n1_tp{i}", [P, KC, P], F32)) for i in range(3)]
        x_in, pad_done, small_in = sem("n1_x_in"), sem("n1_pad"), sem("n1_small_in")
        squared, mean_ready, rstd_ready, scaled, h_ready, turned, placed, consts, passed = (
            sem("n1_" + n) for n in ("squared", "mean", "rstd", "scaled", "h", "turned", "placed", "consts", "passed"))
        block = ctx.enter_context(nc.Block())

        @block.sync
        def _(sp):
            sp.dma_start(x[:, 0:NT, :], d["x_prompt"][0].rearrange("(t p) n -> p t n", p=P)).then_inc(x_in, 16)
            sp.wait_ge(pad_done, 1)
            sp.dma_start(x[0:DEC, NT, :], d["x_sample"][0]).then_inc(x_in, 16)
            sp.dma_start(ident[:], d["ident"]).then_inc(small_in, 16)
            for s in range(2):
                sp.dma_start(modb[:, s, :, :], d["mod"][s:s + 1, 0:2 * D].to_broadcast([P, 2 * D])
                             .rearrange("p (a n) -> p a n", a=2)).then_inc(small_in, 16)

        @block.gpsimd
        def _(pool):
            nc.gpsimd.memset(x[:, NT, :], 0.0).then_inc(pad_done, 1)
            nc.gpsimd.memset(half[:], -0.5).then_inc(consts, 1)
            pool.wait_ge(consts, 1)
            pool.wait_ge(mean_ready, 1)
            nc.gpsimd.tensor_tensor(rstd[:], mse[:], half[:], ALU.pow).then_inc(rstd_ready, 1)

        @block.scalar
        def _(act):
            act.wait_ge(x_in, 32)
            for t in range(TILES):
                if t >= 2:
                    act.wait_ge(squared, t - 1)
                nc.scalar.activation(sq[:, t % 2, :], x[:, t, :], ACT.Square, scale=D ** -0.5,
                                     accum_out=ms[:, t:t + 1]).then_inc(squared, 1)

            with act.Fori(0, TILES // 3) as r:
                for u in range(3):
                    hold(act, passed, turned, r * 3 + (u + 1))
                    nc.scalar.activation(hT[:, :, bass.ds(r * (3 * P) + u * P, P)], tp[u][:], ACT.Copy).then_inc(placed, 1)

        @block.vector
        def _(dve):
            dve.wait_ge(squared, TILES)
            nc.vector.tensor_scalar(mse[:], ms[:], EPS, None, ALU.add).then_inc(mean_ready, 1)
            dve.wait_ge(rstd_ready, 1)
            dve.wait_ge(small_in, 48)

            def tile(t, u, s):
                nc.vector.scalar_tensor_tensor(xn[:, u, :], x[:, t, :], rstd[:, t:t + 1], modb[:, s, 1, :],
                                               ALU.mult, ALU.mult).then_inc(scaled, 1)
                dve.wait_ge(scaled, t + 1)
                if t >= 3:
                    dve.wait_ge(turned, t - 2)
                nc.vector.tensor_tensor(h[u][:], xn[:, u, :], modb[:, s, 0, :], ALU.add).then_inc(h_ready, 1)

            for t in range(TILES):
                tile(t, t % 3, t // NT)

        @block.tensor
        def _(pe):
            pe.wait_ge(small_in, 48)
            for t in range(TILES):
                pe.wait_ge(h_ready, t + 1)
                if t >= 3:
                    pe.wait_ge(placed, t - 2)
                for k in range(KC):
                    tr = nc.tensor.transpose(tp[t % 3][:, k, :], h[t % 3][:, k * P:(k + 1) * P], ident[:])
                tr.then_inc(turned, 1)


def project(nc, sem, d, hT, qkT, laT):
    RING = 6
    U_T, U_L, U_A = 2 * GH * GROUPS, GROUPS, GH * GROUPS
    with ExitStack() as ctx:
        def sb(name, shape, dt=F32):
            return ctx.enter_context(nc.sbuf_tensor(name, shape, dt))

        wt = [sb(f"pj_wt{i}", [P, KC, P]) for i in range(2)]
        wl = sb("pj_wl", [P, KC, GLR])
        wa = sb("pj_wa", [GLR, GH * GDK])
        ba = sb("pj_ba", [P, GH])
        wn = [sb(f"pj_wn{i}", [P, KC, BANK]) for i in range(2)]
        stage = [sb(f"pj_stage{i}", [P, BANK]) for i in range(RING)]
        lowT = sb("pj_lowT", [GLR, TOK])
        ax, ex, lx, mn = (sb("pj_" + n, [P, 2, GCOL]) for n in ("abs", "exp", "ln", "min"))
        acc = [ctx.enter_context(nc.psum_tensor(f"pj_acc{i}", [P, BANK], F32)) for i in range(RING)]
        wt_in = [sem(f"pj_wt_in{i}") for i in range(2)]
        wn_in = [sem(f"pj_wn_in{i}", True) for i in range(2)]
        out_done = [sem(f"pj_out{i}") for i in range(RING)]
        small_in = sem("pj_small_in", True)
        made, freed, staged, passed = (sem("pj_" + n) for n in ("made", "freed", "staged", "passed"))
        abs_done, exp_done, ln_done, min_done, sub_done, freed_la = (
            sem("pj_" + n) for n in ("abs", "exp", "ln", "min", "sub", "freed_la"))
        U0 = U_T + U_L
        UN = U0 + U_A
        PAIR = 2 * TILES
        w_in = d["w_in"][0]
        block = ctx.enter_context(nc.Block())

        def w_cols(start, n):
            return w_in[:, bass.ds(start, n)].rearrange("(k p) n -> p k n", p=P)

        @block.gpsimd
        def _(pool):
            nc.gpsimd.dma_start(wl[:], w_cols(W_GLR, GLR)).then_inc(small_in, 16)
            nc.gpsimd.dma_start(wa[:], d["w_alpha"][0]).then_inc(small_in, 16)
            nc.gpsimd.dma_start(ba[:], d["b_alpha"][0].rearrange("(h p) -> p h", p=P), allow_slow_non_contiguous=True).then_inc(small_in, 16)
            for i in range(4):
                if i >= 2:
                    pool.wait_ge(made, UN + (i - 1) * TILES)
                nc.gpsimd.dma_start(wn[i % 2][:], w_cols(W_GVR + i * BANK, BANK)).then_inc(wn_in[i % 2], 16)

        @block.sync
        def _(sp):
            for i in range(2):
                sp.dma_start(wt[i][:], w_cols(i * P, P)).then_inc(wt_in[i], 16)
            with sp.Fori(0, GH - 1) as r:
                for i in range(2):
                    hold(sp, passed, made, r * RING + (i + 1) * GROUPS)
                    sp.dma_start(wt[i][:], w_cols(r * (2 * P) + (2 + i) * P, P)).then_inc(wt_in[i], 16)
            with sp.Fori(0, 2) as r:
                for u in range(PAIR):
                    c, t = u // TILES, u % TILES
                    hold(sp, passed, staged, r * PAIR + (RING + u + 1))
                    dst = d["z"][t * P:(t + 1) * P, bass.ds(r * (2 * BANK) + c * BANK, BANK)]
                    sp.dma_start(dst, stage[u % RING][:]).then_inc(out_done[u % RING], 16)
            for i in range(RING):
                sp.wait_ge(out_done[i], 16 * 2 * PAIR // RING)

        @block.tensor
        def _(pe):
            with pe.Fori(0, GH) as r:
                for i in range(2):
                    hold(pe, passed, wt_in[i], r * 16 + 16)
                    for g in range(GROUPS):
                        u = i * GROUPS + g
                        hold(pe, passed, freed, r * RING + (u + 1))
                        for k in range(KC):
                            mm = nc.tensor.matmul(acc[u][:, 0:GCOL], wt[i][:, k, :], hT[:, k, g * GCOL:(g + 1) * GCOL],
                                                  start=(k == 0), stop=(k == KC - 1))
                        mm.then_inc(made, 1)
            pe.wait_ge(small_in, 48)
            for g in range(GROUPS):
                u = U_T + g
                pe.wait_ge(freed, u + 1)
                for k in range(KC):
                    mm = nc.tensor.matmul(acc[u % RING][0:GLR, 0:GCOL], wl[:, k, :], hT[:, k, g * GCOL:(g + 1) * GCOL],
                                          start=(k == 0), stop=(k == KC - 1))
                mm.then_inc(made, 1)
            pe.wait_ge(freed, RING + U0)
            for u in range(U_A):
                h, g = u // GROUPS, u % GROUPS
                if u >= RING:
                    pe.wait_ge(freed_la, u - RING + 1)
                nc.tensor.matmul(acc[(U0 + u) % RING][:, 0:GCOL], wa[:, h * GDK:(h + 1) * GDK],
                                 lowT[:, g * GCOL:(g + 1) * GCOL], start=True, stop=True).then_inc(made, 1)
            pe.wait_ge(freed_la, U_A)
            with pe.Fori(0, 2) as r:
                for u in range(PAIR):
                    c, t = u // TILES, u % TILES
                    if t == 0:
                        hold(pe, passed, wn_in[c], r * 16 + 16)
                    hold(pe, passed, staged, r * PAIR + (u + 1))
                    for k in range(KC):
                        mm = nc.tensor.matmul(acc[(UN + u) % RING][:], hT[:, k, t * P:(t + 1) * P], wn[c][:, k, :],
                                              start=(k == 0), stop=(k == KC - 1))
                    mm.then_inc(made, 1)

        @block.scalar
        def _(act):
            act.sem_inc(freed, RING)
            act.sem_inc(staged, RING)

            def place(r, first, scale):
                for u in range(RING):
                    i, g = u // GROUPS, u % GROUPS
                    hold(act, passed, made, r * RING + (first * RING + u + 1))
                    dst = qkT[:, bass.ds(r * (2 * TOK) + (first * 2 + i) * TOK + g * GCOL, GCOL)]
                    nc.scalar.activation(dst, acc[u][:, 0:GCOL], ACT.Copy, scale=scale).then_inc(freed, 1)

            with act.Fori(0, GH // 2) as r:
                place(r, 0, GDK ** -0.5)
            with act.Fori(0, GH // 2) as r:
                place(r, GH // 2, 1.0)
            for g in range(GROUPS):
                act.wait_ge(made, U_T + g + 1)
                nc.scalar.activation(lowT[:, g * GCOL:(g + 1) * GCOL], acc[(U_T + g) % RING][0:GLR, 0:GCOL],
                                     ACT.Copy).then_inc(freed, 1)
            act.wait_ge(small_in, 48)
            for u in range(U_A):
                h, b = u // GROUPS, u % 2
                act.wait_ge(made, U0 + u + 1)
                if u >= 2:
                    act.wait_ge(sub_done, u - 1)
                nc.scalar.activation(ax[:, b, :], acc[(U0 + u) % RING][:, 0:GCOL], ACT.Abs,
                                     bias=ba[:, h:h + 1]).then_inc(abs_done, 1)
                act.wait_ge(abs_done, u + 1)
                nc.scalar.activation(ex[:, b, :], ax[:, b, :], ACT.Exp, scale=-1.0).then_inc(exp_done, 1)
                act.wait_ge(exp_done, u + 1)
                nc.scalar.activation(lx[:, b, :], ex[:, b, :], ACT.Ln, bias=1.0).then_inc(ln_done, 1)

            def store(r, first, func):
                for u in range(PAIR):
                    hold(act, passed, made, r * PAIR + (UN + first * PAIR + u + 1))
                    if first or u >= RING:
                        n = first * (PAIR // RING) + u // RING
                        hold(act, passed, out_done[u % RING], r * (16 * (PAIR // RING)) + 16 * n)
                    nc.scalar.activation(stage[u % RING][:], acc[(UN + u) % RING][:], func).then_inc(staged, 1)

            store(0, 0, ACT.Copy)
            store(0, 1, ACT.Silu)

        @block.vector
        def _(dve):
            dve.wait_ge(small_in, 48)
            for u in range(U_A):
                h, g, b = u // GROUPS, u % GROUPS, u % 2
                dve.wait_ge(ln_done, u + 1)
                nc.vector.tensor_scalar(mn[:, b, :], acc[(U0 + u) % RING][:, 0:GCOL], ba[:, h:h + 1], 0.0,
                                        ALU.add, ALU.min).then_inc(min_done, 1)
                dve.wait_ge(min_done, u + 1)
                nc.vector.tensor_tensor(mn[:, b, :], mn[:, b, :], lx[:, b, :], ALU.subtract).then_inc(sub_done, 1)
                dve.wait_ge(sub_done, u + 1)
                nc.vector.tensor_scalar(laT[:, h, g * GCOL:(g + 1) * GCOL], mn[:, b, :], 1.0 / GTAU, None,
                                        ALU.mult).then_inc(freed_la, 1)


def gla(nc, sem, d, hT, qkT, laT):
    UNITS, ROUND, STAGES = 6, 2 * TILES, 3
    NB = P // GBLK
    OFF = [GBLK * i * (i + 1) // 2 for i in range(NB + 1)]
    with ExitStack() as ctx:
        def sb(name, shape, dt=F32):
            return ctx.enter_context(nc.sbuf_tensor(name, shape, dt))

        def ps(name, shape):
            return ctx.enter_context(nc.psum_tensor(name, shape, F32))

        ident, causal, ones = sb("gl_ident", [P, P]), sb("gl_causal", [P, P]), sb("gl_ones", [P, P])
        gain = sb("gl_gain", [P, GDV])
        v = [sb(f"gl_v{i}", [P, GH * GDV]) for i in range(3)]
        gate = [sb(f"gl_gate{i}", [P, GH * GDV]) for i in range(3)]
        wn = [sb(f"gl_wn{i}", [P, KC, BANK]) for i in range(2)]
        staging = [sb(f"gl_stage{i}", [P, BANK]) for i in range(STAGES)]
        state = [sb("gl_state_p", [P, GH, GDV]), sb("gl_state_s", [P, GH, GDV])]
        cum = sb("gl_cum", [P, GH, P + 1])
        blk = sb("gl_blk", [P, GH, P])
        e_blk, e_cum, e_end = (sb("gl_e_" + n, [P, GH, P]) for n in ("blk", "cum", "end"))
        e_key = sb("gl_e_key", [P, GH, OFF[NB]])
        q_cum = sb("gl_q_cum", [P, GH, P])
        q_blk, k_end = e_blk, e_end
        k_blk = sb("gl_k_blk", [P, GH, NB, P])
        attn = sb("gl_attn", [P, GH, P])
        k_tok = sb("gl_k_tok", [P, GH, GDK])
        ms, mse, rstd, half = (sb("gl_" + n, [P, GH]) for n in ("ms", "mse", "rstd", "half"))
        on = sb("gl_on", [P, GH * GDV])
        sq = on[:].rearrange("p (h c) -> p h c", h=GH)
        p_attn, p_k = ps("gl_p_attn", [P, GH, P]), ps("gl_p_k", [P, GH, P])
        p_o, p_kv = ps("gl_p_o", [P, GH, GDV]), ps("gl_p_kv", [P, GH, GDV])
        p_t = p_kv[:].rearrange("p h c -> p (h c)").rearrange("p (k t) -> p k t", k=KC)
        p_u = [ps(f"gl_p_u{b}", [P, BANK]) for b in range(2)]
        names = ("small_in consts scanned blocked decays keyed scored masked turned_k placed_k out_made kv_made "
                 "state_ready squared mean rstd normed gated turned placed stored passed")
        (small_in, consts, scanned, blocked, decays, keyed, scored, masked, turned_k, placed_k, out_made, kv_made,
         state_ready, squared, mean_ready, rstd_ready, normed, gated, turned, placed, stored, passed) = (
            sem("gl_" + n) for n in names.split())
        unit_made, unit_staged = sem("gl_unit_made"), sem("gl_unit_staged")
        v_in = [sem(f"gl_v_in{i}") for i in range(3)]
        oa_out = [sem(f"gl_oa_out{i}") for i in range(3)]
        unit_out = [sem(f"gl_unit_out{i}") for i in range(STAGES)]
        wn_in = [sem(f"gl_wn_in{i}", True) for i in range(2)]
        block = ctx.enter_context(nc.Block())

        def at(r, u, each, c):
            return r * (3 * each) + (u * each + c)

        def over_tiles(eng, tile):
            for u in range(3):
                tile(0, u, P)
            with eng.Fori(1, 2) as r:
                for u in range(3):
                    tile(r, u, P)
            for u in range(3):
                tile(2, u, P if u < 2 else DEC)

        def unit(r, u, j):
            x = u * UNITS + j
            return x, x // TILES, x % TILES

        @block.sync
        def _(sp):
            sp.dma_start(ident[:], d["ident"]).then_inc(small_in, 16)
            sp.dma_start(causal[:], d["causal"]).then_inc(small_in, 16)
            sp.dma_start(gain[:], d["gla_gain"].to_broadcast([P, GDV])).then_inc(small_in, 16)
            sp.dma_start(state[1][:], d["state_gla"][0, 0].rearrange("h k v -> k h v")).then_inc(small_in, 16)

            def load(r, u):
                b = u % 3
                hold(sp, passed, oa_out[b], (r + u // 3) * 16)
                for dst, part in ((v[b], ZV), (gate[b], ZR)):
                    sp.dma_start(dst[:], d["z"][bass.ds(r * (3 * P) + u * P, P), part * D:(part + 1) * D]).then_inc(v_in[b], 16)

            def tile(r, u, n):
                for j in range(UNITS):
                    x, c, t = unit(r, u, j)
                    hold(sp, passed, unit_staged, at(r, u, UNITS, 2 + j + 1))
                    dst = d["z"][t * P:(t + 1) * P, bass.ds(r * (2 * BANK) + (ZQ * D + c * BANK), BANK)]
                    sp.dma_start(dst, staging[x % STAGES][:]).then_inc(unit_out[x % STAGES], 16)
                hold(sp, passed, placed, at(r, u, 1, 1))
                sp.dma_start(d["oaT"][:, :, bass.ds(r * (3 * P) + u * P, P)].rearrange("k p t -> p k t"),
                             v[u][:].rearrange("p (k t) -> p k t", k=KC)).then_inc(oa_out[u], 16)
                if isinstance(r, int) and r == 2 and u > 0:
                    return
                load(r, u + 2)

            load(0, 0)
            load(0, 1)
            over_tiles(sp, tile)
            for i in range(3):
                sp.wait_ge(oa_out[i], 48)
                sp.wait_ge(unit_out[i], 16 * 3 * ROUND // STAGES)
            sp.wait_ge(state_ready, GH * NT)
            sp.dma_start(d["gla_prompt"][0, 0].rearrange("h k v -> k h v"), state[0][:]).then_inc(stored, 16)
            sp.wait_ge(state_ready, GH * TILES)
            sp.dma_start(d["gla_sample"][0, 0].rearrange("h k v -> k h v"), state[1][:]).then_inc(stored, 16)
            sp.wait_ge(stored, 32)

        @block.gpsimd
        def _(pool):
            for t in (cum, k_blk, state[0]):
                nc.gpsimd.memset(t[:], 0.0).then_inc(consts, 1)
            nc.gpsimd.memset(ones[:], 1.0).then_inc(consts, 1)
            nc.gpsimd.memset(half[:], -0.5).then_inc(consts, 1)

            def weights(r, c):
                cols = d["w_in"][0, :, bass.ds(r * (2 * BANK) + (W_D + c * BANK), BANK)]
                nc.gpsimd.dma_start(wn[c][:], cols.rearrange("(k p) n -> p k n", p=P)).then_inc(wn_in[c], 16)

            weights(0, 0)
            weights(0, 1)
            pool.wait_ge(consts, 5)

            def tile(r, u, n):
                hold(pool, passed, mean_ready, at(r, u, 1, 1))
                nc.gpsimd.tensor_tensor(rstd[0:n, :], mse[0:n, :], half[0:n, :], ALU.pow).then_inc(rstd_ready, 1)
                if u > 0 and not (isinstance(r, int) and r == 2):
                    hold(pool, passed, unit_made, r * ROUND + u * TILES)
                    weights(r + 1, u - 1)

            over_tiles(pool, tile)

        @block.scalar
        def _(act):
            act.wait_ge(consts, 5)

            def evacuate(r, u, first, last):
                for j in range(first, last):
                    x, _, _ = unit(r, u, j)
                    hold(act, passed, unit_made, at(r, u, UNITS, j + 1))
                    hold(act, passed, unit_out[x % STAGES], r * (16 * ROUND // STAGES) + 16 * (x // STAGES))
                    nc.scalar.activation(staging[x % STAGES][:], p_u[x % 2][:], ACT.Copy).then_inc(unit_staged, 1)

            def tile(r, u, n):
                nb = n // GBLK
                for h in range(GH):
                    hold(act, passed, blocked, at(r, u, GH, h + 1))
                    nc.scalar.activation(e_blk[:, h, 0:n], blk[:, h, 0:n], ACT.Exp)
                    nc.scalar.activation(e_cum[:, h, 0:n], cum[:, h, 1:n + 1], ACT.Exp)
                    nc.scalar.activation(e_end[:, h, 0:n], cum[:, h, 1:n + 1], ACT.Exp, scale=-1.0, bias=cum[:, h, n:n + 1])
                    for i in range(nb):
                        e = nc.scalar.activation(e_key[:, h, OFF[i]:OFF[i + 1]], cum[:, h, 1:GBLK * (i + 1) + 1], ACT.Exp,
                                                 scale=-1.0, bias=cum[:, h, GBLK * i:GBLK * i + 1])
                    e.then_inc(decays, 1)
                evacuate(r, u, 0, 3)
                hold(act, passed, turned_k, at(r, u, GH, GH))
                for h in range(GH):
                    nc.scalar.activation(k_tok[0:n, h, :], p_k[0:n, h, :], ACT.Copy).then_inc(placed_k, 1)
                evacuate(r, u, 3, 4)
                hold(act, passed, out_made, at(r, u, GH, GH))
                for h in range(GH):
                    nc.scalar.activation(sq[0:n, h, :], p_o[0:n, h, :], ACT.Square, scale=GDV ** -0.5,
                                         accum_out=ms[0:n, h:h + 1]).then_inc(squared, 1)
                evacuate(r, u, 4, UNITS)
                hold(act, passed, turned, at(r, u, 1, 1))
                nc.scalar.activation(v[u][:].rearrange("p (k t) -> p k t", k=KC)[:, :, 0:n], p_t[:, :, 0:n], ACT.Copy).then_inc(placed, 1)

            over_tiles(act, tile)

        @block.vector
        def _(dve):
            dve.wait_ge(consts, 5)
            dve.wait_ge(small_in, 64)
            dve.sem_inc(unit_staged, 2)

            def tile(r, u, n):
                nb = n // GBLK
                s = state[0 if n == P else 1]
                for h in range(GH):
                    nc.vector.tensor_tensor_scan(cum[:, h, 1:n + 1], ones[:, 0:n], laT[:, h, bass.ds(r * (3 * P) + u * P, n)],
                                                 0.0, ALU.mult, ALU.add).then_inc(scanned, 1)
                hold(dve, passed, scanned, at(r, u, GH, GH))
                for h in range(GH):
                    start = cum[:, h, 0:n].rearrange("p (b c) -> p b c", c=GBLK)[:, :, 0:1].to_broadcast([P, nb, GBLK])
                    nc.vector.tensor_tensor(blk[:, h, 0:n].rearrange("p (b c) -> p b c", c=GBLK),
                                            cum[:, h, 1:n + 1].rearrange("p (b c) -> p b c", c=GBLK), start,
                                            ALU.subtract).then_inc(blocked, 1)
                for h in range(GH):
                    hold(dve, passed, decays, at(r, u, GH, h + 1))
                    q = qkT[:, bass.ds(r * (3 * P) + (u * P + h * TOK), n)]
                    nc.vector.tensor_tensor(q_blk[:, h, 0:n], q, e_blk[:, h, 0:n], ALU.mult)
                    nc.vector.tensor_tensor(q_cum[:, h, 0:n], q, e_cum[:, h, 0:n], ALU.mult)
                    for i in range(nb):
                        w = GBLK * (i + 1)
                        k = qkT[:, bass.ds(r * (3 * P) + (u * P + (GH + h) * TOK), w)]
                        nc.vector.tensor_tensor(k_blk[:, h, i, 0:w], k, e_key[:, h, OFF[i]:OFF[i + 1]], ALU.mult)
                    k = qkT[:, bass.ds(r * (3 * P) + (u * P + (GH + h) * TOK), n)]
                    nc.vector.tensor_tensor(k_end[:, h, 0:n], k, e_end[:, h, 0:n], ALU.mult).then_inc(keyed, 1)
                hold(dve, passed, scored, at(r, u, GH, GH))
                for h in range(GH):
                    nc.vector.tensor_tensor(attn[0:n, h, 0:n], p_attn[0:n, h, 0:n], causal[0:n, 0:n], ALU.mult).then_inc(masked, 1)
                hold(dve, passed, kv_made, at(r, u, GH, GH))
                for h in range(GH):
                    nc.vector.scalar_tensor_tensor(s[:, h, :], s[:, h, :], e_cum[:, h, n - 1:n], p_kv[:, h, :],
                                                   ALU.mult, ALU.add).then_inc(state_ready, 1)
                hold(dve, passed, squared, at(r, u, GH, GH))
                nc.vector.tensor_scalar(mse[0:n, :], ms[0:n, :], EPS, None, ALU.add).then_inc(mean_ready, 1)
                hold(dve, passed, rstd_ready, at(r, u, 1, 1))
                for h in range(GH):
                    o = nc.vector.scalar_tensor_tensor(on[0:n, h * GDV:(h + 1) * GDV], p_o[0:n, h, :], rstd[0:n, h:h + 1],
                                                       gain[0:n, :], ALU.mult, ALU.mult)
                o.then_inc(normed, 1)
                hold(dve, passed, normed, at(r, u, 1, 1))
                nc.vector.tensor_tensor(on[0:n, :], on[0:n, :], gate[u][0:n, :], ALU.mult).then_inc(gated, 1)

            over_tiles(dve, tile)

        @block.tensor
        def _(pe):
            pe.wait_ge(small_in, 64)
            pe.wait_ge(consts, 5)

            def project(r, u, first, last):
                for j in range(first, last):
                    x, c, t = unit(r, u, j)
                    if t == 0:
                        hold(pe, passed, wn_in[c], r * 16 + 16)
                    hold(pe, passed, unit_staged, at(r, u, UNITS, j + 1))
                    for k in range(KC):
                        mm = nc.tensor.matmul(p_u[x % 2][:], hT[:, k, t * P:(t + 1) * P], wn[c][:, k, :],
                                              start=(k == 0), stop=(k == KC - 1))
                    mm.then_inc(unit_made, 1)

            def tile(r, u, n):
                s = state[0 if n == P else 1]
                project(r, u, 0, 3)
                for h in range(GH):
                    hold(pe, passed, keyed, at(r, u, GH, h + 1))
                    for i in range(n // GBLK):
                        mm = nc.tensor.matmul(p_attn[0:n, h, i * GBLK:(i + 1) * GBLK], k_blk[:, h, i, 0:n],
                                              q_blk[:, h, i * GBLK:(i + 1) * GBLK], start=True, stop=True)
                    mm.then_inc(scored, 1)
                    nc.tensor.transpose(p_k[0:n, h, :], k_end[:, h, 0:n], ident[:]).then_inc(turned_k, 1)
                hold(pe, passed, v_in[u], r * 32 + 32)
                project(r, u, 3, 4)
                for h in range(GH):
                    hold(pe, passed, masked, at(r, u, GH, h + 1))
                    nc.tensor.matmul(p_o[0:n, h, :], attn[0:n, h, 0:n], v[u][0:n, h * GDV:(h + 1) * GDV], start=True, stop=False)
                    nc.tensor.matmul(p_o[0:n, h, :], q_cum[:, h, 0:n], s[:, h, :], start=False, stop=True).then_inc(out_made, 1)
                for h in range(GH):
                    hold(pe, passed, placed_k, at(r, u, GH, h + 1))
                    nc.tensor.matmul(p_kv[:, h, :], k_tok[0:n, h, :], v[u][0:n, h * GDV:(h + 1) * GDV],
                                     start=True, stop=True).then_inc(kv_made, 1)
                project(r, u, 4, UNITS)
                hold(pe, passed, gated, at(r, u, 1, 1))
                for k in range(KC):
                    tr = nc.tensor.transpose(p_t[:, k, 0:n], on[0:n, k * P:(k + 1) * P], ident[0:n, 0:n])
                tr.then_inc(turned, 1)

            over_tiles(pe, tile)


def rope(nc, sem, d):
    N = 2 * DH
    H = HD // 2
    with ExitStack() as ctx:
        def sb(name, shape, dt=F32):
            return ctx.enter_context(nc.sbuf_tensor(name, shape, dt))

        ident = sb("rp_ident", [P, P])
        gains = sb("rp_gains", [P, 2, 2 * HD])
        cs, sn = sb("rp_cos", [P, TILES, H]), sb("rp_sin", [P, TILES, H])
        x = [sb(f"rp_x{i}", [P, 2, D]) for i in range(2)]
        cache = [sb(f"rp_cache{i}", [P, D]) for i in range(2)]
        sq = sb("rp_sq", [P, 2, D])
        ms, mse, half = (sb("rp_" + n, [P, 2 * N]) for n in ("ms", "mse", "half"))
        rstd = [sb(f"rp_rstd{u}", [P, 2 * N]) for u in range(2)]
        own, other = sb("rp_own", [P, 2, 2 * HD]), sb("rp_other", [P, 2, 2 * HD])
        xn, xa, xb = (sb("rp_" + n, [P, 2, D]) for n in ("xn", "xa", "xb"))
        y = sb("rp_y", [P, 2, D])
        tT = [sb(f"rp_tT{i}", [P, DH, P]) for i in range(2)]
        p_t = [ctx.enter_context(nc.psum_tensor(f"rp_p_t{i}", [P, DH, P], F32)) for i in range(2)]
        names = "small_in consts squared summed mean rstd normed tabled own other rotated turned placed passed"
        (small_in, consts, squared, summed, mean_ready, rstd_ready, normed, tabled, own_done, other_done, rotated,
         turned, placed, passed) = (sem("rp_" + n) for n in names.split())
        krow_out = sem("rp_krow_out", True)
        x_in = [sem(f"rp_x_in{i}") for i in range(2)]
        c_in = [sem(f"rp_c_in{i}") for i in range(2)]
        t_out = [sem(f"rp_t_out{i}") for i in range(2)]
        v_out = sem("rp_v_out")
        block = ctx.enter_context(nc.Block())

        def at(r, u, each, c):
            return r * (2 * each) + (u * each + c)

        def over_tiles(eng, tile):
            for u in range(2):
                tile(0, u, P)
            with eng.Fori(1, NT // 2) as r:
                for u in range(2):
                    tile(r, u, P)
            tile(NT // 2, 0, DEC)

        def ahead(eng, front, back):
            def turn(r, u):
                front(r, u + 1)
                back(r, u, P)

            front(0, 0)
            turn(0, 0)
            turn(0, 1)
            with eng.Fori(1, NT // 2) as r:
                turn(r, 0)
                turn(r, 1)
            back(NT // 2, 0, DEC)

        @block.sync
        def _(sp):
            sp.dma_start(ident[:], d["ident"]).then_inc(small_in, 16)
            for a, g in enumerate(("q_gain", "k_gain")):
                sp.dma_start(gains[:, a, :], d[g].rearrange("o a c -> o (a c)").to_broadcast([P, 2 * HD])).then_inc(small_in, 16)
            sp.dma_start(cs[:], d["rope_cos"].rearrange("(t p) c -> p t c", p=P)).then_inc(small_in, 16)
            sp.dma_start(sn[:], d["rope_sin"].rearrange("(t p) c -> p t c", p=P)).then_inc(small_in, 16)

            def load(r, u, n):
                hold(sp, passed, normed, at(r, u, 1, 1))
                rows = d["z"][bass.ds(r * (2 * P) + u * P, P), ZQ * D:(ZK + 1) * D]
                sp.dma_start(x[u][:], rows.rearrange("p (a n) -> p a n", a=2)).then_inc(x_in[u], 16)

            over_tiles(sp, load)
            z_v = d["z"][:, ZDV * D:(ZDV + 1) * D]
            sp.dma_start(d["v_prompt"][0, 0].rearrange("t h v -> t (h v)"), z_v[0:SEQ, :]).then_inc(v_out, 16)
            sp.dma_start(d["v_sample"][0, 0].rearrange("t h v -> t (h v)"), z_v[SEQ:SEQ + DEC, :]).then_inc(v_out, 16)
            for c in range(PAST // P):
                if c >= 2:
                    sp.wait_ge(turned, 2 + 2 * TILES + c - 1)
                sp.dma_start(cache[c % 2][:], d["cache_k"][0, 0, c * P:(c + 1) * P].rearrange("t h v -> t (h v)")).then_inc(c_in[c % 2], 16)
            sp.wait_ge(v_out, 32)

        @block.gpsimd
        def _(pool):
            nc.gpsimd.memset(half[:], -0.5).then_inc(consts, 1)
            pool.wait_ge(consts, 1)

            def power(r, u):
                hold(pool, passed, mean_ready, at(r, u, 1, 1))
                nc.gpsimd.tensor_tensor(rstd[u % 2][:], mse[:], half[:], ALU.pow).then_inc(rstd_ready, 1)

            def store(r, u, n):
                hold(pool, passed, rotated, at(r, u, 1, 1))
                dst = (d["k_prompt"][0, 0, bass.ds(r * (2 * P) + u * P, P)] if n == P else d["k_sample"][0, 0])
                nc.gpsimd.dma_start(dst.rearrange("t h c -> t (h c)"), y[0:n, 1, :]).then_inc(krow_out, 16)

            ahead(pool, power, store)
            pool.wait_ge(krow_out, 16 * TILES)

        @block.scalar
        def _(act):
            def place(r, u, j, cols, name):
                hold(act, passed, turned, at(r, u, 2, j + 3))
                hold(act, passed, t_out[j], at(r, u, 16, 0))
                nc.scalar.activation(tT[j][:], p_t[j][:], ACT.Copy).then_inc(placed, 1)
                hold(act, passed, placed, at(r, u, 2, j + 3))
                act.dma_start(d[name][:, :, cols].rearrange("h p t -> p h t"), tT[j][:]).then_inc(t_out[j], 16)

            def square(r, u):
                hold(act, passed, x_in[u % 2], r * 16 + 16 * (1 + u // 2))
                hold(act, passed, summed, at(r, u, 1, 1))
                nc.scalar.activation(sq[:], x[u % 2][:], ACT.Square, scale=HD ** -0.5).then_inc(squared, 1)

            def tile(r, u, n):
                cols = bass.ds(r * (2 * P) + u * P, P)
                for j, name in enumerate(("qT", "kT")):
                    place(r, u, j, cols, name)

            ahead(act, square, tile)
            for c in range(PAST // P):
                j = c % 2
                n = 2 + 2 * TILES + c
                act.wait_ge(turned, n + 1)
                act.wait_ge(t_out[j], 16 * (TILES + c // 2))
                nc.scalar.activation(tT[j][:], p_t[j][:], ACT.Copy).then_inc(placed, 1)
                act.wait_ge(placed, n + 1)
                act.dma_start(d["kT"][:, :, TOK + c * P:TOK + (c + 1) * P].rearrange("h p t -> p h t"), tT[j][:]).then_inc(t_out[j], 16)
            for j in range(2):
                act.wait_ge(t_out[j], 16 * (TILES + PAST // P // 2))

        @block.vector
        def _(dve):
            dve.wait_ge(small_in, 80)
            dve.sem_inc(normed, 2)
            dve.sem_inc(summed, 1)

            def halves(ap):
                return ap.rearrange("p (m e c) -> p m e c", m=2, e=2)

            def mean(r, u):
                hold(dve, passed, rstd_ready, at(r, u, 1, 0))
                hold(dve, passed, squared, at(r, u, 1, 1))
                nc.vector.tensor_reduce(ms[:], sq[:].rearrange("p a (g c) -> p (a g) c", c=HD), AX.X, ALU.add).then_inc(summed, 1)
                hold(dve, passed, summed, at(r, u, 1, 2))
                nc.vector.tensor_scalar(mse[:], ms[:], EPS, None, ALU.add).then_inc(mean_ready, 1)

            def tile(r, u, n):
                c = cs[:].rearrange("p t c -> p (t c)")[:, bass.ds(r * (2 * H) + u * H, H)]
                s = sn[:].rearrange("p t c -> p (t c)")[:, bass.ds(r * (2 * H) + u * H, H)]
                c4 = c.unsqueeze(1).to_broadcast([P, 4, H])
                s2 = s.unsqueeze(1).to_broadcast([P, 2, H])
                hold(dve, passed, other_done, at(r, u, 1, 1))
                for a in range(2):
                    scale = (HD ** -0.5, 1.0)[a]
                    g = gains[:, a, :]
                    nc.vector.scalar_tensor_tensor(own[:, a, :].rearrange("p (m c) -> p m c", m=4),
                                                   g.rearrange("p (m c) -> p m c", m=4), scale, c4, ALU.mult, ALU.mult)
                    gh, oh = halves(g), halves(other[:, a, :])
                    nc.vector.scalar_tensor_tensor(oh[:, :, 0, :], gh[:, :, 1, :], -scale, s2, ALU.mult, ALU.mult)
                    w = nc.vector.scalar_tensor_tensor(oh[:, :, 1, :], gh[:, :, 0, :], scale, s2, ALU.mult, ALU.mult)
                w.then_inc(tabled, 1)
                hold(dve, passed, rstd_ready, at(r, u, 1, 1))
                nc.vector.tensor_tensor(xn[:].rearrange("p a (g c) -> p (a g) c", c=HD), x[u][:].rearrange("p a (g c) -> p (a g) c", c=HD),
                                        rstd[u][:].unsqueeze(2).to_broadcast([P, 2 * N, HD]), ALU.mult).then_inc(normed, 1)
                hold(dve, passed, normed, at(r, u, 1, 3))
                for a in range(2):
                    o = own[:, a, :].unsqueeze(1).to_broadcast([P, DH, 2 * HD])
                    nc.vector.tensor_tensor(xa[:, a, :].rearrange("p (h c) -> p h c", h=DH), xn[:, a, :].rearrange("p (h c) -> p h c", h=DH), o, ALU.mult)
                    for e in range(2):
                        for m in range(2):
                            def part(ap, e):
                                return ap.rearrange("p (h m e c) -> p h m e c", h=DH, m=2, e=2)[:, :, m, e, :]
                            f = other[:, a, :].rearrange("p (m e c) -> p m e c", m=2, e=2)[:, m, e, :].unsqueeze(1).to_broadcast([P, DH, H])
                            b = nc.vector.tensor_tensor(part(xb[:, a, :], e), part(xn[:, a, :], 1 - e), f, ALU.mult)
                b.then_inc(other_done, 1)
                hold(dve, passed, other_done, at(r, u, 1, 2))
                hold(dve, passed, turned, at(r, u, 2, 2))
                hold(dve, passed, krow_out, at(r, u, 16, 0))
                nc.vector.tensor_tensor(y[:], xa[:], xb[:], ALU.add).then_inc(rotated, 1)

            dve.sem_inc(other_done, 1)
            dve.sem_inc(turned, 2)
            dve.sem_inc(placed, 2)
            ahead(dve, mean, tile)

        @block.tensor
        def _(pe):
            pe.wait_ge(small_in, 80)

            def tile(r, u, n):
                hold(pe, passed, rotated, at(r, u, 1, 1))
                for j in range(2):
                    hold(pe, passed, placed, at(r, u, 2, j + 1))
                    for h in range(DH):
                        tr = nc.tensor.transpose(p_t[j][:, h, :], y[:, j, h * P:(h + 1) * P], ident[:])
                    tr.then_inc(turned, 1)

            over_tiles(pe, tile)
            for c in range(PAST // P):
                j = c % 2
                pe.wait_ge(c_in[j], 16 * (c // 2 + 1))
                pe.wait_ge(placed, 2 * TILES + c + 1)
                for h in range(DH):
                    tr = nc.tensor.transpose(p_t[j][:, h, :], cache[j][:, h * P:(h + 1) * P], ident[:])
                tr.then_inc(turned, 1)


def attend(nc, sem, d, obT, oaT):
    KEYS = TOK + PAST
    HALF = P // 2
    UNITS = []
    for i in range(NT):
        tiles = [(j * P, j, P) for j in range(i + 1)]
        n = (i + 1) * P
        UNITS.append((i * P, P, tiles, [(c, c, min(BANK, n - c)) for c in range(0, n, BANK)]))
    UNITS.append((SEQ, DEC, [(TOK + j * P, TILES + j, P) for j in range(PAST // P)] + [(SEQ, NT, DEC)],
                  [(TOK, 0, PAST), (SEQ, PAST, DEC)]))
    NU = len(UNITS)
    GRP = [(i, g) for i, (_, _, tiles, _) in enumerate(UNITS) for g in range(0, len(tiles), 4)]
    NG = len(GRP)
    assert NG % 2 == 0
    with ExitStack() as ctx:
        def sb(name, shape, dt=F32):
            return ctx.enter_context(nc.sbuf_tensor(name, shape, dt))

        def ps(name, shape):
            return ctx.enter_context(nc.psum_tensor(name, shape, F32))

        ident = sb("at_ident", [P, P])
        lamv, lamp = sb("at_lamv", [P, 4, HD]), sb("at_lamp", [P, 2, HD])
        lams, lame, nlam = sb("at_lams", [P, 2]), sb("at_lame", [P, 2]), sb("at_nlam", [P, 1])
        gain = sb("at_gain", [P, VD])
        q = [sb(f"at_q{u}", [P, TOK]) for u in range(2)]
        k = [sb(f"at_k{u}", [P, KEYS]) for u in range(2)]
        v = [sb(f"at_v{u}", [P, TILES + PAST // P, VD]) for u in range(2)]
        prob = [sb(f"at_prob{m}", [P, SEQ]) for m in range(2)]
        mix = sb("at_mix", [P, SEQ])
        mixT = [sb(f"at_mixT{b}", [P, 4, P]) for b in range(2)]
        negmax, total, recip = (sb("at_" + n, [P, 2, 2]) for n in ("negmax", "total", "recip"))
        ratio = sb("at_ratio", [P, 2])
        out = [sb(f"at_out{u}", [P, TILES, VD]) for u in range(2)]
        sq = sb("at_sq", [P, TILES, VD])
        ms, mse, rstd, half = (sb("at_" + n, [P, TILES]) for n in ("ms", "mse", "rstd", "half"))
        p_s = [ps(f"at_p_s{m}", [P, SEQ]) for m in range(2)]
        p_t = [ps(f"at_p_t{b}", [P, 4, P]) for b in range(2)]
        p_o = [ps(f"at_p_o{b}", [P, BANK]) for b in range(2)]
        names = ("small_in consts lam_a lam_b lam_c masked recips ratios mixed turned copied applied "
                 "out_made out_read squared summed mean rstd normed gained head_turned head_placed passed")
        (small_in, consts, lam_a, lam_b, lam_c, masked, recips, ratios, mixed, turned, copied, applied, out_made, out_read,
         squared, summed, mean_ready, rstd_ready, normed, gained, head_turned, head_placed, passed) = (
            sem("at_" + n) for n in names.split())
        scored, maxed, exped = ([sem(f"at_{n}{m}") for m in range(2)] for n in ("scored", "maxed", "exped"))
        oa_in = sem("at_oa_in")
        h_in = [sem(f"at_h_in{u}") for u in range(2)]
        block = ctx.enter_context(nc.Block())

        def at(r, u, each, c):
            return r * (2 * each) + (u * each + c)

        @block.sync
        def _(sp):
            sp.dma_start(ident[:], d["ident"]).then_inc(small_in, 16)
            for n, name in enumerate(("lam_q1", "lam_k1", "lam_q2", "lam_k2")):
                sp.dma_start(lamv[:, n, :], d[name].to_broadcast([P, HD])).then_inc(small_in, 16)
            sp.dma_start(gain[:], d["diff_gain"].to_broadcast([P, VD])).then_inc(small_in, 16)
            sp.dma_start(oaT[:], d["oaT"].rearrange("k p t -> p k t")).then_inc(oa_in, 16)
            with sp.Fori(0, DH // 2) as r:
                for u in range(2):
                    hold(sp, passed, head_placed, at(r, u, 1, 1))
                    sp.dma_start(q[u][:], d["qT"][bass.ds(r * 2 + u, 1)].rearrange("o p t -> (o p) t")).then_inc(h_in[u], 16)
                    sp.dma_start(k[u][:], d["kT"][bass.ds(r * 2 + u, 1)].rearrange("o p t -> (o p) t")).then_inc(h_in[u], 16)
                    zv = d["z"][:, bass.ds(r * (2 * VD) + (ZDV * D + u * VD), VD)].rearrange("(t p) c -> p t c", p=P)
                    sp.dma_start(v[u][:, 0:TILES, :], zv).then_inc(h_in[u], 16)
                    cv = d["cache_v"][0, 0].rearrange("t h c -> t (h c)")[:, bass.ds(r * (2 * VD) + u * VD, VD)]
                    sp.dma_start(v[u][:, TILES:, :], cv.rearrange("(t p) c -> p t c", p=P)).then_inc(h_in[u], 16)
            sp.wait_ge(oa_in, 16)

        @block.gpsimd
        def _(pool):
            nc.gpsimd.memset(half[:], -0.5).then_inc(consts, 1)
            for u in range(2):
                nc.gpsimd.memset(out[u][:, NT, :], 0.0).then_inc(consts, 1)
            pool.wait_ge(consts, 3)
            with pool.Fori(0, DH // 2) as r:
                for u in range(2):
                    hold(pool, passed, mean_ready, at(r, u, 1, 1))
                    nc.gpsimd.tensor_tensor(rstd[:], mse[:], half[:], ALU.pow).then_inc(rstd_ready, 1)

        @block.tensor
        def _(pe):
            pe.wait_ge(small_in, 96)

            def scores(r, u, i):
                qc, n, _, chunks = UNITS[i]
                for m in range(2):
                    hold(pe, passed, exped[m], at(r, u, NU, i + 1))
                    rows = slice(m * HD, (m + 1) * HD)
                    for kc, c, w in chunks:
                        mm = nc.tensor.matmul(p_s[m][0:n, c:c + w], q[u][rows, qc:qc + n], k[u][rows, kc:kc + w],
                                              start=True, stop=True)
                    mm.then_inc(scored[m], 1)

            def apply(r, u, i):
                _, n, tiles, _ = UNITS[i]
                hold(pe, passed, mixed, at(r, u, NU, i + 1))
                groups = [G for G, (a, _) in enumerate(GRP) if a == i]
                for G in groups:
                    b, first = G % 2, GRP[G][1]
                    hold(pe, passed, copied, at(r, u, NG, G + 1))
                    for j, (_, _, w) in enumerate(tiles[first:first + 4]):
                        tr = nc.tensor.transpose(p_t[b][0:w, j, 0:n], mix[0:n, (first + j) * P:(first + j) * P + w], ident[0:n, 0:n])
                    tr.then_inc(turned, 1)
                hold(pe, passed, out_read, at(r, u, NU, i + 1))
                for G in groups:
                    b, first = G % 2, GRP[G][1]
                    hold(pe, passed, copied, at(r, u, NG, 2 + G + 1))
                    for j, (_, vt, w) in enumerate(tiles[first:first + 4]):
                        mm = nc.tensor.matmul(p_o[(u * NU + i) % 2][0:n, 0:VD], mixT[b][0:w, j, 0:n], v[u][0:w, vt, :],
                                              start=(first + j == 0), stop=(first + j == len(tiles) - 1))
                    mm.then_inc(applied, 1)

            with pe.Fori(0, DH // 2) as r:
                for u in range(2):
                    hold(pe, passed, h_in[u], r * 64 + 64)
                    hold(pe, passed, head_placed, at(r, u, 1, 2))
                    scores(r, u, 0)
                    for i in range(NU):
                        if i + 1 < NU:
                            scores(r, u, i + 1)
                        apply(r, u, i)
                    hold(pe, passed, gained, at(r, u, 1, 1))
                    hold(pe, passed, exped[1], at(r, u, NU, 1 + NU))
                    for t in range(TILES):
                        dst = p_s[0][:, t * P:(t + 1) * P] if t < NT else p_s[1][:, 0:P]
                        tr = nc.tensor.transpose(dst, sq[:, t, :], ident[:])
                    tr.then_inc(head_turned, 1)

        @block.scalar
        def _(act):
            act.wait_ge(lam_a, 3)
            nc.scalar.activation(lame[:], lams[:], ACT.Exp).then_inc(lam_b, 1)
            for m in range(2):
                act.sem_inc(exped[m], 1)
            act.sem_inc(copied, 2)
            act.sem_inc(head_placed, 2)

            def exps(r, u, i):
                n, nk = UNITS[i][1], sum(w for _, _, w in UNITS[i][2])
                b = (u * NU + i) % 2
                for m in range(2):
                    hold(act, passed, maxed[m], at(r, u, NU, i + 1))
                    nc.scalar.activation(prob[m][0:n, 0:nk], p_s[m][0:n, 0:nk], ACT.Exp, bias=negmax[0:n, b, m:m + 1],
                                         accum_out=total[0:n, b, m:m + 1]).then_inc(exped[m], 1)

            def copies(r, u, i):
                n = UNITS[i][1]
                for G, (a, first) in enumerate(GRP):
                    if a == i:
                        part = UNITS[i][2][first:first + 4]
                        hold(act, passed, turned, at(r, u, NG, G + 1))
                        hold(act, passed, applied, at(r, u, NG, G + 1))
                        w = part[-1][2] if len(part) == 1 else P
                        nc.scalar.activation(mixT[G % 2][0:w, 0:len(part), 0:n], p_t[G % 2][0:w, 0:len(part), 0:n],
                                             ACT.Copy).then_inc(copied, 1)

            with act.Fori(0, DH // 2) as r:
                for u in range(2):
                    exps(r, u, 0)
                    for i in range(NU):
                        if i + 1 < NU:
                            exps(r, u, i + 1)
                        copies(r, u, i)
                    hold(act, passed, out_read, at(r, u, NU, 2 + NU))
                    nc.scalar.activation(sq[:], out[u][:], ACT.Square, scale=VD ** -0.5).then_inc(squared, 1)
                    hold(act, passed, head_turned, at(r, u, 1, 1))
                    nc.scalar.activation(obT[:, bass.ds(r * (2 * TOK) + u * TOK, SEQ)], p_s[0][:], ACT.Copy)
                    nc.scalar.activation(obT[:, bass.ds(r * (2 * TOK) + (u * TOK + SEQ), P)], p_s[1][:, 0:P],
                                         ACT.Copy).then_inc(head_placed, 1)

        @block.vector
        def _(dve):
            dve.wait_ge(small_in, 96)
            dve.sem_inc(applied, 2)
            dve.sem_inc(out_read, 2)
            lv = lamv[:].rearrange("p (a b) c -> p a b c", b=2)
            nc.vector.tensor_tensor(lamp[:], lv[:, :, 0, :], lv[:, :, 1, :], ALU.mult).then_inc(lam_a, 1)
            dve.wait_ge(lam_a, 1)
            nc.vector.tensor_reduce(lams[:], lamp[:], AX.X, ALU.add).then_inc(lam_a, 1)
            nc.vector.tensor_scalar(gain[:], gain[:], 1.0 - LAM_INIT, None, ALU.mult).then_inc(lam_a, 1)
            dve.wait_ge(lam_b, 1)
            nc.vector.tensor_tensor(nlam[:], lame[:, 1:2], lame[:, 0:1], ALU.subtract).then_inc(lam_c, 1)
            dve.wait_ge(lam_c, 1)
            nc.vector.tensor_scalar(nlam[:], nlam[:], -LAM_INIT, None, ALU.add).then_inc(lam_c, 1)
            dve.wait_ge(lam_c, 2)
            dve.wait_ge(consts, 3)

            def maxima(r, u, i):
                n, nk = UNITS[i][1], sum(w for _, _, w in UNITS[i][2])
                b = (u * NU + i) % 2
                for m in range(2):
                    hold(dve, passed, scored[m], at(r, u, NU, i + 1))
                    if i < NT:
                        nc.vector.memset(p_s[m][0:HALF, i * P + HALF:(i + 1) * P], -1e30).then_inc(masked, 1)
                        hold(dve, passed, masked, at(r, u, 2 * NT, 2 * i + m + 1))
                    nc.vector.tensor_reduce(negmax[0:n, b, m:m + 1], p_s[m][0:n, 0:nk], AX.X, ALU.max,
                                            negate=True).then_inc(maxed[m], 1)

            def combine(r, u, i):
                n, nk = UNITS[i][1], sum(w for _, _, w in UNITS[i][2])
                b = (u * NU + i) % 2
                hold(dve, passed, exped[1], at(r, u, NU, i + 2))
                nc.vector.reciprocal(recip[0:n, b, :], total[0:n, b, :]).then_inc(recips, 1)
                hold(dve, passed, recips, at(r, u, NU, i + 1))
                nc.vector.scalar_tensor_tensor(ratio[0:n, b:b + 1], recip[0:n, b, 1:2], nlam[0:n, :], total[0:n, b, 0:1],
                                               ALU.mult, ALU.mult).then_inc(ratios, 1)
                hold(dve, passed, ratios, at(r, u, NU, i + 1))
                nc.vector.scalar_tensor_tensor(mix[0:n, 0:nk], prob[1][0:n, 0:nk], ratio[0:n, b:b + 1], prob[0][0:n, 0:nk],
                                               ALU.mult, ALU.add).then_inc(mixed, 1)

            def read_out(r, u, i):
                n, b = UNITS[i][1], (u * NU + i) % 2
                G = max(G for G, (a, _) in enumerate(GRP) if a == i)
                hold(dve, passed, applied, at(r, u, NG, 2 + G + 1))
                nc.vector.tensor_scalar(out[u][0:n, i, :], p_o[b][0:n, 0:VD], recip[0:n, b, 0:1], None,
                                        ALU.mult).then_inc(out_read, 1)

            with dve.Fori(0, DH // 2) as r:
                for u in range(2):
                    maxima(r, u, 0)
                    for i in range(NU):
                        combine(r, u, i)
                        if i + 1 < NU:
                            maxima(r, u, i + 1)
                        read_out(r, u, i)
                    hold(dve, passed, squared, at(r, u, 1, 1))
                    nc.vector.tensor_reduce(ms[:], sq[:], AX.X, ALU.add).then_inc(summed, 1)
                    hold(dve, passed, summed, at(r, u, 1, 1))
                    nc.vector.tensor_scalar(mse[:], ms[:], EPS, None, ALU.add).then_inc(mean_ready, 1)
                    hold(dve, passed, rstd_ready, at(r, u, 1, 1))
                    nc.vector.tensor_tensor(sq[:], out[u][:], rstd[:].unsqueeze(2).to_broadcast([P, TILES, VD]),
                                            ALU.mult).then_inc(normed, 1)
                    hold(dve, passed, normed, at(r, u, 1, 1))
                    nc.vector.tensor_tensor(sq[:], sq[:], gain[:].unsqueeze(1).to_broadcast([P, TILES, VD]),
                                            ALU.mult).then_inc(gained, 1)


def merge(nc, sem, d, hT, oaT, obT):
    UNIT = 2 * GROUPS
    with ExitStack() as ctx:
        def sb(name, shape, dt=F32):
            return ctx.enter_context(nc.sbuf_tensor(name, shape, dt))

        w = [[sb(f"mg_w{i}_{n}", [P, KC, P]) for n in range(4)] for i in range(2)]
        sig = [sb(f"mg_sig{b}", [P, 2, GCOL]) for b in range(2)]
        prod = [sb(f"mg_prod{b}", [P, 2, GCOL]) for b in range(2)]
        m = [sb(f"mg_m{i}", [P, TOK]) for i in range(2)]
        p = [[ctx.enter_context(nc.psum_tensor(f"mg_p{b}_{n}", [P, BANK], F32)) for n in range(4)] for b in range(2)]
        made_g, made, gated, multiplied, summed, passed = (sem("mg_" + n) for n in ("made_g", "made", "gated", "multiplied", "summed", "passed"))
        w_in = [sem(f"mg_w_in{i}") for i in range(2)]
        m_out = [sem(f"mg_m_out{i}", True) for i in range(2)]
        obT3 = obT[:].rearrange("p (h t) -> p h t", h=DH)
        block = ctx.enter_context(nc.Block())

        @block.sync
        def _(sp):
            with sp.Fori(0, KC // 2) as r:
                for i in range(2):
                    hold(sp, passed, summed, r * UNIT + (i * GROUPS + 1))
                    for n, (src, col) in enumerate(((d["w_in"], W_GATE), (d["w_in"], W_GATE + D), (d["w_gla_out"], 0), (d["w_diff_out"], 0))):
                        cols = src[0, :, bass.ds(r * (2 * P) + (col + i * P), P)]
                        sp.dma_start(w[i][n][:], cols.rearrange("(k p) n -> p k n", p=P)).then_inc(w_in[i], 16)

        @block.tensor
        def _(pe):
            with pe.Fori(0, KC // 2) as r:
                for i in range(2):
                    hold(pe, passed, w_in[i], r * 64 + 64)
                    for g in range(GROUPS):
                        u = i * GROUPS + g
                        b, cols = u % 2, slice(g * GCOL, (g + 1) * GCOL)
                        hold(pe, passed, multiplied, r * UNIT + (u + 1))
                        for n, src in enumerate((hT, hT, oaT, obT3)):
                            for k in range(KC):
                                mm = nc.tensor.matmul(p[b][n][:, 0:GCOL], w[i][n][:, k, :], src[:, k, cols],
                                                      start=(k == 0), stop=(k == KC - 1))
                            if n == 1:
                                mm.then_inc(made_g, 1)
                        mm.then_inc(made, 1)

        @block.scalar
        def _(act):
            with act.Fori(0, KC // 2) as r:
                for u in range(UNIT):
                    b = u % 2
                    hold(act, passed, made_g, r * UNIT + (u + 1))
                    hold(act, passed, multiplied, r * UNIT + (u + 1))
                    for n in range(2):
                        s = nc.scalar.activation(sig[b][:, n, :], p[b][n][:, 0:GCOL], ACT.Sigmoid)
                    s.then_inc(gated, 1)

        @block.vector
        def _(dve):
            dve.sem_inc(multiplied, 2)
            dve.sem_inc(summed, UNIT + 1 - GROUPS)

            def unit(r, u):
                i, b, g = u // GROUPS, u % 2, u % GROUPS
                hold(dve, passed, gated, r * UNIT + (u + 1))
                hold(dve, passed, made, r * UNIT + (u + 1))
                for n in range(2):
                    x = nc.vector.tensor_tensor(prod[b][:, n, :], sig[b][:, n, :], p[b][2 + n][:, 0:GCOL], ALU.mult)
                x.then_inc(multiplied, 1)
                if g == 0:
                    hold(dve, passed, m_out[i], r * 16)
                hold(dve, passed, multiplied, r * UNIT + (2 + u + 1))
                nc.vector.tensor_tensor(m[i][:, g * GCOL:(g + 1) * GCOL], prod[b][:, 0, :], prod[b][:, 1, :],
                                        ALU.add).then_inc(summed, 1)

            for u in range(UNIT):
                unit(0, u)
            with dve.Fori(1, KC // 2) as r:
                for u in range(UNIT):
                    unit(r, u)

        @block.gpsimd
        def _(pool):
            with pool.Fori(0, KC // 2) as r:
                for i in range(2):
                    hold(pool, passed, summed, r * UNIT + (UNIT + 1 - GROUPS + (i + 1) * GROUPS))
                    nc.gpsimd.dma_start(d["mT"][bass.ds(r * 2 + i, 1)].rearrange("o p t -> (o p) t"), m[i][:]).then_inc(m_out[i], 16)
            for i in range(2):
                pool.wait_ge(m_out[i], 16 * KC // 2)


def mix_out(nc, sem, d, h2T):
    with ExitStack() as ctx:
        def sb(name, shape, dt=F32):
            return ctx.enter_context(nc.sbuf_tensor(name, shape, dt))

        ident, w = sb("mo_ident", [P, P]), sb("mo_w", [P, KC, D])
        rows = sb("mo_rows", [P, 2, 3, D])
        mt = [sb(f"mo_mt{u}", [P, KC, P]) for u in range(2)]
        x = [sb(f"mo_x{u}", [P, D]) for u in range(2)]
        xm, xs, sq = (sb("mo_" + n, [P, D]) for n in ("xm", "xs", "sq"))
        x1 = [sb(f"mo_x1{u}", [P, D]) for u in range(2)]
        h2 = [sb(f"mo_h2{u}", [P, D]) for u in range(2)]
        ms, mse, rstd, half = (sb("mo_" + n, [P, 1]) for n in ("ms", "mse", "rstd", "half"))
        p_m = [ctx.enter_context(nc.psum_tensor(f"mo_pm{b}", [P, D], F32)) for b in range(2)]
        p_t = ctx.enter_context(nc.psum_tensor("mo_pt", [P, KC, P], F32))
        names = "small_in consts made scaled added squared mean rstd normed shifted turned placed passed"
        (small_in, consts, made, scaled, added, squared, mean_ready, rstd_ready, normed, shifted, turned, placed,
         passed) = (sem("mo_" + n) for n in names.split())
        t_in = [sem(f"mo_t_in{u}") for u in range(2)]
        x1_out = [sem(f"mo_x1_out{u}", True) for u in range(2)]
        block = ctx.enter_context(nc.Block())

        def at(r, u, each, c):
            return r * (2 * each) + (u * each + c)

        def over_tiles(eng, tile):
            for u in range(2):
                tile(0, u, 0)
            with eng.Fori(1, NT // 2) as r:
                for u in range(2):
                    tile(r, u, 0)
            tile(NT // 2, 0, 1)

        def cols(r, u):
            return bass.ds(r * (2 * P) + u * P, P)

        @block.sync
        def _(sp):
            sp.dma_start(w[:], d["w_out"][0].rearrange("(k p) n -> p k n", p=P)).then_inc(small_in, 16)
            sp.dma_start(ident[:], d["ident"]).then_inc(small_in, 16)
            for s in range(2):
                sp.dma_start(rows[:, s, :, :], d["mod"][s:s + 1, GT1 * D:(SC2 + 1) * D].to_broadcast([P, 3 * D])
                             .rearrange("p (a n) -> p a n", a=3)).then_inc(small_in, 16)

            def tile(r, u, s):
                hold(sp, passed, added, at(r, u, 1, -1))
                sp.dma_start(mt[u][:], d["mT"][:, :, cols(r, u)].rearrange("k p t -> p k t")).then_inc(t_in[u], 16)
                if s:
                    sp.wait_ge(consts, 3)
                    sp.dma_start(x[u][0:DEC, :], d["x_sample"][0]).then_inc(t_in[u], 16)
                else:
                    sp.dma_start(x[u][:], d["x_prompt"][0, cols(r, u)]).then_inc(t_in[u], 16)

            over_tiles(sp, tile)

        @block.gpsimd
        def _(pool):
            nc.gpsimd.memset(half[:], -0.5).then_inc(consts, 1)
            pool.wait_ge(consts, 1)

            def tile(r, u, s):
                hold(pool, passed, mean_ready, at(r, u, 1, 1))
                nc.gpsimd.tensor_tensor(rstd[:], mse[:], half[:], ALU.pow).then_inc(rstd_ready, 1)
                hold(pool, passed, shifted, at(r, u, 1, 1))
                nc.gpsimd.dma_start(d["x1"][cols(r, u), :], x1[u][:]).then_inc(x1_out[u], 16)
                nc.gpsimd.dma_start(d["h2"][cols(r, u), :], h2[u][:]).then_inc(x1_out[u], 16)

            for u in range(2):
                tile(0, u, 0)
            with pool.Fori(1, NT // 2) as r:
                for u in range(2):
                    tile(r, u, 0)
            nc.gpsimd.memset(x[0][:], 0.0).then_inc(consts, 2)
            tile(NT // 2, 0, 1)
            pool.wait_ge(x1_out[0], 32 * (NT // 2 + 1))
            pool.wait_ge(x1_out[1], 32 * (NT // 2))

        @block.tensor
        def _(pe):
            pe.wait_ge(small_in, 64)

            def tile(r, u, s):
                hold(pe, passed, t_in[u], r * 32 + 32)
                hold(pe, passed, scaled, at(r, u, 1, -1))
                for c in range(2):
                    for k in range(KC):
                        mm = nc.tensor.matmul(p_m[u][:, c * BANK:(c + 1) * BANK], mt[u][:, k, :], w[:, k, c * BANK:(c + 1) * BANK],
                                              start=(k == 0), stop=(k == KC - 1))
                mm.then_inc(made, 1)

            def turn(r, u, s):
                hold(pe, passed, shifted, at(r, u, 1, 1))
                hold(pe, passed, placed, at(r, u, 1, 0))
                for k in range(KC):
                    tr = nc.tensor.transpose(p_t[:, k, :], h2[u][:, k * P:(k + 1) * P], ident[:])
                tr.then_inc(turned, 1)

            tile(0, 0, 0)
            tile(0, 1, 0)
            turn(0, 0, 0)
            with pe.Fori(1, NT // 2) as r:
                tile(r, 0, 0)
                turn(r - 1, 1, 0)
                tile(r, 1, 0)
                turn(r, 0, 0)
            tile(NT // 2, 0, 1)
            turn(NT // 2 - 1, 1, 0)
            turn(NT // 2, 0, 1)

        @block.scalar
        def _(act):
            def tile(r, u, s):
                hold(act, passed, added, at(r, u, 1, 1))
                nc.scalar.activation(sq[:], x1[u][:], ACT.Square, scale=D ** -0.5, accum_out=ms[:]).then_inc(squared, 1)
                hold(act, passed, turned, at(r, u, 1, 1))
                nc.scalar.activation(h2T[:, :, cols(r, u)], p_t[:], ACT.Copy).then_inc(placed, 1)

            over_tiles(act, tile)

        @block.vector
        def _(dve):
            dve.wait_ge(small_in, 64)

            def tile(r, u, s):
                hold(dve, passed, t_in[u], r * 32 + 32)
                hold(dve, passed, made, at(r, u, 1, 1))
                nc.vector.tensor_tensor(xm[:], p_m[u][:], rows[:, s, 0, :], ALU.mult).then_inc(scaled, 1)
                hold(dve, passed, scaled, at(r, u, 1, 1))
                hold(dve, passed, x1_out[u], r * 32)
                nc.vector.tensor_tensor(x1[u][:], xm[:], x[u][:], ALU.add).then_inc(added, 1)
                hold(dve, passed, squared, at(r, u, 1, 1))
                nc.vector.tensor_scalar(mse[:], ms[:], EPS, None, ALU.add).then_inc(mean_ready, 1)
                hold(dve, passed, rstd_ready, at(r, u, 1, 1))
                nc.vector.scalar_tensor_tensor(xs[:], x1[u][:], rstd[:], rows[:, s, 2, :], ALU.mult, ALU.mult).then_inc(normed, 1)
                hold(dve, passed, normed, at(r, u, 1, 1))
                hold(dve, passed, turned, at(r, u, 1, -1))
                nc.vector.tensor_tensor(h2[u][:], xs[:], rows[:, s, 1, :], ALU.add).then_inc(shifted, 1)

            over_tiles(dve, tile)


def keys(nc, sem, d, h2T):
    UNIT = 2 * GROUPS
    with ExitStack() as ctx:
        def sb(name, shape, dt=F32):
            return ctx.enter_context(nc.sbuf_tensor(name, shape, dt))

        ident = sb("ky_ident", [P, P])
        sub, subT = sb("ky_sub", [P, 2, P]), sb("ky_subT", [P, 2, P])
        w = [sb(f"ky_w{i}", [P, KC, P]) for i in range(2)]
        qc = [sb(f"ky_q{i}", [P, TOK]) for i in range(2)]
        sc = [sb(f"ky_s{i}", [P, TILES, NKEY]) for i in range(2)]
        p_q = [ctx.enter_context(nc.psum_tensor(f"ky_pq{g}", [P, BANK], F32)) for g in range(GROUPS)]
        p_s = [ctx.enter_context(nc.psum_tensor(f"ky_ps{g}", [P, GROUPS, NKEY], F32)) for g in range(TILES // 3)]
        small_in, turned, made, copied, scored, placed, passed = (
            sem("ky_" + n) for n in ("small_in", "turned", "made", "copied", "scored", "placed", "passed"))
        w_in = [sem(f"ky_w_in{i}") for i in range(2)]
        s_out = [sem(f"ky_s_out{i}", True) for i in range(2)]
        block = ctx.enter_context(nc.Block())

        @block.sync
        def _(sp):
            sp.dma_start(ident[:], d["ident"]).then_inc(small_in, 16)
            for n, s in enumerate(("sub_keys1", "sub_keys2")):
                sp.dma_start(sub[:, n, :], d[s][0]).then_inc(small_in, 16)
            with sp.Fori(0, PH) as r:
                for i in range(2):
                    hold(sp, passed, copied, r * UNIT + (i + 1) * GROUPS)
                    sp.dma_start(w[i][:], d["w_pq"][0, :, bass.ds(r * (2 * P) + i * P, P)].rearrange("(k p) n -> p k n", p=P)).then_inc(w_in[i], 16)

        @block.tensor
        def _(pe):
            pe.wait_ge(small_in, 48)
            for n in range(2):
                tr = nc.tensor.transpose(p_s[0][:, n, :], sub[:, n, :], ident[:])
            tr.then_inc(turned, 1)
            pe.wait_ge(turned, 2)
            with pe.Fori(0, PH) as r:
                for i in range(2):
                    hold(pe, passed, w_in[i], r * 16 + 16)
                    for g in range(GROUPS):
                        hold(pe, passed, copied, r * UNIT + (UNIT - GROUPS + i * GROUPS + g + 1))
                        for k in range(KC):
                            mm = nc.tensor.matmul(p_q[g][:, 0:GCOL], w[i][:, k, :], h2T[:, k, g * GCOL:(g + 1) * GCOL],
                                                  start=(k == 0), stop=(k == KC - 1))
                        mm.then_inc(made, 1)
                for i in range(2):
                    hold(pe, passed, copied, r * UNIT + (UNIT + (i + 1) * GROUPS))
                    for g in range(GROUPS):
                        hold(pe, passed, placed, r * UNIT + (i * GROUPS + g + 1))
                        for t in range(GROUPS):
                            c = (g * GROUPS + t) * P
                            mm = nc.tensor.matmul(p_s[g][:, t, :], qc[i][:, c:c + P], subT[:, i, :], start=True, stop=True)
                        mm.then_inc(scored, 1)

        @block.scalar
        def _(act):
            act.sem_inc(copied, UNIT)
            with act.Fori(0, PH) as r:
                for i in range(2):
                    hold(act, passed, scored, r * UNIT + (i + 1) * GROUPS)
                    for g in range(GROUPS):
                        hold(act, passed, made, r * UNIT + (i * GROUPS + g + 1))
                        nc.scalar.activation(qc[i][:, g * GCOL:(g + 1) * GCOL], p_q[g][:, 0:GCOL], ACT.Copy).then_inc(copied, 1)

        @block.vector
        def _(dve):
            dve.sem_inc(placed, GROUPS)
            dve.sem_inc(scored, UNIT)
            dve.wait_ge(turned, 1)
            nc.vector.tensor_copy(subT[:], p_s[0][:, 0:2, :]).then_inc(turned, 1)

            def round_(r):
                for i in range(2):
                    hold(dve, passed, s_out[i], r * 16)
                    for g in range(GROUPS):
                        hold(dve, passed, scored, r * UNIT + (UNIT + i * GROUPS + g + 1))
                        nc.vector.tensor_copy(sc[i][:, g * GROUPS:(g + 1) * GROUPS, :], p_s[g][:]).then_inc(placed, 1)

            round_(0)
            with dve.Fori(1, PH) as r:
                round_(r)

        @block.gpsimd
        def _(pool):
            with pool.Fori(0, PH) as r:
                for i in range(2):
                    hold(pool, passed, placed, r * UNIT + (GROUPS + (i + 1) * GROUPS))
                    dst = d["scores"].rearrange("t j n -> t (j n)")[:, bass.ds(r * (2 * NKEY) + i * NKEY, NKEY)]
                    nc.gpsimd.dma_start(dst.rearrange("(t p) n -> p t n", p=P), sc[i][:]).then_inc(s_out[i], 16)
            for i in range(2):
                pool.wait_ge(s_out[i], 16 * PH)


def retrieve(nc, sem, d):
    SLOTS = PH * TOPK
    STEPS = 18
    W, RING = 8, 16
    ROUNDS = SLOTS // RING
    FAR = -3.0e38
    COPIES = P // DEC
    FEW = SLOTS // COPIES
    SHARE = (1, 5, 9, 13)
    SEGMENTS = [(0, 2, True), (2, 3, False), (5, 3, True)]
    ON_DVE = sum(n * len(SHARE) for _, n, shared in SEGMENTS if shared)
    ON_PE = SLOTS - ON_DVE

    def slots_of(n):
        return SLOTS if n == P else FEW

    def rounds_of(n):
        return slots_of(n) // RING

    def segments_of(n):
        return SEGMENTS if n == P else [(0, rounds_of(n), False)]

    with ExitStack() as ctx:
        def sb(name, shape, dt=F32):
            return ctx.enter_context(nc.sbuf_tensor(name, shape, dt))

        ident = sb("rt_ident", [P, P])
        zero = sb("rt_zero", [P, BANK])
        iota = sb("rt_iota", [P, TOPK])
        gate2 = sb("rt_gate2", [P, 2, D])
        sc, sc2 = sb("rt_sc", [P, 2 * PH, NKEY]), sb("rt_sc2", [P, 2 * PH, NKEY])
        val, ind, indf = sb("rt_val", [P, 2 * PH, TOPK]), sb("rt_ind", [P, 2 * PH, TOPK], U32), sb("rt_indf", [P, 2 * PH, TOPK])
        cand, cand2 = sb("rt_cand", [P, PH, TOPK * TOPK]), sb("rt_cand2", [P, PH, TOPK * TOPK])
        best, pos = sb("rt_best", [P, PH, TOPK]), sb("rt_pos", [P, PH, TOPK], U32)
        part, partf = sb("rt_part", [P, 2, SLOTS], U32), sb("rt_partf", [P, 2, SLOTS])
        pick = [sb(f"rt_pick{i}", [P, SLOTS, TOPK]) for i in range(2)]
        chosen = sb("rt_chosen", [P, 2, SLOTS])
        idxf = sb("rt_idxf", [P, SLOTS])
        idx = [sb(f"rt_idx{u}", [P, SLOTS], U32) for u in range(2)]
        win = [sb(f"rt_win{w}", [P, W], U32) for w in range(2)]
        below, e, esum, erec = sb("rt_below", [P, PH, TOPK]), sb("rt_e", [P, PH, TOPK]), sb("rt_esum", [P, PH]), sb("rt_erec", [P, PH])
        prob = [sb(f"rt_prob{u}", [P, SLOTS]) for u in range(2)]
        dot, act_dot = sb("rt_dot", [P, SLOTS]), sb("rt_act_dot", [P, SLOTS])
        weight = sb("rt_weight", [P, SLOTS])
        h2 = [sb(f"rt_h2{u}", [P, D]) for u in range(2)]
        x1 = [sb(f"rt_x1{u}", [P, D]) for u in range(2)]
        y = [sb(f"rt_y{u}", [P, D]) for u in range(2)]
        acc = sb("rt_acc", [P, D])
        stack = sb("rt_stack", [P, DEC])
        few_idx, few_prob = sb("rt_few_idx", [P, FEW], U32), sb("rt_few_prob", [P, FEW])
        ring = [sb(f"rt_ring{b}", [P, D]) for b in range(RING)]
        diag = [sb(f"rt_diag{b}", [P, P]) for b in range(W)]
        ffn = ctx.enter_context(nc.psum_tensor("rt_ffn", [P, D], F32))
        names = ("small_in consts sc_in sc_used step idx_ready shifted exped dotted gelued weighted diag_ready added "
                 "ffn_done ffn_read y_ready windowed cleared shared_add gated2 passed")
        (small_in, consts, sc_in, sc_used, step, idx_ready, shifted, exped, dotted, gelued, weighted, diag_ready, added,
         ffn_done, ffn_read, y_ready, windowed, cleared, shared_add, gated2, passed) = (sem("rt_" + n) for n in names.split())
        idx_spread, prob_spread = sem("rt_idx_spread"), sem("rt_prob_spread")
        rows_in = [sem(f"rt_rows_in{u}") for u in range(2)]
        slot_in = [sem(f"rt_slot_in{b}", True) for b in range(RING)]
        y_out = [sem(f"rt_y_out{u}") for u in range(2)]
        block = ctx.enter_context(nc.Block())

        def at(r, u, each, c):
            return r * (2 * each) + (u * each + c)

        def over_tiles(eng, tile):
            with eng.Fori(0, NT // 2) as r:
                for u in range(2):
                    tile(r, u, P)
            tile(NT // 2, 0, DEC)

        @block.sync
        def _(sp):
            sp.dma_start(ident[:], d["ident"]).then_inc(small_in, 16)
            sp.dma_start(stack[:], d["stack"]).then_inc(small_in, 16)
            sp.dma_start(iota[:], d["iota"].to_broadcast([P, TOPK])).then_inc(small_in, 16)
            for s in range(2):
                sp.dma_start(gate2[:, s, :], d["mod"][s:s + 1, GT2 * D:].to_broadcast([P, D])).then_inc(small_in, 16)

            def load(r, u, n):
                rows = bass.ds(r * (2 * P) + u * P, P)
                hold(sp, passed, sc_used, at(r, u, 1, 1))
                sp.dma_start(sc[:], d["scores"][rows]).then_inc(sc_in, 16)
                hold(sp, passed, y_ready, at(r, u, 1, 1))
                if n == P:
                    sp.dma_start(h2[u % 2][:], d["h2"][rows]).then_inc(rows_in[u % 2], 16)
                else:
                    for a in range(COPIES):
                        sp.dma_start(h2[u % 2][a * DEC:(a + 1) * DEC, :], d["h2"][SEQ:SEQ + DEC]).then_inc(rows_in[u % 2], 16)
                sp.dma_start(x1[u % 2][:], d["x1"][rows]).then_inc(rows_in[u % 2], 16)

            def store(r, u, n):
                hold(sp, passed, y_ready, at(r, u, 1, 3))
                dst = d["y_prompt"][0, bass.ds(r * (2 * P) + u * P, P)] if n == P else d["y_sample"][0]
                sp.dma_start(dst, y[u % 2][0:n, :]).then_inc(y_out[u % 2], 16)

            load(0, 0, P)
            load(0, 1, P)
            with sp.Fori(0, NT // 2 - 1) as r:
                for u in range(2):
                    store(r, u, P)
                    load(r, u + 2, P)
            store(NT // 2 - 1, 0, P)
            load(NT // 2, 0, DEC)
            sp.wait_ge(idx_ready, TILES)
            for a in range(COPIES):
                sp.dma_start(few_idx[a * DEC:(a + 1) * DEC, :], idx[0][0:DEC, a * FEW:(a + 1) * FEW]).then_inc(idx_spread, 16)
            sp.wait_ge(step, STEPS * TILES)
            for a in range(COPIES):
                sp.dma_start(few_prob[a * DEC:(a + 1) * DEC, :], prob[0][0:DEC, a * FEW:(a + 1) * FEW]).then_inc(prob_spread, 16)
            store(NT // 2 - 1, 1, P)
            store(NT // 2, 0, DEC)
            sp.wait_ge(y_out[0], 16 * (NT // 2 + 1))
            sp.wait_ge(y_out[1], 16 * (NT // 2))

        @block.gpsimd
        def _(pool):
            nc.gpsimd.memset(zero[:], 0.0).then_inc(consts, 1)

            def fetch(r, u, n, table, first_dot, first_add, phase):
                src = idx[u] if n == P else few_idx
                with pool.Fori(0, rounds_of(n)) as q:
                    for w in range(2):
                        hold(pool, passed, dotted, first_dot(q, w))
                        hold(pool, passed, added, first_add(q, w))
                        nc.gpsimd.tensor_copy(win[w][:], src[:, bass.ds(q * RING + w * W, W)]).then_inc(windowed, 1)
                        hold(pool, passed, windowed, at(r, u, 4 * ROUNDS, phase * 2 * rounds_of(n) + w + 1) + q * 2)
                        for b in range(W):
                            s = w * W + b
                            nc.gpsimd.indirect_dma_start(ring[s][:], None, table,
                                                         bass.IndirectOffsetOnAxis(ap=win[w][:, b:b + 1], axis=0)).then_inc(slot_in[s], 16)

            def tile(r, u, n):
                hold(pool, passed, idx_ready, at(r, u, 1, 1))
                if n != P:
                    pool.wait_ge(idx_spread, 16 * COPIES)
                fetch(r, u, n, d["peer_u"][0],
                      lambda q, w: at(r, u, SLOTS, W * (w + 1)) + q * RING,
                      lambda q, w: at(r, u, SLOTS, W * (w + 1)), 0)
                fetch(r, u, n, d["peer_v"][0],
                      lambda q, w: at(r, u, SLOTS, slots_of(n) + W * (w + 1)),
                      lambda q, w: at(r, u, SLOTS, W * (w + 1)) + q * RING, 1)

            over_tiles(pool, tile)

        @block.scalar
        def _(act):
            def softmax_exp(r, u):
                hold(act, passed, shifted, at(r, u, 1, 1))
                nc.scalar.activation(e[:], below[:], ACT.Exp).then_inc(exped, 1)

            def tile(r, u, n):
                k = slots_of(n)
                hold(act, passed, dotted, at(r, u, SLOTS, RING + k))
                nc.scalar.activation(act_dot[:, 0:k], dot[:, 0:k], ACT.Gelu).then_inc(gelued, 1)
                hold(act, passed, weighted, at(r, u, 1, 1))
                for first, rounds, shared in segments_of(n):
                    with act.Fori(0, rounds) as q:
                        for s in range(RING):
                            if shared and s in SHARE:
                                continue
                            hold(act, passed, added, at(r, u, SLOTS, (first + 1) * RING + s + 1 - W) + q * RING)
                            nc.scalar.activation(diag[s % W][:, 0:n], (ident if n == P else stack)[:, 0:n], ACT.Copy,
                                                 scale=weight[:, bass.ds(q * RING + (first * RING + s), 1)]).then_inc(diag_ready, 1)
                    if n == P and first == SEGMENTS[1][0]:
                        softmax_exp(r, u + 1)

            act.wait_ge(small_in, 80)
            softmax_exp(0, 0)
            over_tiles(act, tile)

        @block.tensor
        def _(pe):
            pe.wait_ge(consts, 1)
            pe.wait_ge(small_in, 80)

            def edge(n, first):
                for c in range(D // BANK):
                    mm = nc.tensor.matmul(ffn[0:n, c * BANK:(c + 1) * BANK], zero[0:n, 0:n], zero[0:n, :],
                                          start=first, stop=not first)
                return mm

            def tile(r, u, n):
                hold(pe, passed, ffn_read, at(r, u, 1, 1))
                edge(n, True)
                diags, shares = 0, 0
                for first, rounds, shared in segments_of(n):
                    each = RING - len(SHARE) if shared else RING
                    with pe.Fori(0, rounds) as q:
                        mine = 0
                        for s in range(RING):
                            if not (shared and s in SHARE):
                                mine += 1
                                hold(pe, passed, diag_ready, at(r, u, ON_PE, diags + mine) + q * each)
                                hold(pe, passed, slot_in[s], at(r, u, 32 * ROUNDS, 16 * (rounds_of(n) + first) + 16) + q * 16)
                                theirs = 0
                                if shared and s % W == W - 1:
                                    theirs = sum(s - W < x <= s for x in SHARE)
                                    hold(pe, passed, shared_add, at(r, u, ON_DVE, 1 + shares + sum(x <= s for x in SHARE)) + q * len(SHARE))
                                for c in range(D // BANK):
                                    mm = nc.tensor.matmul(ffn[0:n, c * BANK:(c + 1) * BANK], diag[s % W][:, 0:n],
                                                          ring[s][:, c * BANK:(c + 1) * BANK], start=False, stop=False)
                                mm.then_inc(added, 1 + theirs)
                    diags += rounds * each
                    shares += rounds * len(SHARE) if shared else 0
                edge(n, False).then_inc(ffn_done, 1)

            over_tiles(pe, tile)

        @block.vector
        def _(dve):
            dve.wait_ge(small_in, 80)
            dve.sem_inc(sc_used, 1)
            dve.sem_inc(y_ready, 2)
            dve.sem_inc(dotted, RING)
            dve.sem_inc(added, RING)
            dve.sem_inc(ffn_read, 1)
            dve.sem_inc(shared_add, 1)

            def select(r, u):
                done = [0]

                def settle(ins):
                    done[0] += 1
                    ins.then_inc(step, 1)
                    hold(dve, passed, step, at(r, u, STEPS, done[0]))

                hold(dve, passed, sc_in, at(r, u, 16, 16))
                maps, heads = range(2 * PH), range(PH)

                def top16(rows, values, spare, top, where):
                    for j in rows:
                        m = nc.vector.max(top[:, j, 0:8], values[:, j, :])
                    settle(m)
                    for j in rows:
                        nc.vector.max_index(where[:, j, 0:8], top[:, j, 0:8], values[:, j, :])
                        m = nc.vector.match_replace(spare[:, j, :], top[:, j, 0:8], values[:, j, :], FAR)
                    settle(m)
                    for j in rows:
                        m = nc.vector.max(top[:, j, 8:16], spare[:, j, :])
                    settle(m)
                    for j in rows:
                        m = nc.vector.max_index(where[:, j, 8:16], top[:, j, 8:16], spare[:, j, :])
                    settle(m)

                top16(maps, sc, sc2, val, ind)
                dve.sem_inc(sc_used, 1)
                pair = val[:].rearrange("p (h e) k -> p h e k", e=2)
                nc.vector.tensor_copy(indf[:], ind[:])
                settle(nc.vector.tensor_tensor(cand[:].rearrange("p h (i j) -> p h i j", j=TOPK),
                                               pair[:, :, 0, :].unsqueeze(3).to_broadcast([P, PH, TOPK, TOPK]),
                                               pair[:, :, 1, :].unsqueeze(2).to_broadcast([P, PH, TOPK, TOPK]), ALU.add))
                top16(heads, cand, cand2, best, pos)
                nc.vector.tensor_tensor(below[:], best[:], best[:, :, 0:1].to_broadcast([P, PH, TOPK]), ALU.subtract).then_inc(shifted, 1)
                flat = pos[:].rearrange("p h k -> p (h k)")
                nc.vector.tensor_scalar(part[:, 0, :], flat, 4, None, ALU.logical_shift_right)
                settle(nc.vector.tensor_scalar(part[:, 1, :], flat, TOPK - 1, None, ALU.bitwise_and))
                settle(nc.vector.tensor_copy(partf[:], part[:]))
                for i in range(2):
                    eq = nc.vector.tensor_tensor(pick[i][:], partf[:, i, :].unsqueeze(2).to_broadcast([P, SLOTS, TOPK]),
                                                 iota[:].unsqueeze(1).to_broadcast([P, SLOTS, TOPK]), ALU.is_equal)
                settle(eq)
                lists = indf[:].rearrange("p (h e) k -> p h e k", e=2)
                for i in range(2):
                    grid = pick[i][:].rearrange("p (h k) i -> p h k i", h=PH)
                    mu = nc.vector.tensor_tensor(grid, grid, lists[:, :, i, :].unsqueeze(2).to_broadcast([P, PH, TOPK, TOPK]), ALU.mult)
                settle(mu)
                for i in range(2):
                    re = nc.vector.tensor_reduce(chosen[:, i, :], pick[i][:], AX.X, ALU.add)
                settle(re)
                settle(nc.vector.scalar_tensor_tensor(idxf[:], chosen[:, 0, :], float(NKEY), chosen[:, 1, :], ALU.mult, ALU.add))
                nc.vector.tensor_copy(idx[u % 2][:], idxf[:]).then_inc(idx_ready, 1)
                hold(dve, passed, exped, at(r, u, 1, 1))
                settle(nc.vector.tensor_reduce(esum[:], e[:], AX.X, ALU.add))
                settle(nc.vector.reciprocal(erec[:], esum[:]))
                nc.vector.tensor_tensor(prob[u % 2][:].rearrange("p (h k) -> p h k", h=PH), e[:],
                                        erec[:].unsqueeze(2).to_broadcast([P, PH, TOPK]), ALU.mult).then_inc(step, 1)
                assert done[0] + 1 == STEPS, done

            def dots(r, u, n):
                extra = 0 if n == P else 16 * (COPIES - 1)
                hold(dve, passed, rows_in[u % 2], r * 32 + (32 + 32 * (u // 2) + extra))
                with dve.Fori(0, rounds_of(n)) as q:
                    for s in range(RING):
                        hold(dve, passed, slot_in[s], at(r, u, 32 * ROUNDS, 16) + q * 16)
                        nc.vector.scalar_tensor_tensor(ring[s][:], ring[s][:], 1.0, h2[u % 2][:], ALU.mult, ALU.mult,
                                                       accum_out=dot[:, bass.ds(q * RING + s, 1)]).then_inc(dotted, 1)

            def weigh(r, u, n):
                hold(dve, passed, gelued, at(r, u, 1, 1))
                hold(dve, passed, step, at(r, u, STEPS, STEPS))
                if n != P:
                    dve.wait_ge(prob_spread, 16 * COPIES)
                k, share_of = slots_of(n), prob[u % 2] if n == P else few_prob
                nc.vector.tensor_tensor(weight[:, 0:k], act_dot[:, 0:k], share_of[:], ALU.mult).then_inc(weighted, 1)
                nc.vector.memset(acc[:], 0.0).then_inc(cleared, 1)
                hold(dve, passed, cleared, at(r, u, 1, 1))
                hold(dve, passed, weighted, at(r, u, 1, 1))

            def share(r, u, n, segment):
                first, rounds, _ = SEGMENTS[segment]
                before = sum(k * len(SHARE) for _, k, shared in SEGMENTS[:segment] if shared)
                with dve.Fori(0, rounds) as q:
                    for i, s in enumerate(SHARE):
                        hold(dve, passed, slot_in[s], at(r, u, 32 * ROUNDS, 16 * (ROUNDS + first) + 16) + q * 16)
                        hold(dve, passed, shared_add, at(r, u, ON_DVE, before + i + 1) + q * len(SHARE))
                        nc.vector.scalar_tensor_tensor(acc[0:n, :], ring[s][0:n, :], weight[0:n, bass.ds(q * RING + (first * RING + s), 1)],
                                                       acc[0:n, :], ALU.mult, ALU.add).then_inc(shared_add, 1)

            def finish(r, u, n):
                b = u % 2
                hold(dve, passed, ffn_done, at(r, u, 1, 1))
                hold(dve, passed, y_out[b], r * 16 + 16 * (u // 2))
                nc.vector.tensor_tensor(y[b][0:n, :], ffn[0:n, :], acc[0:n, :], ALU.add).then_inc(ffn_read, 1)
                hold(dve, passed, ffn_read, at(r, u, 1, 2))
                nc.vector.tensor_tensor(y[b][0:n, :], y[b][0:n, :], gate2[0:n, 0 if n == P else 1, :], ALU.mult).then_inc(gated2, 1)
                hold(dve, passed, gated2, at(r, u, 1, 1))
                nc.vector.tensor_tensor(y[b][0:n, :], y[b][0:n, :], x1[b][0:n, :], ALU.add).then_inc(y_ready, 1)

            def turn(r, u, n, after):
                weigh(r, u, n)
                share(r, u, n, 0)
                select(r, u + 1)
                share(r, u, n, 2)
                dots(r, u + 1, after)
                finish(r, u, n)

            select(0, 0)
            dots(0, 0, P)
            for u in range(2):
                turn(0, u, P, P)
            with dve.Fori(1, NT // 2 - 1) as r:
                for u in range(2):
                    turn(r, u, P, P)
            turn(NT // 2 - 1, 0, P, P)
            turn(NT // 2 - 1, 1, P, DEC)
            weigh(NT // 2, 0, DEC)
            finish(NT // 2, 0, DEC)


SCRATCH = {"mod": (2, 6 * D), "z": (TOK, 5 * D), "qT": (DH, P, TOK), "kT": (DH, P, TOK + PAST), "oaT": (KC, P, TOK), "mT": (KC, P, TOK), "x1": (TOK, D), "h2": (TOK, D),
           "scores": (TOK, 2 * PH, NKEY)}


def trunk(nc, d):
    for name, shape in SCRATCH.items():
        if name not in d:
            d[name] = nc.dram_tensor("scratch_" + name, shape, F32, kind="Internal").ap()
    def stage(build, *args):
        with ExitStack() as ctx:
            used = []

            def sem(name, software_dma=False):
                if software_dma:
                    return nc.alloc_semaphore(name)
                used.append(ctx.enter_context(nc.semaphore(name)))
                return used[-1]

            build(nc, sem, d, *args)
            with nc.Block() as block:
                @block.sync
                def _(sp):
                    for s in used:
                        sp.sem_clear(s)

    stage(modulation)
    with ExitStack() as outer:
        hT = outer.enter_context(nc.sbuf_tensor("hT", [P, KC, TOK], F32))
        stage(norm_in, hT)
        with ExitStack() as inner:
            qkT = inner.enter_context(nc.sbuf_tensor("qkT", [P, 2 * GH * TOK], F32))
            laT = inner.enter_context(nc.sbuf_tensor("laT", [P, GH, TOK], F32))
            stage(project, hT, qkT, laT)
            stage(gla, hT, qkT, laT)
        stage(rope)
        oaT = outer.enter_context(nc.sbuf_tensor("oaT", [P, KC, TOK], F32))
        obT = outer.enter_context(nc.sbuf_tensor("obT", [P, DH * TOK], F32))
        stage(attend, obT, oaT)
        stage(merge, hT, oaT, obT)
    with ExitStack() as outer:
        h2T = outer.enter_context(nc.sbuf_tensor("h2T", [P, KC, TOK], F32))
        stage(mix_out, h2T)
        stage(keys, h2T)
    stage(retrieve)


def _inputs(inputs):
    import numpy as np
    out = {k: np.ascontiguousarray(v) for k, v in inputs.items()}
    out["ident"] = np.eye(P, dtype=np.float32)
    out["stack"] = np.tile(np.eye(DEC, dtype=np.float32), (P // DEC, 1))
    out["iota"] = np.arange(TOPK, dtype=np.float32)[None, :]
    out["causal"] = np.triu(np.ones((P, P), np.float32))
    pos = np.concatenate([np.arange(SEQ), PAST + np.arange(P)]).astype(np.float64)
    inv = (np.float32(10000.0) ** (-np.arange(HD // 2, dtype=np.float32) / np.float32(HD // 2)))
    ang = pos.astype(np.float32)[:, None] * inv[None, :]
    out["rope_cos"] = np.cos(ang).astype(np.float32)
    out["rope_sin"] = np.sin(ang).astype(np.float32)
    return out


_OUTS = [("y_prompt", (1, SEQ, D)), ("y_sample", (1, DEC, D)),
         ("k_prompt", (1, 1, SEQ, DH, 2 * HD)), ("v_prompt", (1, 1, SEQ, DH, VD)), ("gla_prompt", (1, 1, GH, GDK, GDV)),
         ("k_sample", (1, 1, DEC, DH, 2 * HD)), ("v_sample", (1, 1, DEC, DH, VD)), ("gla_sample", (1, 1, GH, GDK, GDV))]


def kernel(**inputs):
    import concourse.bacc as bacc
    from concourse.bass_utils import run_bass_kernel_spmd

    nc = bacc.Bacc("TRN2", target_bir_lowering=False, num_devices=1)
    arrays, d = {}, {}
    for name, a in _inputs(inputs).items():
        arrays["in_" + name] = a
        d[name] = nc.dram_tensor("in_" + name, a.shape, mybir.dt.from_np(a.dtype), kind="ExternalInput").ap()
    for name, shape in _OUTS:
        d[name] = nc.dram_tensor("out_" + name, shape, F32, kind="ExternalOutput").ap()
    trunk(nc, d)
    r = run_bass_kernel_spmd(nc, [arrays], core_ids=[0])
    return tuple(r.results[0]["out_" + name] for name, _ in _OUTS)
```
